# Optimizing a Trainium2 kernel written in Bass

```python
import jax
import jax.numpy as jnp
from jax import lax
import numpy as np
import jax, jax.numpy as jnp

D_MODEL = 1024
BATCH = 1
SEQ = 512
DEPTH = 1

GRID_W = 64
CTX_LEN = 256
FNET_DIM = 512
FNET_GROUPS = 4
FNET_GROUP_DIM = FNET_DIM // FNET_GROUPS
HG_DIM = 512
HG_HEADS = 4
HG_HEAD_DIM = HG_DIM // HG_HEADS
HG_CHUNK = 16
D_FF = 2816
CONV_K = 3
N_MOD = 6
EPS = 1e-6

OFF_FNET = 0
OFF_Q = OFF_FNET + FNET_DIM
OFF_FF = OFF_Q + HG_DIM
OFF_FB = OFF_FF + HG_DIM
OFF_I = OFF_FB + HG_DIM
OFF_G = OFF_I + HG_DIM
OFF_GA = OFF_G + HG_DIM
OFF_GB = OFF_GA + D_MODEL
IN_DIM = OFF_GB + D_MODEL


def rmsnorm(x, g):
    xf = x.astype(jnp.float32)
    y = xf * lax.rsqrt(jnp.mean(xf * xf, axis=-1, keepdims=True) + EPS) * g.astype(jnp.float32)
    return y.astype(x.dtype)

def modulate(h, shift, scale):
    return h * (1.0 + scale) + shift

def fourier_mix(u):
    b, l, _ = u.shape
    ug = u.astype(jnp.float32).reshape(b, l, FNET_GROUPS, FNET_GROUP_DIM)
    y = jnp.fft.fft2(ug, axes=(1, 3), norm='ortho').real
    return y.reshape(b, l, FNET_DIM).astype(u.dtype)

def hgrn_chunk_scan(q, k, v, logf, s0):
    b, l, h, _ = q.shape
    dv = v.shape[-1]
    n = l // HG_CHUNK

    def to_chunks(t):
        return t.reshape(b, n, HG_CHUNK, h, t.shape[-1]).transpose(1, 0, 3, 2, 4)

    qc, kc, vc, gc = to_chunks(q), to_chunks(k), to_chunks(v), to_chunks(logf)
    lower = jnp.tril(jnp.ones((HG_CHUNK, HG_CHUNK), dtype=bool))[:, :, None]

    def step(state, inp):
        qi, ki, vi, gi = inp
        cum = jnp.cumsum(gi, axis=-2)
        total = cum[..., -1:, :]
        rel = cum[..., :, None, :] - cum[..., None, :, :]
        decay = jnp.exp(jnp.where(lower, rel, -jnp.inf))
        attn = jnp.einsum('bhtd,bhsd,bhtsd->bhts', qi, ki, decay)
        o = (jnp.einsum('bhts,bhsv->bhtv', attn, vi)
             + jnp.einsum('bhtd,bhdv->bhtv', qi * jnp.exp(cum), state))
        k_dec = ki * jnp.exp(total - cum)
        new_state = state * jnp.exp(total)[..., 0, :, None] + jnp.einsum('bhsd,bhsv->bhdv', k_dec, vi)
        return new_state, o

    s_final, o = lax.scan(step, s0, (qc, kc, vc, gc))
    o = o.transpose(1, 0, 3, 2, 4).reshape(b, l, h, dv)
    return o, s_final

def hgrn_inputs(u, lb):
    uf = u.astype(jnp.float32)
    b, l, _ = u.shape

    def heads(t):
        return t.reshape(b, l, HG_HEADS, HG_HEAD_DIM)

    q = heads(jax.nn.silu(uf[..., OFF_Q:OFF_Q + HG_DIM]))
    v = heads(uf[..., OFF_I:OFF_I + HG_DIM])
    f_fwd = lb + (1.0 - lb) * jax.nn.sigmoid(uf[..., OFF_FF:OFF_FF + HG_DIM])
    f_bwd = lb + (1.0 - lb) * jax.nn.sigmoid(uf[..., OFF_FB:OFF_FB + HG_DIM])
    return (q, v, heads(1.0 - f_fwd), heads(jnp.log(f_fwd)), heads(1.0 - f_bwd), heads(jnp.log(f_bwd)))

def hgrn_bidir(q, v, k_f, g_f, k_b, g_b, s0_f, s0_b):
    o_f, s_f = hgrn_chunk_scan(q, k_f, v, g_f, s0_f)
    flip = lambda t: jnp.flip(t, axis=1)
    o_b, s_b = hgrn_chunk_scan(flip(q), flip(k_b), flip(v), flip(g_b), s0_b)
    return o_f + flip(o_b), s_f, s_b

def hgrn_readout(u, o, onorm_g):
    b, l = o.shape[0], o.shape[1]
    on = o * lax.rsqrt(jnp.mean(o * o, axis=-1, keepdims=True) + EPS)
    on = on.reshape(b, l, HG_DIM) * onorm_g.astype(jnp.float32)
    on = on * jax.nn.silu(u[..., OFF_G:OFF_G + HG_DIM].astype(jnp.float32))
    return on.astype(u.dtype)

def merge_branches(u, y_hgrn, w_a, w_b, w_out):
    y_a = fourier_mix(u[..., OFF_FNET:OFF_FNET + FNET_DIM]) @ w_a
    y_b = y_hgrn @ w_b
    g_a = jax.nn.sigmoid(u[..., OFF_GA:OFF_GB])
    g_b = jax.nn.sigmoid(u[..., OFF_GB:IN_DIM])
    return (g_a * y_a + g_b * y_b) @ w_out

def conv_ffn(h, w_up, conv_w, conv_b, w_down, rows, cols):
    b, l, _ = h.shape
    z = (h @ w_up).reshape(b, rows, cols, 2 * D_FF)
    z = lax.conv_general_dilated(z, conv_w[:, :, None, :], window_strides=(1, 1), padding='SAME',
                                 dimension_numbers=('NHWC', 'HWIO', 'NHWC'),
                                 feature_group_count=2 * D_FF)
    z = z.reshape(b, l, 2 * D_FF) + conv_b
    return (jax.nn.silu(z[..., :D_FF]) * z[..., D_FF:]) @ w_down

def first_inputs(seed: int = 0) -> dict:
    key = jax.random.key(seed)
    ks = jax.random.split(key, 19)

    def nrm(k, shape):
        return jax.random.normal(k, shape, jnp.float32)

    def w(k, shape, fan_in, scale=1.0):
        return nrm(k, shape) * (scale * fan_in ** -0.5)

    def gain(k, shape):
        return 1.0 + 0.1 * nrm(k, shape)

    return {
        'x': nrm(ks[0], (BATCH, SEQ, D_MODEL)),
        'c': nrm(ks[1], (BATCH, D_MODEL)),
        'ctx': nrm(ks[2], (BATCH, CTX_LEN, D_MODEL)),
        'c_ctx': nrm(ks[3], (D_MODEL,)),
        'ada_w': w(ks[4], (DEPTH, D_MODEL, N_MOD * D_MODEL), D_MODEL, 0.5),
        'ada_b': 0.02 * nrm(ks[5], (DEPTH, N_MOD * D_MODEL)),
        'norm1_g': gain(ks[6], (DEPTH, D_MODEL)),
        'w_in': w(ks[7], (DEPTH, D_MODEL, IN_DIM), D_MODEL),
        'hg_lb': 0.1 * nrm(ks[8], (DEPTH + 1, HG_DIM)),
        'hg_onorm_g': gain(ks[9], (DEPTH, HG_DIM)),
        'w_a': w(ks[10], (DEPTH, FNET_DIM, D_MODEL), FNET_DIM),
        'w_b': w(ks[11], (DEPTH, HG_DIM, D_MODEL), HG_DIM),
        'w_out': w(ks[12], (DEPTH, D_MODEL, D_MODEL), D_MODEL),
        'norm2_g': gain(ks[13], (DEPTH, D_MODEL)),
        'ffn_up': w(ks[14], (DEPTH, D_MODEL, 2 * D_FF), D_MODEL),
        'ffn_conv_w': w(ks[15], (DEPTH, CONV_K, CONV_K, 2 * D_FF), CONV_K * CONV_K),
        'ffn_conv_b': 0.02 * nrm(ks[16], (DEPTH, 2 * D_FF)),
        'ffn_down': w(ks[17], (DEPTH, D_FF, D_MODEL), D_FF),
        'final_g': gain(ks[18], (D_MODEL,)),
    }

def first_block(x, c, ctx, c_ctx, ada_w, ada_b, norm1_g, w_in, hg_lb, hg_onorm_g, w_a, w_b, w_out,
              norm2_g, ffn_up, ffn_conv_w, ffn_conv_b, ffn_down, final_g):
    b, seq, _ = x.shape
    rows = seq // GRID_W
    ctx_len = ctx.shape[1]
    lb_all = jnp.cumsum(jax.nn.softmax(hg_lb.astype(jnp.float32), axis=0), axis=0)
    s_zero = jnp.zeros((b, HG_HEADS, HG_HEAD_DIM, HG_HEAD_DIM), jnp.float32)
    for layer in range(DEPTH):
        last = layer == DEPTH - 1
        mx = (jax.nn.silu(c) @ ada_w[layer] + ada_b[layer]).reshape(b, 1, N_MOD, D_MODEL)
        mc = (jax.nn.silu(c_ctx) @ ada_w[layer] + ada_b[layer]).reshape(N_MOD, D_MODEL)
        lb = lb_all[layer]

        hx = modulate(rmsnorm(x, norm1_g[layer]), mx[:, :, 0], mx[:, :, 1])
        hc = modulate(rmsnorm(ctx, norm1_g[layer]), mc[0], mc[1])
        ux = hx @ w_in[layer]
        uc = hc @ w_in[layer]
        oc, sc_f, sc_b = hgrn_bidir(*hgrn_inputs(uc, lb), s_zero, s_zero)
        ox, _, _ = hgrn_bidir(*hgrn_inputs(ux, lb), sc_f, sc_b)
        yx = merge_branches(ux, hgrn_readout(ux, ox, hg_onorm_g[layer]), w_a[layer], w_b[layer], w_out[layer])
        x = x + mx[:, :, 2] * yx
        if not last:
            yc = merge_branches(uc, hgrn_readout(uc, oc, hg_onorm_g[layer]), w_a[layer], w_b[layer], w_out[layer])
            ctx = ctx + mc[2] * yc

        h2 = modulate(rmsnorm(x, norm2_g[layer]), mx[:, :, 3], mx[:, :, 4])
        x = x + mx[:, :, 5] * conv_ffn(h2, ffn_up[layer], ffn_conv_w[layer], ffn_conv_b[layer],
                                       ffn_down[layer], rows, GRID_W)
        if not last:
            h2c = modulate(rmsnorm(ctx, norm2_g[layer]), mc[3], mc[4])
            ctx = ctx + mc[5] * conv_ffn(h2c, ffn_up[layer], ffn_conv_w[layer], ffn_conv_b[layer],
                                         ffn_down[layer], 1, ctx_len)
    return rmsnorm(x, final_g)


DEPTH_2 = 2

N_MIXERS = 2
RET_HEADS = 4
RET_QK_DIM = D_MODEL // RET_HEADS
RET_V_DIM = 2 * D_MODEL // RET_HEADS
RET_CHUNK = 128
DECAY_EXP_FWD = 5.0
DECAY_EXP_BWD = 5.5
ROPE_BASE = 10000.0
CONV_WIDTH = 3
FFN_HIDDEN = -(-8 * D_MODEL // (3 * 256)) * 256
N_RET_LAYERS = (DEPTH_2 + N_MIXERS - 1) // N_MIXERS
N_CONV_LAYERS = DEPTH_2 // N_MIXERS


def rms_norm(x, gain=None):
    xf = x.astype(jnp.float32)
    y = xf * lax.rsqrt(jnp.mean(xf * xf, axis=-1, keepdims=True) + EPS)
    if gain is not None:
        y = y * gain.astype(jnp.float32)
    return y.astype(x.dtype)

def ada_params(cond, w, b):
    return jnp.split(jax.nn.silu(cond) @ w + b, 6, axis=-1)

def modulate_2(x, shift, scale):
    return x * (1 + scale) + shift

def rope_1d(x, pos):
    n = x.shape[-1] // 2
    freqs = ROPE_BASE ** (-jnp.arange(n, dtype=jnp.float32) / n)
    ang = pos.astype(jnp.float32)[:, None] * freqs[None, :]
    cos, sin = jnp.cos(ang).astype(x.dtype), jnp.sin(ang).astype(x.dtype)
    x1, x2 = x[..., :n], x[..., n:]
    return jnp.concatenate([x1 * cos - x2 * sin, x1 * sin + x2 * cos], axis=-1)

def rope_2d(x, row, col):
    half = x.shape[-1] // 2
    return jnp.concatenate([rope_1d(x[..., :half], row), rope_1d(x[..., half:], col)], axis=-1)

def retention_log_decays():
    h = jnp.arange(RET_HEADS, dtype=jnp.float32)
    lg_f = jnp.log1p(-jnp.exp2(-DECAY_EXP_FWD - h))
    lg_b = jnp.log1p(-jnp.exp2(-DECAY_EXP_BWD - h))
    return lg_f, lg_b

def retention_chunk_scan(q, k, v, log_g, s0):
    bsz, nh, L, _ = q.shape
    dv = v.shape[-1]
    n_chunks = L // RET_CHUNK

    def to_chunks(t):
        return t.reshape(bsz, nh, n_chunks, RET_CHUNK, t.shape[-1]).transpose(2, 0, 1, 3, 4)

    idx = jnp.arange(RET_CHUNK, dtype=jnp.float32)
    diff = idx[:, None] - idx[None, :]
    decay_mat = jnp.where(diff[None] >= 0,
                          jnp.exp(jnp.maximum(diff, 0.0)[None] * log_g[:, None, None]), 0.0)
    q_dec = jnp.exp((idx[None, :] + 1.0) * log_g[:, None])[None, :, :, None]
    k_dec = jnp.exp((RET_CHUNK - 1.0 - idx[None, :]) * log_g[:, None])[None, :, :, None]
    chunk_dec = jnp.exp(RET_CHUNK * log_g)[None, :, None, None]

    def step(s, inp):
        qc, kc, vc = inp
        scores = jnp.einsum('bhid,bhjd->bhij', qc, kc) * decay_mat[None]
        intra = jnp.einsum('bhij,bhje->bhie', scores, vc)
        cross = jnp.einsum('bhid,bhde->bhie', qc * q_dec, s)
        s_new = s * chunk_dec + jnp.einsum('bhjd,bhje->bhde', kc * k_dec, vc)
        return s_new, intra + cross

    _, out = lax.scan(step, s0, (to_chunks(q), to_chunks(k), to_chunks(v)))
    return out.transpose(1, 2, 0, 3, 4).reshape(bsz, nh, L, dv)

def context_state(k, v, log_g, reverse):
    L = k.shape[2]
    j = jnp.arange(L, dtype=jnp.float32)
    dist = j if reverse else (L - 1.0) - j
    w = jnp.exp(dist[None, :] * log_g[:, None])
    return jnp.einsum('bhld,bhle->bhde', k * w[None, :, :, None], v)

def context_parallel(q, k, v, lg_f, lg_b):
    L = q.shape[2]
    idx = jnp.arange(L, dtype=jnp.float32)
    diff = idx[:, None] - idx[None, :]
    d_f = jnp.where(diff[None] >= 0, jnp.exp(jnp.maximum(diff, 0.0)[None] * lg_f[:, None, None]), 0.0)
    d_b = jnp.where(diff[None] <= 0, jnp.exp(jnp.maximum(-diff, 0.0)[None] * lg_b[:, None, None]), 0.0)
    scores = jnp.einsum('bhid,bhjd->bhij', q, k) * (d_f + d_b)[None]
    return jnp.einsum('bhij,bhje->bhie', scores, v)

def retention_output(o, g, w_o):
    bsz, nh, L, dv = o.shape
    o = o * lax.rsqrt(jnp.mean(o * o, axis=-1, keepdims=True) + EPS)
    o = o.transpose(0, 2, 1, 3).reshape(bsz, L, nh * dv).astype(g.dtype)
    return (jax.nn.silu(g) * o) @ w_o

def retention_mixer(ax, ac, w_qkvg, w_o, row, col, with_ctx_out):
    D = D_MODEL
    scale = RET_QK_DIM ** -0.5

    def heads(t, d):
        return t.reshape(t.shape[0], t.shape[1], RET_HEADS, d).transpose(0, 2, 1, 3).astype(jnp.float32)

    qx, kx, vx, gx = jnp.split(ax @ w_qkvg, [D, 2 * D, 4 * D], axis=-1)
    qx = rope_2d(heads(qx, RET_QK_DIM), row, col)
    kx = rope_2d(heads(kx, RET_QK_DIM), row, col) * scale
    vx = heads(vx, RET_V_DIM)

    if with_ctx_out:
        qc, kc, vc, gc = jnp.split(ac @ w_qkvg, [D, 2 * D, 4 * D], axis=-1)
    else:
        kc, vc = jnp.split(ac @ w_qkvg[:, D:4 * D], [D], axis=-1)
    kc = heads(kc, RET_QK_DIM) * scale
    vc = heads(vc, RET_V_DIM)

    lg_f, lg_b = retention_log_decays()
    s_f = context_state(kc, vc, lg_f, reverse=False)
    s_b = context_state(kc, vc, lg_b, reverse=True)

    o_f = retention_chunk_scan(qx, kx, vx, lg_f, s_f)
    o_b = jnp.flip(retention_chunk_scan(jnp.flip(qx, 2), jnp.flip(kx, 2), jnp.flip(vx, 2), lg_b, s_b), 2)
    yx = retention_output(o_f + o_b, gx, w_o)

    yc = None
    if with_ctx_out:
        yc = retention_output(context_parallel(heads(qc, RET_QK_DIM), kc, vc, lg_f, lg_b), gc, w_o)
    return yx, yc

def short_conv(u, w):
    return lax.conv_general_dilated(
        u, w[:, None, :].astype(u.dtype), window_strides=(1,),
        padding=[(CONV_WIDTH // 2, CONV_WIDTH // 2)],
        dimension_numbers=('NWC', 'WIO', 'NWC'), feature_group_count=u.shape[-1])

def conv_mixer(h, w_in, w_conv, w_out):
    b_gate, c_gate, xv = jnp.split(h @ w_in, 3, axis=-1)
    return (b_gate * short_conv(c_gate * xv, w_conv)) @ w_out

def swiglu(h, w1, w3, w2):
    return (jax.nn.silu(h @ w1) * (h @ w3)) @ w2

def second_inputs(seed: int = 0) -> dict:
    key = jax.random.key(seed)
    ks = jax.random.split(key, 20)
    D, F = D_MODEL, FFN_HIDDEN
    nrm = jax.random.normal
    f32 = jnp.float32
    return {
        "x": nrm(ks[0], (BATCH, SEQ, D), f32),
        "c": nrm(ks[1], (BATCH, D), f32),
        "ctx": nrm(ks[2], (BATCH, CTX_LEN, D), f32),
        "c_ctx": nrm(ks[3], (D,), f32),
        "ada_w": nrm(ks[4], (DEPTH_2, D, 6 * D), f32) * (0.5 * D ** -0.5),
        "ada_b": nrm(ks[5], (DEPTH_2, 6 * D), f32) * 0.02,
        "norm_mix": 1.0 + 0.02 * nrm(ks[6], (DEPTH_2, D), f32),
        "norm_ffn": 1.0 + 0.02 * nrm(ks[7], (DEPTH_2, D), f32),
        "ret_w_qkvg": nrm(ks[8], (N_RET_LAYERS, D, 6 * D), f32) * D ** -0.5,
        "ret_w_o": nrm(ks[9], (N_RET_LAYERS, 2 * D, D), f32) * (2 * D) ** -0.5,
        "conv_w_in": nrm(ks[10], (N_CONV_LAYERS, D, 3 * D), f32) * D ** -0.5,
        "conv_w": nrm(ks[11], (N_CONV_LAYERS, CONV_WIDTH, D), f32) * CONV_WIDTH ** -0.5,
        "conv_w_out": nrm(ks[12], (N_CONV_LAYERS, D, D), f32) * D ** -0.5,
        "ffn_w1": nrm(ks[13], (DEPTH_2, D, F), f32) * D ** -0.5,
        "ffn_w3": nrm(ks[14], (DEPTH_2, D, F), f32) * D ** -0.5,
        "ffn_w2": nrm(ks[15], (DEPTH_2, F, D), f32) * F ** -0.5,
        "final_norm": 1.0 + 0.02 * nrm(ks[16], (D,), f32),
    }

def second_block(x, c, ctx, c_ctx, ada_w, ada_b, norm_mix, norm_ffn, ret_w_qkvg, ret_w_o,
              conv_w_in, conv_w, conv_w_out, ffn_w1, ffn_w3, ffn_w2, final_norm):
    T = x.shape[1]
    rows = T // GRID_W
    row = jnp.repeat(jnp.arange(rows, dtype=jnp.int32), GRID_W)
    col = jnp.tile(jnp.arange(GRID_W, dtype=jnp.int32), rows)

    hx, hc = x, ctx
    for i in range(DEPTH_2):
        mixer = i % N_MIXERS
        ctx_needed = any(j % N_MIXERS == 0 for j in range(i + 1, DEPTH_2))
        sh1, sc1, g1, sh2, sc2, g2 = [t[:, None, :] for t in ada_params(c, ada_w[i], ada_b[i])]
        ax = modulate_2(rms_norm(hx, norm_mix[i]), sh1, sc1)
        if mixer == 0 or ctx_needed:
            csh1, csc1, cg1, csh2, csc2, cg2 = ada_params(c_ctx, ada_w[i], ada_b[i])
            ac = modulate_2(rms_norm(hc, norm_mix[i]), csh1, csc1)

        if mixer == 0:
            r = i // N_MIXERS
            yx, yc = retention_mixer(ax, ac, ret_w_qkvg[r], ret_w_o[r], row, col, ctx_needed)
        else:
            r = i // N_MIXERS
            yx = conv_mixer(ax, conv_w_in[r], conv_w[r], conv_w_out[r])
            yc = conv_mixer(ac, conv_w_in[r], conv_w[r], conv_w_out[r]) if ctx_needed else None

        hx = hx + g1 * yx
        fx = modulate_2(rms_norm(hx, norm_ffn[i]), sh2, sc2)
        hx = hx + g2 * swiglu(fx, ffn_w1[i], ffn_w3[i], ffn_w2[i])

        if ctx_needed:
            hc = hc + cg1 * yc
            fc = modulate_2(rms_norm(hc, norm_ffn[i]), csh2, csc2)
            hc = hc + cg2 * swiglu(fc, ffn_w1[i], ffn_w3[i], ffn_w2[i])

    return rms_norm(hx, final_norm)


def setup_inputs(seed=0):
    out = dict(first_inputs(seed))
    for name, value in second_inputs(seed + 1).items():
        if name != "x":
            out[name + "_2"] = value
    return out


def reference(
    x, c, ctx, c_ctx, ada_w, ada_b, norm1_g, w_in, hg_lb, hg_onorm_g, w_a, w_b, w_out, norm2_g,
    ffn_up, ffn_conv_w, ffn_conv_b, ffn_down, final_g, c_2, ctx_2, c_ctx_2, ada_w_2, ada_b_2,
    norm_mix_2, norm_ffn_2, ret_w_qkvg_2, ret_w_o_2, conv_w_in_2, conv_w_2, conv_w_out_2,
    ffn_w1_2, ffn_w3_2, ffn_w2_2, final_norm_2,
):
    x = first_block(
        x, c, ctx, c_ctx, ada_w, ada_b, norm1_g, w_in, hg_lb, hg_onorm_g, w_a, w_b, w_out,
        norm2_g, ffn_up, ffn_conv_w, ffn_conv_b, ffn_down, final_g,
    )
    return second_block(
        x, c_2, ctx_2, c_ctx_2, ada_w_2, ada_b_2, norm_mix_2, norm_ffn_2, ret_w_qkvg_2,
        ret_w_o_2, conv_w_in_2, conv_w_2, conv_w_out_2, ffn_w1_2, ffn_w3_2, ffn_w2_2,
        final_norm_2,
    )


_drawn_inputs = setup_inputs


def setup_inputs(seed=0):
    import zlib

    import numpy as np

    out = dict(_drawn_inputs(seed))
    spreads = {}
    factors = {'ctx': 8.0,
     'c_ctx': 8.0,
     'hg_lb': 8.0,
     'hg_onorm_g': 4.394,
     'ffn_conv_b': 8.0,
     'norm_mix_2': 3.888,
     'norm_ffn_2': 6.544,
     'final_norm_2': 2.698}
    for name, (base, spread) in spreads.items():
        noise = np.random.default_rng([zlib.crc32(name.encode()), seed]).standard_normal(out[name].shape)
        drawn = base * np.exp(spread * noise) if base else spread * noise
        out[name] = jnp.asarray(drawn.astype(out[name].dtype))
    for name, factor in factors.items():
        out[name] = (out[name] * factor).astype(out[name].dtype)
    return out
```

```python
from contextlib import ExitStack

import numpy as np
import concourse.bass as bass
from concourse import mybir

F32 = mybir.dt.float32
F32R = mybir.dt.float32r
I32 = mybir.dt.int32
ALU = mybir.AluOpType
ACT = mybir.ActivationFunctionType

P = 128
D = 1024
KT = D // P
L, LC = 512, 256
LT, LCT = L // P, LC // P
GRID = 64
ROWS = L // GRID
FF = 2816
HT = FF // P
HEADS = 4
LEVELS = 7
EPS = 1e-6
BLK = KT * P

RING = 4
RAW = 2
AHEAD = RING - 1

B_GATES = 0
B_VAL = B_GATES + 8
B_Q = B_VAL + 4
B_FNET = B_Q + 4
B_G = B_FNET + 4
B_MERGE = B_G + 4
B_OUT = B_MERGE + 24
B_UP = B_OUT + 8
B_DOWN = B_UP + 2 * HT
B_RET = B_DOWN + HT
B_SW0 = B_RET + 16 * HEADS
B_SD0 = B_SW0 + 2 * HT
B_CIN = B_SD0 + HT
B_COUT = B_CIN + 24
B_SW1 = B_COUT + 8
B_SD1 = B_SW1 + 2 * HT
N_BLOCKS = B_SD1 + HT

COLS = {}
_at = 0
for _name, _n in [("c", 8), ("c_ctx", 8), ("norm1", 8), ("norm2", 8), ("final1", 8), ("lb0", 4),
                  ("lb1", 4), ("onorm", 4), ("conv", HT * 20), ("ada_b", 144), ("mix", 16),
                  ("ffn", 16), ("final2", 8), ("sconv", 24)]:
    COLS[_name] = _at
    _at += _n
N_COLS = _at

DEC_W = L + (LT - 1) * P
DEC_N = DEC_W + 2 * L + 2 * LCT


class Block:

    def __init__(self, at, i=None, per=0):
        self.at, self.i, self.per = at, i, per

    def plus(self, n):
        return Block(self.at + n, self.i, self.per)

    def count(self, n=0):
        return self.at + n if self.i is None else self.i * self.per + (self.at + n)

    def loads(self):
        first = 16 * (self.at // RAW + 1)
        return first if self.i is None else self.i * (16 * self.per // RAW) + first


def program(nc, wstream, ada_kn, ada_nk, x_in, ctx1_in, ctx2_in, cols_in, crow_in, ident_in, masks_in,
            dft1_in, dft2_in, rope_in, dec_in, out):
    with ExitStack() as ctx:
        def sem(name):
            return ctx.enter_context(nc.semaphore(name))

        base = (nc.sbuf_base + 63) // 64 * 64
        cursor = [base]

        def region(nbytes):
            at = cursor[0]
            cursor[0] += (nbytes + 31) // 32 * 32
            assert cursor[0] <= nc.sbuf_usable_end, cursor[0] - nc.sbuf_usable_end
            return at

        def sb(name, shape, dt=F32, at=None):
            nbytes = 4 * int(np.prod(shape[1:]))
            return nc.alloc_sbuf_tensor_at(name, shape, dt, offset=region(nbytes) if at is None else at)

        w_raw = [sb(f"w_raw{s}", [P, BLK]) for s in range(RAW)]
        w_hi = [sb(f"w_hi{s}", [P, BLK], F32R) for s in range(RING)]
        w_lo = [sb(f"w_lo{s}", [P, BLK], F32R) for s in range(RING)]
        res = sb("res", [P, KT, L])
        KB = 1024
        r_hx = region(32 * KB)
        hx_hi = sb("hx_hi", [P, KT, L], F32R, r_hx)
        hx_lo = sb("hx_lo", [P, KT, L], F32R, r_hx + 16 * KB)
        x_tok = sb("x_tok", [P, LT, D], F32, r_hx)
        ctx_tok = sb("ctx_tok", [P, LCT, D], F32, r_hx + 16 * KB)
        ada_raw = [sb(f"ada_raw{s}", [P, D]) for s in range(2)]
        crow = sb("crow", [P, 3, D])
        cols = sb("cols", [P, N_COLS])
        ident = sb("ident", [P, P])
        ones = sb("ones", [P, P])
        eps_col = sb("eps_col", [P, 1])
        scol = sb("scol", [P, 2, KT])
        ada_sum = sb("ada_sum", [P, 8])
        ada0 = sb("ada0", [P, 16, 2])
        ada = sb("ada", [P, 128])
        ada_c = sb("ada_c", [P, 16])
        mod_a = sb("mod_a", [P, 2, KT])
        lb = sb("lb", [P, HEADS])
        oml = sb("oml", [P, HEADS])
        dft1 = sb("dft1", [P, 2 * P])
        r_scr = region(12 * KB)
        r_hc = region(16 * KB)
        r_arena = region(80 * KB)
        hc_hi = sb("hc_hi", [P, KT, LC], F32R, r_hc)
        hc_lo = sb("hc_lo", [P, KT, LC], F32R, r_hc + 8 * KB)
        sq = [sb(f"sq{s}", [P, L], F32, r_scr + 2 * KB * s) for s in range(2)]
        std = sb("std", [P, L], F32, r_scr + 4 * KB)
        rstd = sb("rstd", [P, L], F32, r_scr + 6 * KB)
        tnorm = [sb(f"tnorm{s}", [P, L], F32, r_scr + (8 + 2 * s) * KB) for s in range(2)]
        ada_w0 = sb("ada_w0", [P, 16, D], F32, r_arena)
        ctx_t = sb("ctx_t", [P, KT, LC], F32, r_arena + 64 * KB)
        r_q, r_k, r_f, r_x, r_v = (r_arena + 16 * KB * n for n in range(5))
        hq = sb("hq", [P, LT, 2, HEADS, P], F32, r_q)
        hk = sb("hk", [P, LT, 2, HEADS, P], F32, r_k)
        hf = sb("hf", [P, LT, 2, HEADS, P], F32, r_f)
        kc = sb("kc", [P, 2, HEADS, LC], F32, r_x)
        fc = sb("fc", [P, 2, HEADS, LC], F32, r_x + 8 * KB)
        v_x = sb("v_x", [P, LT, L], F32, r_v)
        v_c = sb("v_c", [P, LCT, L], F32, r_v + 8 * KB)
        masks = sb("masks", [P, LEVELS, P], I32, r_v + 12 * KB)
        sig = [sb(f"sig{s}", [P, L + LC], F32, r_scr + 3 * KB * s) for s in range(2)]
        tc = [sb("tc0", [P, 2 * HEADS * LC // 2], F32, r_scr + 6 * KB),
              sb("tc1", [P, 2 * HEADS * LC // 4], F32, r_scr + 10 * KB)]
        kd_c = sb("kd_c", [P, 2, HEADS, LCT, P], F32, r_scr)
        s_init = sb("s_init", [P, 2, HEADS, P], F32, r_scr + 8 * KB)
        ksum = [sb(f"ksum{s}", [P, HEADS, P], F32, r_scr + 2 * KB * s) for s in range(2)]
        kd_x = [sb(f"kd_x{s}", [P, HEADS, P], F32, r_scr + (4 + 2 * s) * KB) for s in range(2)]
        level_k = [sb(f"level_k{s}", [P, HEADS * P], F32, r_scr + (4 + 2 * s) * KB) for s in range(2)]
        tx = [[sb(f"tx{s}_0", [P, 512], F32, r_x + 3 * KB * s),
               sb(f"tx{s}_1", [P, 256], F32, r_x + 3 * KB * s + 2 * KB)] for s in range(2)]
        att = [sb(f"att{c}", [P, HEADS, P], F32, r_x + (6 + 2 * c) * KB) for c in range(LT)]
        ttot = sb("ttot", [P, LT, 2 * HEADS])
        ho = sb("ho", [P, LT, 2, HEADS, P], F32, r_f)
        yb_hi = sb("yb_hi", [P, HEADS, L], F32R, r_q)
        yb_lo = sb("yb_lo", [P, HEADS, L], F32R, r_q + 8 * KB)
        ut = sb("ut", [P, HEADS, L], F32, r_hc)
        gs = sb("gs", [P, HEADS, L], F32, r_hc + 8 * KB)
        pq = sb("pq", [P, LT, HEADS, 2 * P], F32, r_k)
        dft2 = sb("dft2", [P, 2, LT, L], F32, r_v)
        ya_hi = sb("ya_hi", [P, HEADS, L], F32R, r_x)
        ya_lo = sb("ya_lo", [P, HEADS, L], F32R, r_x + 8 * KB)
        yt = [sb(f"yt{s}", [P, L], F32, r_scr + (8 + 2 * s) * KB) for s in range(2)]
        gate_a = [sb(f"gate_a{s}", [P, L], F32, r_scr + 2 * KB * s) for s in range(2)]
        gate_b = [sb(f"gate_b{s}", [P, L], F32, r_scr + (4 + 2 * s) * KB) for s in range(2)]
        mt = [sb(f"mt{s}", [P, L], F32, r_scr + (8 + 2 * s) * KB) for s in range(2)]
        m_hi = sb("m_hi", [P, KT, L], F32R, r_k)
        m_lo = sb("m_lo", [P, KT, L], F32R, r_f)
        hid_hi = sb("hid_hi", [P, HT, L], F32R, r_hc)
        hid_lo = sb("hid_lo", [P, HT, L], F32R, r_hc + 44 * KB)
        acc = [[sb(f"acc{s}{k}", [P, ROWS, GRID], F32, r_hc + (88 + 4 * s + 2 * k) * KB) for k in range(2)]
               for s in range(2)]
        zpad = [[sb(f"zpad{s}{k}", [P, ROWS + 2, GRID + 2], F32, r_scr + 2656 * (2 * s + k)) for k in range(2)]
                for s in range(2)]
        sw = [sb(f"sw{s}", [P, L], F32, r_scr + 2 * KB * s) for s in range(2)]
        r_a = r_arena
        rq = sb("rq", [P, 2, L], F32, r_a)
        rk = sb("rk", [P, 2, L], F32, r_a + 4 * KB)
        ro = sb("ro", [P, HEADS, L], F32, r_a)
        rv = sb("rv", [P, LT, L], F32, r_a + 8 * KB)
        rg = sb("rg", [P, HEADS, L], F32, r_a + 16 * KB)
        rkc = sb("rkc", [P, 2, LCT, 2 * P], F32, r_a + 24 * KB)
        rvc = sb("rvc", [P, LCT, L], F32, r_a + 28 * KB)
        rsc = sb("rsc", [P, LT, L], F32, r_a + 24 * KB)
        rst = sb("rst", [P, 2, 2, L], F32, r_a + 32 * KB)
        rqd = sb("rqd", [P, 2, 2, L], F32, r_a + 40 * KB)
        ry_hi = sb("ry_hi", [P, HEADS, L], F32R, r_a + 48 * KB)
        ry_lo = sb("ry_lo", [P, HEADS, L], F32R, r_a + 56 * KB)
        rope = sb("rope", [P, 4, L], F32, r_a + 64 * KB)
        dec = sb("dec", [P, DEC_N], F32, r_a + 72 * KB)
        rt = [sb(f"rt{s}", [P, L], F32, r_scr + (8 + 2 * s) * KB) for s in range(2)]
        rsq = [sb(f"rsq{s}", [P, L], F32, r_scr + 2 * KB * s) for s in range(2)]
        ctx2_tok = sb("ctx2_tok", [P, LCT, D], F32, r_a)
        ctx2_t = sb("ctx2_t", [P, KT, LC], F32, r_a + 8 * KB)
        cy_hi = sb("cy_hi", [P, KT, L], F32R, r_a)
        cy_lo = sb("cy_lo", [P, KT, L], F32R, r_a + 16 * KB)
        cb = [sb(f"cb{s}", [P, L], F32, r_a + (32 + 2 * s) * KB) for s in range(2)]
        cc = [sb(f"cc{s}", [P, L], F32, r_a + (36 + 2 * s) * KB) for s in range(2)]
        cacc = [sb(f"cacc{s}", [P, L], F32, r_a + (40 + 2 * s) * KB) for s in range(2)]
        cpad = [sb(f"cpad{s}", [P, L + 2], F32, r_a + 44 * KB + 2112 * s) for s in range(2)]
        out_tok = sb("out_tok", [P, LT, D], F32, r_a)

        bank = [ctx.enter_context(nc.psum_tensor(f"bank{n}", [P, L], F32)) for n in range(8)]
        bx, by = bank[0:2], bank[2:4]
        bn = bank[5]
        bw = bank[6:8]

        raw_ready = [sem(f"raw_ready{s}") for s in range(RAW)]
        hi_ready, lo_ready, block_done = sem("hi_ready"), sem("lo_ready"), sem("block_done")
        x_free, y_free = sem("x_free"), sem("y_free")
        ada_in = [sem(f"ada_in{s}") for s in range(2)]
        ada_done = sem("ada_done")
        ada_cols = sem("ada_cols")
        x_landed, ctx_landed = sem("x_landed"), sem("ctx_landed")
        cols_landed, crow_landed, ident_landed = sem("cols_landed"), sem("crow_landed"), sem("ident_landed")
        dft1_landed, dft2_landed, masks_landed = sem("dft1_landed"), sem("dft2_landed"), sem("masks_landed")
        ada0_in = [sem(f"ada0_in{n}") for n in range(4)]
        consts, crow_silu, scol_ready = sem("consts"), sem("crow_silu"), sem("scol_ready")
        turned, ada0_mm, ada0_ready = sem("turned"), sem("ada0_mm"), sem("ada0_ready")
        mod_ready = sem("mod_ready")
        lb_ready = sem("lb_ready")
        f_ready, k_ready, v_ready = sem("f_ready"), sem("k_ready"), sem("v_ready")
        kc_level, kc_turned, kd_ready, s0_mm, s_ready = (
            sem("kc_level"), sem("kc_turned"), sem("kd_ready"), sem("s0_mm"), sem("s_ready"))
        gs_ready = sem("gs_ready")
        level_ready, level_mm, chunk_ready = sem("level_ready"), sem("level_mm"), sem("chunk_ready")
        k_gathered = sem("k_gathered")
        k_turned, kd_copied, upd_mm, upd_done = sem("k_turned"), sem("kd_copied"), sem("upd_mm"), sem("upd_done")
        o_mm, o_ready, osq_ready, osum_mm, ostd, orstd, on_ready, yb_f, yb_h, yb_l = (
            sem("o_mm"), sem("o_ready"), sem("osq_ready"), sem("osum_mm"), sem("ostd"), sem("orstd"),
            sem("on_ready"), sem("yb_f"), sem("yb_h"), sem("yb_l"))
        pq_mm, pq_ready, ya_mm, ya_f, ya_h, ya_l = (
            sem("pq_mm"), sem("pq_ready"), sem("ya_mm"), sem("ya_f"), sem("ya_h"), sem("ya_l"))
        m_f, m_h, m_l = sem("m_f"), sem("m_h"), sem("m_l")
        z_zero, tap_done, silu_done, hid_f, hid_h, hid_l = (
            sem("z_zero"), sem("tap_done"), sem("silu_done"), sem("hid_f"), sem("hid_h"), sem("hid_l"))
        ctx2_landed, turned2, rope_landed, dec_landed = (
            sem("ctx2_landed"), sem("turned2"), sem("rope_landed"), sem("dec_landed"))
        rot_done, qd_done, rv_done = sem("rot_done"), sem("qd_done"), sem("rv_done")
        st_mm, st_done, sc_mm, ro_mm, ro_done, rsum_mm, rstd_s, rstd_r = (
            sem("st_mm"), sem("st_done"), sem("sc_mm"), sem("ro_mm"), sem("ro_done"), sem("rsum_mm"),
            sem("rstd_s"), sem("rstd_r"))
        ry_t, ry_f, ry_h, ry_l = sem("ry_t"), sem("ry_f"), sem("ry_h"), sem("ry_l")
        sw_h = [sem("sw_h0"), sem("sw_h1")]
        sw_l = [sem("sw_l0"), sem("sw_l1")]
        cpad_zero, cacc_step, cy_f, cy_h, cy_l = (
            sem("cpad_zero"), sem("cacc_step"), sem("cy_f"), sem("cy_h"), sem("cy_l"))
        turned_out, out_copied, out_stored = sem("turned_out"), sem("out_copied"), sem("out_stored")

        norm_sq, norm_sum, norm_std, norm_rstd = sem("norm_sq"), sem("norm_sum"), sem("norm_std"), sem("norm_rstd")
        norm_scaled, norm_hi, norm_lo = sem("norm_scaled"), sem("norm_hi"), sem("norm_lo")

        class Norm:

            def __init__(self, n, split):
                self.once, self.tiles, self.split_tiles = n, KT * n, KT * split

        n1x, n1c, n2, nf1, nmx, nmc, nffn0, nmix1, nffn1, nf2 = (
            Norm(n, s) for n, s in enumerate((0, 1, 2, 3, 3, 4, 5, 6, 7, 8)))

        def split_hi(act, b):
            nb = b.plus(AHEAD)
            if nb.at >= N_BLOCKS:
                return
            act.wait_ge(raw_ready[nb.at % RAW], nb.loads())
            if nb.at >= RING:
                act.wait_ge(block_done, nb.count(1 - RING))
            nc.scalar.activation(w_hi[nb.at % RING][:], w_raw[nb.at % RAW][:], ACT.Copy).then_inc(hi_ready, 1)

        def split_lo(dve, b):
            nb = b.plus(AHEAD)
            if nb.at >= N_BLOCKS:
                return
            dve.wait_ge(hi_ready, nb.count(1))
            nc.vector.tensor_tensor(w_lo[nb.at % RING][:], w_raw[nb.at % RAW][:],
                                    w_hi[nb.at % RING][:].bitcast(F32), ALU.subtract).then_inc(lo_ready, 1)

        def ada_load(act, a, i=None, per=0):
            n = a if i is None else i * per + a
            if a >= 2:
                act.wait_ge(ada_done, n - 1)
            src = ada_nk[a] if i is None else ada_nk[bass.ds(n, 1)].rearrange("o p n -> (o p) n")
            act.dma_start(ada_raw[a % 2][:], src).then_inc(ada_in[a % 2], 16)

        def ada_reduce(dve, a, row, i=None, per=0, row_c=None):
            landed = 16 * (a // 2 + 1)
            dve.wait_ge(ada_in[a % 2], landed if i is None else i * (16 * per // 2) + landed)
            n = a if i is None else i * per + a
            w = ada_raw[a % 2]
            if row_c is not None:
                nc.vector.tensor_tensor_reduce(crow[:, 0, :], w[:], crow[:, row_c, :], 1.0, 0.0, ALU.mult, ALU.add,
                                               ada_sum[:, 4 + a % 4:5 + a % 4])
            nc.vector.tensor_tensor_reduce(w[:], w[:], crow[:, row, :], 1.0, 0.0, ALU.mult, ALU.add,
                                           ada_sum[:, a % 4:a % 4 + 1]).then_inc(ada_done, 1)
            dve.wait_ge(ada_done, n + 1)
            bias = COLS["ada_b"] + 16 + a
            if row_c is not None:
                nc.vector.tensor_tensor(ada_c[:, a - 32:a - 31], ada_sum[:, 4 + a % 4:5 + a % 4],
                                        cols[:, bias:bias + 1], ALU.add)
            if i is None:
                dst, bcol = ada[:, a:a + 1], cols[:, bias:bias + 1]
            else:
                dst, bcol = ada[:, bass.ds(n, 1)], cols[:, bass.ds(n + (COLS["ada_b"] + 16), 1)]
            nc.vector.tensor_tensor(dst, ada_sum[:, a % 4:a % 4 + 1], bcol, ALU.add).then_inc(ada_cols, 1)

        def three(out_ap, terms, first, last):
            n = 3 * len(terms)
            at = 0
            for sh, sl, mh, ml in terms:
                for s, m in ((sh, mh), (sh, ml), (sl, mh)):
                    ins = nc.tensor.matmul(out_ap, s, m, start=first and at == 0, stop=last and at == n - 1)
                    at += 1
            return ins

        def wtile(b, t):
            s = b.at % RING
            return w_hi[s][:, t * P:(t + 1) * P], w_lo[s][:, t * P:(t + 1) * P]

        def wrow(b, r):
            s = b.at % RING
            return w_hi[s][:, r * L:(r + 1) * L], w_lo[s][:, r * L:(r + 1) * L]

        def norm_pe(pe, nm, n, dst_bank):
            for j in range(KT):
                pe.wait_ge(norm_sq, nm.tiles + j + 1)
                nc.tensor.matmul(dst_bank[:, :n], ones[:], sq[j % 2][:, :n], start=(j == 0),
                                 stop=(j == KT - 1)).then_inc(norm_sum, 1)

        def norm_act(act, nm, src, n, src_bank, wait_src, shift, dst, scr_free=None):
            for j in range(KT):
                wait_src(j)
                if j >= 2:
                    act.wait_ge(norm_sum, nm.tiles + j - 1)
                nc.scalar.activation(sq[j % 2][:, :n], src[:, j, :], ACT.Square).then_inc(norm_sq, 1)
            act.wait_ge(norm_sum, nm.tiles + KT)
            nc.scalar.activation(std[:, :n], src_bank[:, :n], ACT.Sqrt, scale=1.0 / D,
                                 bias=eps_col[:]).then_inc(norm_std, 1)
            if dst is not None:
                for j in range(KT):
                    act.wait_ge(norm_scaled, nm.split_tiles + j + 1)
                    nc.scalar.activation(dst[:, j, :], tnorm[j % 2][:, :n], ACT.Identity,
                                         bias=shift(j)).then_inc(norm_hi, 1)

        def norm_dve(dve, nm, src, n, gain, shift, dst_hi, dst_lo):
            dve.wait_ge(norm_std, nm.once + 1)
            nc.vector.reciprocal(rstd[:, :n], std[:, :n]).then_inc(norm_rstd, 1)
            dve.wait_ge(norm_rstd, nm.once + 1)

            def rest(j):
                dve.wait_ge(norm_hi, nm.split_tiles + j + 1)
                nc.vector.scalar_tensor_tensor(out=dst_lo[:, j, :], in0=tnorm[j % 2][:, :n], scalar=shift(j),
                                               in1=dst_hi[:, j, :].bitcast(F32), op0=ALU.add,
                                               op1=ALU.subtract).then_inc(norm_lo, 1)

            for j in range(KT):
                if nm.tiles + j >= 2:
                    dve.wait_ge(norm_lo, nm.tiles + j - 1)
                nc.vector.scalar_tensor_tensor(out=tnorm[j % 2][:, :n], in0=src[:, j, :], scalar=gain(j),
                                               in1=rstd[:, :n], op0=ALU.mult, op1=ALU.mult).then_inc(norm_scaled, 1)
                if j >= 1:
                    dve.wait_ge(norm_scaled, nm.split_tiles + j)
                    rest(j - 1)
            dve.wait_ge(norm_scaled, nm.split_tiles + KT)
            rest(KT - 1)

        def rms_dve(dve, nm, gain):
            dve.wait_ge(norm_std, nm.once + 1)
            nc.vector.reciprocal(rstd[:], std[:]).then_inc(norm_rstd, 1)
            dve.wait_ge(norm_rstd, nm.once + 1)
            for j in range(KT):
                nc.vector.scalar_tensor_tensor(out=res[:, j, :], in0=res[:, j, :], scalar=gain(j), in1=rstd[:],
                                               op0=ALU.mult, op1=ALU.mult).then_inc(norm_lo, 1)

        def col(name, j, n=1):
            return cols[:, COLS[name] + j:COLS[name] + j + n]

        def level_step(c0, r, c):
            return (c0 // 2) * 2 * (LEVELS + 1) + 2 * r + c - c0

        def pair_halves(tensor_of, c, l, h=None):
            t = tensor_of[:, c, 0, 0 if h is None else h, :]
            n = HEADS * P if h is None else P
            return bass.AP(tensor=t.tensor, offset=t.offset,
                           ap=[list(t.ap[0]), [2 << l, n >> (l + 1)], [HEADS * P + (1 << l), 2], [1, 1 << l]])

        def halves(flat, l, right):
            return flat.rearrange("p (b h i) -> p b h i", h=2, i=1 << l)[:, :, int(right), :]

        def half_decay(t_in, d, l, right):
            t = t_in.rearrange("p (d b h) -> p d b h", d=2, h=2)[:, d, :, int(right):int(right) + 1]
            return t.to_broadcast([P, t.shape[1], 1 << l])

        def decay_keys(k_of, t_in, l, t_out):
            fwd, bwd = (k_of[:, d].rearrange("p h n -> p (h n)") for d in range(2))
            nc.vector.tensor_tensor(halves(fwd, l, False), halves(fwd, l, False), half_decay(t_in, 1, l, True), ALU.mult)
            ins = nc.vector.tensor_tensor(halves(bwd, l, True), halves(bwd, l, True), half_decay(t_in, 0, l, False),
                                          ALU.mult)
            if t_out is not None:
                t = t_in.rearrange("p (b h) -> p b h", h=2)
                ins = nc.vector.tensor_tensor(t_out, t[:, :, 0], t[:, :, 1], ALU.mult)
            return ins

        def decay_queries(c, t_in, l):
            bwd, fwd = (hq[:, c, d].rearrange("p h n -> p (h n)") for d in range(2))
            nc.vector.tensor_tensor(halves(fwd, l, True), halves(fwd, l, True), half_decay(t_in, 1, l, False), ALU.mult)
            nc.vector.tensor_tensor(halves(bwd, l, False), halves(bwd, l, False), half_decay(t_in, 0, l, True), ALU.mult)

        S_ENTER_F = [s_init[:, 0]] + [hk[:, c, 0] for c in range(LT - 1)]
        S_ENTER_B = [hk[:, c + 1, 1] for c in range(LT - 1)] + [s_init[:, 1]]
        UPDATES = [(0, 0), (LT - 1, 1), (1, 0), (LT - 2, 1), (2, 0), (LT - 3, 1)]

        JX = {"turn": 0, "gates": 8, "q": 16, "merge": 28, "up": 44, "turn2": 88, "ret": 88, "sw0": 88 + 10 * HEADS}
        JX["cin"] = JX["sw0"] + HT
        JX["sw1"] = JX["cin"] + 16
        JX["end"] = JX["sw1"] + HT
        JY = {"turn": 0, "gates": 8, "merge": 16, "out": 32, "down": 40, "turn2": 48, "ret": 56,
              "sw0": 56 + 16 * HEADS}
        JY["sd0"] = JY["sw0"] + HT
        JY["cin"] = JY["sd0"] + 8
        JY["cout"] = JY["cin"] + 8
        JY["sw1"] = JY["cout"] + 8
        JY["sd1"] = JY["sw1"] + HT
        JY["end"] = JY["sd1"] + 8

        def before(base_count, i, per):
            return base_count if i is None else i * per + base_count

        def take_x(pe, job, i=None, per=0):
            if job >= 2:
                pe.wait_ge(x_free, before(job - 1, i, per))
            return bx[job % 2]

        def take_y(pe, job, i=None, per=0):
            if job >= 2:
                pe.wait_ge(y_free, before(job - 1, i, per))
            return by[job % 2]

        def down_jobs(first_block):
            for ct in range(KT):
                yield ct, [(Block(first_block + (ct * HT + k) // KT), (ct * HT + k) % KT, k) for k in range(HT)]

        block = ctx.enter_context(nc.Block())

        @block.sync
        def _(sp):
            sp.dma_start(cols[:], cols_in).then_inc(cols_landed, 16)
            sp.dma_start(x_tok[:], x_in).then_inc(x_landed, 16)
            sp.dma_start(ident[:], ident_in).then_inc(ident_landed, 16)
            sp.dma_start(ctx_tok[:], ctx1_in).then_inc(ctx_landed, 16)
            for s in range(RAW):
                sp.dma_start(w_raw[s][:], wstream[s]).then_inc(raw_ready[s], 16)
            for n in range(4):
                sp.dma_start(ada_w0[:, 4 * n:4 * n + 4, :], ada_kn[4 * n:4 * n + 4].rearrange("a p n -> p a n"))\
                    .then_inc(ada0_in[n], 16)
            for n in range(3):
                sp.dma_start(crow[:, n, :], crow_in[n:n + 1, :].to_broadcast([P, D])).then_inc(crow_landed, 16)
            sp.dma_start(dft1[:], dft1_in).then_inc(dft1_landed, 16)
            sp.dma_start(masks[:], masks_in).then_inc(masks_landed, 16)
            with sp.Fori(0, N_BLOCKS // RAW - 1) as i:
                for s in range(RAW):
                    n = i * RAW + (s + RAW)
                    sp.wait_ge(lo_ready, i * RAW + (s + 1))
                    sp.dma_start(w_raw[s][:], wstream[bass.ds(n, 1)].rearrange("o p n -> (o p) n"))\
                        .then_inc(raw_ready[s], 16)
            for t in range(LT):
                sp.wait_ge(out_copied, 2 * t + 2)
                sp.dma_start(out[t * P:(t + 1) * P, :], out_tok[:, t, :]).then_inc(out_stored, 16)
            sp.wait_ge(out_stored, 16 * LT)

        def turn_pe(pe, src_tok, dst_tiles, take, job0, done):
            for j in range(KT):
                b = take(pe, job0 + j)
                for t in range(dst_tiles):
                    ins = nc.tensor.transpose(b[:, t * P:(t + 1) * P], src_tok[:, t, j * P:(j + 1) * P], ident[:])
                ins.then_inc(done, 1)

        def hidden_down_pe(pe, first_block, job0, hid_ready, i_ready):
            for ct, tiles in down_jobs(first_block):
                dst = take_y(pe, job0 + ct)
                for b, t, k in tiles:
                    if t == 0 or k == 0:
                        pe.wait_ge(lo_ready, b.count(1))
                    if ct == 0:
                        pe.wait_ge(hid_ready, k + 1)
                    wh, wl = wtile(b, t)
                    ins = three(dst[:], [(wh, wl, hid_hi[:, k, :], hid_lo[:, k, :])], k == 0, k == HT - 1)
                    if t == KT - 1:
                        ins.then_inc(block_done, 1)
                if tiles[-1][1] != KT - 1:
                    ins.then_inc(down_done[first_block], 1)

        down_done = {B_DOWN: sem("down_done0"), B_SD0: sem("down_done1"), B_SD1: sem("down_done2")}

        def swiglu_pe(pe, first_block, jx, jy, nm):
            with pe.Fori(0, HT // 2) as i:
                for u in range(2):
                    for kind in range(2):
                        b = Block(first_block + 2 * u + kind, i, 4)
                        dst = (take_x if kind == 0 else take_y)(pe, (jx if kind == 0 else jy) + u, i, 2)
                        pe.wait_ge(lo_ready, b.count(1))
                        for k in range(KT):
                            if u == 0 and kind == 0:
                                pe.wait_ge(norm_lo, nm.tiles + k + 1)
                            wh, wl = wtile(b, k)
                            ins = three(dst[:], [(wh, wl, hx_hi[:, k, :], hx_lo[:, k, :])], k == 0, k == KT - 1)
                        ins.then_inc(block_done, 1)

        def square_pe(pe, first_block, jy, m_hi_, m_lo_, ready):
            for j in range(KT):
                b = Block(first_block + j)
                dst = take_y(pe, jy + j)
                pe.wait_ge(lo_ready, b.count(1))
                for k in range(KT):
                    if j == 0:
                        pe.wait_ge(ready, k + 1)
                    wh, wl = wtile(b, k)
                    ins = three(dst[:], [(wh, wl, m_hi_[:, k, :], m_lo_[:, k, :])], k == 0, k == KT - 1)
                ins.then_inc(block_done, 1)

        def values_pe(pe, b0, dsts, i=None, per=0):
            for n in range(4):
                b = Block(b0 + n, i, per)
                pe.wait_ge(lo_ready, b.count(1))
                for r in range(2):
                    k = 2 * n + r
                    wh, wl = wrow(b, r)
                    for t in range(LT + LCT):
                        if t < LT:
                            sh, sl = (h[:, k, t * P:(t + 1) * P] for h in (hx_hi, hx_lo))
                        else:
                            sh, sl = (h[:, k, (t - LT) * P:(t - LT + 1) * P] for h in (hc_hi, hc_lo))
                        ins = three(dsts[t][:], [(sh, sl, wh, wl)], k == 0, k == KT - 1)
                ins.then_inc(block_done, 1)

        six = [bx[0], bx[1], by[0], by[1], bw[0], bw[1]]

        @block.tensor
        def _(pe):
            pe.wait_ge(ident_landed, 16)
            pe.wait_ge(x_landed, 16)
            turn_pe(pe, x_tok, LT, take_x, JX["turn"], turned)
            pe.wait_ge(ctx_landed, 16)
            turn_pe(pe, ctx_tok, LCT, take_y, JY["turn"], turned)
            pe.wait_ge(consts, 2)
            norm_pe(pe, n1x, L, bn)
            pe.wait_ge(scol_ready, 1)
            for a in range(16):
                if a % 4 == 0:
                    pe.wait_ge(ada0_in[a // 4], 16)
                for k in range(KT):
                    ins = nc.tensor.matmul(bw[0][:, 2 * a:2 * a + 2], ada_w0[:, a, k * P:(k + 1) * P],
                                           scol[:, :, k], start=(k == 0), stop=(k == KT - 1))
            ins.then_inc(ada0_mm, 1)
            norm_pe(pe, n1c, LC, bank[4])
            for n in range(8):
                b = Block(B_GATES + n)
                dx, dc = take_x(pe, JX["gates"] + n), take_y(pe, JY["gates"] + n)
                pe.wait_ge(lo_ready, b.count(1))
                for k in range(KT):
                    if n == 0:
                        pe.wait_ge(norm_lo, n1x.tiles + k + 1)
                    wh, wl = wtile(b, k)
                    three(dx[:], [(wh, wl, hx_hi[:, k, :], hx_lo[:, k, :])], k == 0, k == KT - 1)
                for k in range(KT):
                    if n == 0:
                        pe.wait_ge(norm_lo, n1c.tiles + k + 1)
                    wh, wl = wtile(b, k)
                    ins = three(dc[:, :LC], [(wh, wl, hc_hi[:, k, :], hc_lo[:, k, :])], k == 0, k == KT - 1)
                ins.then_inc(block_done, 1)
            pe.wait_ge(x_free, JX["q"])
            pe.wait_ge(y_free, JY["merge"])
            pe.wait_ge(ada0_ready, 1)
            values_pe(pe, B_VAL, six)
            pe.wait_ge(v_ready, 6)
            for n in range(12):
                b = Block(B_Q + n)
                dst = take_x(pe, JX["q"] + n)
                pe.wait_ge(lo_ready, b.count(1))
                for k in range(KT):
                    wh, wl = wtile(b, k)
                    ins = three(dst[:], [(wh, wl, hx_hi[:, k, :], hx_lo[:, k, :])], k == 0, k == KT - 1)
                ins.then_inc(block_done, 1)
            pe.wait_ge(kc_level, LEVELS + 1)
            for g in range(4):
                if g >= 2:
                    pe.wait_ge(kd_ready, g - 1)
                for hh in range(2):
                    h = 2 * (g % 2) + hh
                    for t in range(LCT):
                        ins = nc.tensor.transpose(bw[g % 2][:, (2 * hh + t) * P:(2 * hh + t + 1) * P],
                                                  kc[:, g // 2, h, t * P:(t + 1) * P], ident[:])
                ins.then_inc(kc_turned, 1)
            pe.wait_ge(kd_ready, 4)
            for d in range(2):
                for h in range(HEADS):
                    for t in range(LCT):
                        ins = nc.tensor.matmul(bank[4 + d][:, h * P:(h + 1) * P], kd_c[:, d, h, t, :],
                                               v_c[:, t, h * P:(h + 1) * P], start=(t == 0), stop=(t == LCT - 1))
                ins.then_inc(s0_mm, 1)
            pe.wait_ge(x_free, JX["merge"])
            for c0 in (0, 2):
                for r in range(LEVELS + 1):
                    for c in (c0, c0 + 1):
                        pe.wait_ge(level_ready, level_step(c0, r, c) + 1)
                        if r >= 1:
                            pe.wait_ge(k_gathered, level_step(c0, r, c) - 2 * (c0 // 2) - 1)
                        for h in range(HEADS):
                            dst = bw[c % 2][:, h * P:(h + 1) * P]
                            if r == 0:
                                ins = nc.tensor.matmul(dst, ksum[c % 2][:, h, :], hq[:, c, 0, h, :],
                                                       start=True, stop=True)
                            else:
                                ins = nc.tensor.matmul(dst, level_k[c % 2][:, h * P:(h + 1) * P],
                                                       pair_halves(hq, c, r - 1, h), start=True, stop=True)
                        ins.then_inc(level_mm, 1)
            for n, (c, d) in enumerate(UPDATES):
                pe.wait_ge(chunk_ready, c + 1)
                if n >= 2:
                    pe.wait_ge(kd_copied, n - 1)
                for h in range(HEADS):
                    ins = nc.tensor.transpose(bx[n % 2][:, h * P:(h + 1) * P], hk[:, c, d, h, :], ident[:])
                ins.then_inc(k_turned, 1)
                pe.wait_ge(kd_copied, n + 1)
                if n >= 2:
                    pe.wait_ge(upd_done, n - 1)
                for h in range(HEADS):
                    ins = nc.tensor.matmul(by[n % 2][:, h * P:(h + 1) * P], kd_x[n % 2][:, h, :],
                                           v_x[:, c, h * P:(h + 1) * P], start=True, stop=True)
                ins.then_inc(upd_mm, 1)
            pe.wait_ge(upd_done, len(UPDATES))
            for c in range(LT):
                if c >= 2:
                    pe.wait_ge(osq_ready, c - 1)
                for h in range(HEADS):
                    dst = bw[c % 2][:, h * P:(h + 1) * P]
                    nc.tensor.matmul(dst, v_x[:, c, h * P:(h + 1) * P], att[c][:, h, :], start=True, stop=False)
                    nc.tensor.matmul(dst, S_ENTER_F[c][:, h, :], hq[:, c, 1, h, :], start=False, stop=False)
                    ins = nc.tensor.matmul(dst, S_ENTER_B[c][:, h, :], hq[:, c, 0, h, :], start=False, stop=True)
                ins.then_inc(o_mm, 1)
            for c in range(LT):
                pe.wait_ge(osq_ready, c + 1)
                if c >= 1:
                    pe.wait_ge(ostd, c)
                nc.tensor.matmul(bn[:], ones[:], sq[c % 2][:], start=True, stop=True).then_inc(osum_mm, 1)
            pe.wait_ge(dft1_landed, 16)
            for t in range(LT):
                for gp in range(2):
                    n = 2 * t + gp
                    if n >= 2:
                        pe.wait_ge(pq_ready, n - 1)
                    else:
                        pe.wait_ge(o_ready, LT)
                    for g in (2 * gp, 2 * gp + 1):
                        ins = nc.tensor.matmul(bw[n % 2][:, (g % 2) * 2 * P:(g % 2 + 1) * 2 * P],
                                               ut[:, g, t * P:(t + 1) * P], dft1[:], start=True, stop=True)
                    ins.then_inc(pq_mm, 1)
            pe.wait_ge(pq_ready, 2 * LT)
            pe.wait_ge(dft2_landed, 16)
            for g in range(HEADS):
                if g >= 2:
                    pe.wait_ge(ya_l, g - 1)
                for cs in range(2):
                    for t in range(LT):
                        ins = nc.tensor.matmul(bw[g % 2][:], pq[:, t, g, cs * P:(cs + 1) * P], dft2[:, cs, t, :],
                                               start=(cs == 0 and t == 0), stop=(cs == 1 and t == LT - 1))
                ins.then_inc(ya_mm, 1)
            pe.wait_ge(kd_copied, len(UPDATES))
            with pe.Fori(0, 2) as i:
                for u in range(4):
                    for kind in range(2):
                        b = Block(B_MERGE + 3 * u + kind, i, 12)
                        dst = take_x(pe, JX["merge"] + 2 * u + kind, i, 8)
                        pe.wait_ge(lo_ready, b.count(1))
                        for k in range(KT):
                            wh, wl = wtile(b, k)
                            ins = three(dst[:], [(wh, wl, hx_hi[:, k, :], hx_lo[:, k, :])], k == 0, k == KT - 1)
                        ins.then_inc(block_done, 1)
                    b = Block(B_MERGE + 3 * u + 2, i, 12)
                    pe.wait_ge(lo_ready, b.count(1))
                    pe.wait_ge(ya_l, HEADS)
                    pe.wait_ge(yb_l, LT)
                    for br, (yh, yl) in enumerate(((ya_hi, ya_lo), (yb_hi, yb_lo))):
                        dst = take_y(pe, JY["merge"] + 2 * u + br, i, 8)
                        for k in range(HEADS):
                            wh, wl = wtile(b, HEADS * br + k)
                            ins = three(dst[:], [(wh, wl, yh[:, k, :], yl[:, k, :])], k == 0, k == HEADS - 1)
                    ins.then_inc(block_done, 1)
            square_pe(pe, B_OUT, JY["out"], m_hi, m_lo, m_l)
            norm_pe(pe, n2, L, bn)
            with pe.Fori(0, HT // 2) as i:
                for u in range(4):
                    b = Block(B_UP + u, i, 4)
                    dst = take_x(pe, JX["up"] + u, i, 4)
                    pe.wait_ge(lo_ready, b.count(1))
                    for k in range(KT):
                        if u == 0:
                            pe.wait_ge(norm_lo, n2.tiles + k + 1)
                        wh, wl = wtile(b, k)
                        ins = three(dst[:], [(wh, wl, hx_hi[:, k, :], hx_lo[:, k, :])], k == 0, k == KT - 1)
                    ins.then_inc(block_done, 1)
            hidden_down_pe(pe, B_DOWN, JY["down"], hid_l, None)
            norm_pe(pe, nf1, L, bn)
            pe.wait_ge(ctx2_landed, 16)
            turn_pe(pe, ctx2_tok, LCT, take_y, JY["turn2"], turned2)
            norm_pe(pe, nmx, L, bn)
            norm_pe(pe, nmc, LC, bank[4])
            with pe.Fori(0, HEADS) as i:
                jx, jy = JX["ret"], JY["ret"]
                for n in range(4):
                    b = Block(B_RET + n, i, 16)
                    dst = take_y(pe, jy + n, i, 16)
                    pe.wait_ge(lo_ready, b.count(1))
                    for k in range(KT):
                        if n == 0:
                            pe.wait_ge(norm_lo, nmx.tiles + k + 1)
                        wh, wl = wtile(b, k)
                        ins = three(dst[:], [(wh, wl, hx_hi[:, k, :], hx_lo[:, k, :])], k == 0, k == KT - 1)
                    if n >= 2:
                        dc = take_x(pe, jx + n - 2, i, 10)
                        pe.wait_ge(norm_lo, nmc.tiles + KT)
                        for t in range(LCT):
                            for k in range(KT):
                                wh, wl = wtile(b, k)
                                ins = three(dc[:, t * P:(t + 1) * P],
                                            [(hc_hi[:, k, t * P:(t + 1) * P], hc_lo[:, k, t * P:(t + 1) * P], wh, wl)],
                                            k == 0, k == KT - 1)
                    ins.then_inc(block_done, 1)
                pe.wait_ge(x_free, before(jx + 2, i, 10))
                pe.wait_ge(y_free, before(jy + 4, i, 16))
                values_pe(pe, B_RET + 4, six, i, 16)
                pe.wait_ge(rv_done, before(6, i, 6))
                for n in range(4):
                    b = Block(B_RET + 8 + n, i, 16)
                    dst = take_x(pe, jx + 2 + n, i, 10)
                    pe.wait_ge(lo_ready, b.count(1))
                    for k in range(KT):
                        wh, wl = wtile(b, k)
                        ins = three(dst[:], [(wh, wl, hx_hi[:, k, :], hx_lo[:, k, :])], k == 0, k == KT - 1)
                    ins.then_inc(block_done, 1)
                for d in range(2):
                    for dt in range(2):
                        n = 2 * d + dt
                        if n >= 2:
                            pe.wait_ge(st_done, before(n - 1, i, 4))
                        for t in range(LCT):
                            ins = nc.tensor.matmul(bw[n % 2][:], rkc[:, d, t, dt * P:(dt + 1) * P], rvc[:, t, :],
                                                   start=(t == 0), stop=(t == LCT - 1))
                        ins.then_inc(st_mm, 1)
                pe.wait_ge(rot_done, before(4, i, 4))
                for s in range(LT):
                    dst = take_y(pe, jy + 4 + s, i, 16)
                    for dt in range(2):
                        ins = nc.tensor.matmul(dst[:], rk[:, dt, s * P:(s + 1) * P], rq[:, dt, :],
                                               start=(dt == 0), stop=(dt == 1))
                    ins.then_inc(sc_mm, 1)
                pe.wait_ge(y_free, before(jy + 8, i, 16))
                pe.wait_ge(qd_done, before(4, i, 4))
                pe.wait_ge(st_done, before(4, i, 4))
                for e in range(HEADS):
                    dst = take_x(pe, jx + 6 + e, i, 10)
                    for s in range(LT):
                        nc.tensor.matmul(dst[:], rv[:, s, e * P:(e + 1) * P], rsc[:, s, :], start=(s == 0), stop=False)
                    for d in range(2):
                        for dt in range(2):
                            ins = nc.tensor.matmul(dst[:], rst[:, d, dt, e * P:(e + 1) * P], rqd[:, d, dt, :],
                                                   start=False, stop=(d == 1 and dt == 1))
                    ins.then_inc(ro_mm, 1)
                    if e >= 1:
                        pe.wait_ge(x_free, before(jx + 6 + e, i, 10))
                        nc.tensor.matmul(bn[:], ones[:], rsq[(e - 1) % 2][:], start=(e == 1), stop=False)\
                            .then_inc(rsum_mm, 1)
                pe.wait_ge(x_free, before(jx + 10, i, 10))
                nc.tensor.matmul(bn[:], ones[:], rsq[(HEADS - 1) % 2][:], start=False, stop=True).then_inc(rsum_mm, 1)
                for n in range(4):
                    b = Block(B_RET + 12 + n, i, 16)
                    pe.wait_ge(lo_ready, b.count(1))
                    for u in range(2):
                        dst = take_y(pe, jy + 8 + 2 * n + u, i, 16)
                        for k in range(HEADS):
                            if n == 0 and u == 0:
                                pe.wait_ge(ry_l, before(k + 1, i, HEADS))
                            wh, wl = wtile(b, HEADS * u + k)
                            ins = three(dst[:], [(wh, wl, ry_hi[:, k, :], ry_lo[:, k, :])], k == 0, k == HEADS - 1)
                    ins.then_inc(block_done, 1)
            norm_pe(pe, nffn0, L, bn)
            swiglu_pe(pe, B_SW0, JX["sw0"], JY["sw0"], nffn0)
            hidden_down_pe(pe, B_SD0, JY["sd0"], sw_l[0], None)
            norm_pe(pe, nmix1, L, bn)
            with pe.Fori(0, 2) as i:
                for u in range(4):
                    for kind in range(3):
                        b = Block(B_CIN + 3 * u + kind, i, 12)
                        if kind < 2:
                            dst = take_x(pe, JX["cin"] + 2 * u + kind, i, 8)
                        else:
                            dst = take_y(pe, JY["cin"] + u, i, 4)
                        pe.wait_ge(lo_ready, b.count(1))
                        for k in range(KT):
                            if u == 0 and kind == 0:
                                pe.wait_ge(norm_lo, nmix1.tiles + k + 1)
                            wh, wl = wtile(b, k)
                            ins = three(dst[:], [(wh, wl, hx_hi[:, k, :], hx_lo[:, k, :])], k == 0, k == KT - 1)
                        ins.then_inc(block_done, 1)
            square_pe(pe, B_COUT, JY["cout"], cy_hi, cy_lo, cy_l)
            norm_pe(pe, nffn1, L, bn)
            swiglu_pe(pe, B_SW1, JX["sw1"], JY["sw1"], nffn1)
            hidden_down_pe(pe, B_SD1, JY["sd1"], sw_l[1], None)
            norm_pe(pe, nf2, L, bn)
            pe.wait_ge(norm_lo, nf2.tiles + KT)
            for t in range(LT):
                for half in range(2):
                    n = 2 * t + half
                    if n >= 2:
                        pe.wait_ge(out_copied, n - 1)
                    for j in range(4):
                        ins = nc.tensor.transpose(bw[n % 2][:, j * P:(j + 1) * P],
                                                  res[:, 4 * half + j, t * P:(t + 1) * P], ident[:])
                    ins.then_inc(turned_out, 1)

        def swiglu_act(act, w, first_block, jx, jy, ada0_at):
            with act.Fori(0, HT // 2) as i:
                for u in range(2):
                    b = Block(first_block + 2 * u, i, 4)
                    split_hi(act, b)
                    if ada0_at is not None:
                        ada_load(act, ada0_at + 2 * u, i, 4)
                    act.wait_ge(block_done, b.count(1))
                    act.wait_ge(lo_ready, b.count(AHEAD - 1))
                    nc.scalar.activation(sw[u][:], bx[(jx + u) % 2][:], ACT.Silu).then_inc(x_free, 1)
                    split_hi(act, b.plus(1))
                    if ada0_at is not None:
                        ada_load(act, ada0_at + 2 * u + 1, i, 4)
                    act.wait_ge(y_free, before(jy + u + 1, i, 2))
                    nc.scalar.activation(hid_hi[:, bass.ds(i * 2 + u, 1), :].rearrange("p o n -> p (o n)"), sw[u][:],
                                         ACT.Copy).then_inc(sw_h[w], 1)

        def osqrt(act, c):
            act.wait_ge(osum_mm, c + 1)
            if c >= 1:
                act.wait_ge(orstd, c)
            nc.scalar.activation(std[:], bn[:], ACT.Sqrt, scale=1.0 / P, bias=eps_col[:]).then_inc(ostd, 1)

        def none(j):
            pass

        @block.scalar
        def _(act):
            act.wait_ge(cols_landed, 16)
            nc.scalar.activation(scol[:], cols[:, COLS["c"]:COLS["c"] + 16].rearrange("p (v k) -> p v k", v=2),
                                 ACT.Silu).then_inc(scol_ready, 1)
            for j in range(KT):
                act.wait_ge(turned, j + 1)
                nc.scalar.activation(res[:, j, :], bx[j % 2][:], ACT.Copy).then_inc(x_free, 1)
            for j in range(KT):
                act.wait_ge(turned, KT + j + 1)
                nc.scalar.activation(ctx_t[:, j, :], by[j % 2][:, :LC], ACT.Copy).then_inc(y_free, 1)
            for b in range(RAW):
                split_hi(act, Block(b - AHEAD))
            act.wait_ge(crow_landed, 48)
            nc.scalar.activation(crow[:], crow[:], ACT.Silu).then_inc(crow_silu, 1)
            act.wait_ge(consts, 2)
            act.wait_ge(lb_ready, 1)
            nc.scalar.activation(lb[:], oml[:], ACT.Sigmoid).then_inc(lb_ready, 1)

            def own(s, n0):
                return lambda j: act.wait_ge(s, n0 + j + 1)
            norm_act(act, n1x, res, L, bn, own(x_free, JX["turn"]), lambda j: ada0[:, j, 0:1], hx_hi)
            norm_act(act, n1c, ctx_t, LC, bank[4], own(y_free, JY["turn"]), lambda j: ada0[:, j, 1:2], hc_hi)
            for b in range(RAW, AHEAD):
                split_hi(act, Block(b - AHEAD))
            act.wait_ge(norm_lo, n1c.tiles + KT)
            act.wait_ge(lb_ready, 3)
            for n in range(8):
                b = Block(B_GATES + n)
                d, h = n // HEADS, n % HEADS
                split_hi(act, b)
                act.wait_ge(block_done, b.count(1))
                if n >= 2:
                    act.wait_ge(f_ready, 2 * n - 2)
                nc.scalar.activation(sig[n % 2][:, :L], bx[n % 2][:], ACT.Sigmoid).then_inc(x_free, 1)
                nc.scalar.activation(sig[n % 2][:, L:], by[n % 2][:, :LC], ACT.Sigmoid).then_inc(y_free, 1)
                act.wait_ge(x_free, JX["gates"] + n + 1)
                nc.scalar.activation(hf[:, :, 1 - d, h, :], sig[n % 2][:, :L].rearrange("p (c t) -> p c t", c=LT),
                                     ACT.Identity, scale=oml[:, h:h + 1], bias=lb[:, h:h + 1]).then_inc(f_ready, 1)
                act.wait_ge(y_free, JY["gates"] + n + 1)
                nc.scalar.activation(fc[:, 1 - d, h, :], sig[n % 2][:, L:], ACT.Identity, scale=oml[:, h:h + 1],
                                     bias=lb[:, h:h + 1]).then_inc(f_ready, 1)
            for n in range(4):
                split_hi(act, Block(B_VAL + n))
            act.wait_ge(block_done, B_VAL + 4)
            for t in range(LT + LCT):
                dst = v_x[:, t, :] if t < LT else v_c[:, t - LT, :]
                nc.scalar.activation(dst, six[t][:], ACT.Copy).then_inc(v_ready, 1)
            for n in range(12):
                b = Block(B_Q + n)
                h = n % HEADS
                split_hi(act, b)
                if n < 8:
                    if n == 0:
                        act.wait_ge(crow_silu, 1)
                    ada_load(act, n)
                act.wait_ge(block_done, b.count(1))
                src = bx[n % 2][:]
                if n < 4:
                    for d in range(2):
                        ins = nc.scalar.activation(hq[:, :, d, h, :], src.rearrange("p (c t) -> p c t", c=LT),
                                                   ACT.Silu)
                    ins.then_inc(x_free, 1)
                elif n < 8:
                    nc.scalar.activation(ut[:, h, :], src, ACT.Copy).then_inc(x_free, 1)
                else:
                    nc.scalar.activation(gs[:, h, :], src, ACT.Silu).then_inc(x_free, 1)
            act.wait_ge(x_free, JX["merge"])
            for h in range(HEADS):
                nc.scalar.activation(gs[:, h, :], gs[:, h, :], ACT.Copy, scale=col("onorm", h)).then_inc(gs_ready, 1)
            for g in range(4):
                act.wait_ge(kc_turned, g + 1)
                nc.scalar.activation(kd_c[:, g // 2, 2 * (g % 2):2 * (g % 2) + 2, :, :].rearrange("p h t n -> p (h t n)"),
                                     bw[g % 2][:], ACT.Copy).then_inc(kd_ready, 1)
            for d in range(2):
                act.wait_ge(s0_mm, d + 1)
                nc.scalar.activation(s_init[:, d, :, :].rearrange("p h n -> p (h n)"), bank[4 + d][:], ACT.Copy)\
                    .then_inc(s_ready, 1)
            for c0 in (0, 2):
                for r in range(1, LEVELS + 1):
                    for c in (c0, c0 + 1):
                        n = level_step(c0, r, c)
                        act.wait_ge(level_ready, n + 1)
                        if r >= 2:
                            act.wait_ge(level_mm, n - 1)
                        nc.scalar.activation(level_k[c % 2][:].rearrange(
                            "p (b h i) -> p b h i", h=2, i=1 << (r - 1)), pair_halves(hk, c, r - 1), ACT.Copy)\
                            .then_inc(k_gathered, 1)
            for n in range(len(UPDATES)):
                act.wait_ge(k_turned, n + 1)
                if n >= 2:
                    act.wait_ge(upd_mm, n - 1)
                nc.scalar.activation(kd_x[n % 2][:].rearrange("p h n -> p (h n)"), bx[n % 2][:], ACT.Copy)\
                    .then_inc(kd_copied, 1)
            for c in range(LT):
                act.wait_ge(o_mm, c + 1)
                nc.scalar.activation(ho[:, c, 0, :, :].rearrange("p h n -> p (h n)"), bw[c % 2][:], ACT.Copy)\
                    .then_inc(o_ready, 1)
                if c >= 2:
                    act.wait_ge(osum_mm, c - 1)
                nc.scalar.activation(sq[c % 2][:], bw[c % 2][:], ACT.Square).then_inc(osq_ready, 1)
                if c >= 1:
                    osqrt(act, c - 1)
            for c in range(LT):
                if c == 1:
                    osqrt(act, LT - 1)
                act.wait_ge(yb_f, c + 1)
                nc.scalar.activation(yb_hi[:, :, c * P:(c + 1) * P],
                                     yt[c % 2][:].rearrange("p (h n) -> p h n", h=HEADS), ACT.Copy).then_inc(yb_h, 1)
            act.wait_ge(o_mm, LT)
            act.dma_start(dft2[:], dft2_in).then_inc(dft2_landed, 16)
            for n in range(2 * LT):
                act.wait_ge(pq_mm, n + 1)
                nc.scalar.activation(pq[:, n // 2, 2 * (n % 2):2 * (n % 2) + 2, :].rearrange("p g n -> p (g n)"),
                                     bw[n % 2][:], ACT.Copy).then_inc(pq_ready, 1)
            for g in range(HEADS):
                act.wait_ge(ya_mm, g + 1)
                nc.scalar.activation(ya_hi[:, g, :], bw[g % 2][:], ACT.Copy).then_inc(ya_h, 1)
            act.wait_ge(yb_l, LT)
            act.wait_ge(ya_l, HEADS)
            with act.Fori(0, 2) as i:
                for u in range(4):
                    for kind in range(2):
                        b = Block(B_MERGE + 3 * u + kind, i, 12)
                        split_hi(act, b)
                        ada_load(act, 8 + 3 * u + kind, i, 12)
                        act.wait_ge(block_done, b.count(1))
                        nc.scalar.activation((gate_a if kind == 0 else gate_b)[u % 2][:], bx[kind][:], ACT.Sigmoid)\
                            .then_inc(x_free, 1)
                    b = Block(B_MERGE + 3 * u + 2, i, 12)
                    split_hi(act, b)
                    ada_load(act, 8 + 3 * u + 2, i, 12)
                    act.wait_ge(m_f, before(u + 1, i, 4))
                    nc.scalar.activation(m_hi[:, bass.ds(i * 4 + u, 1), :].rearrange("p o n -> p (o n)"), mt[u % 2][:],
                                         ACT.Copy).then_inc(m_h, 1)
            for j in range(KT):
                split_hi(act, Block(B_OUT + j))
            act.wait_ge(m_l, KT)
            norm_act(act, n2, res, L, bn, own(y_free, JY["out"]), lambda j: ada[:, 8 + j:9 + j], hx_hi)
            act.wait_ge(norm_lo, n2.tiles + KT)
            act.wait_ge(z_zero, 4)
            with act.Fori(0, HT // 2) as i:
                for u in range(4):
                    b = Block(B_UP + u, i, 4)
                    s, k = u // 2, u % 2
                    split_hi(act, b)
                    act.wait_ge(block_done, b.count(1))
                    act.wait_ge(lo_ready, b.plus(AHEAD - u).count(1))
                    cw = i * 40 + (COLS["conv"] + 20 * s + 10 * k)
                    src = bx[u % 2][:].rearrange("p (r c) -> p r c", r=ROWS)
                    nc.scalar.activation(zpad[s][k][:, 1:ROWS + 1, 1:GRID + 1], src, ACT.Copy)
                    nc.scalar.activation(acc[s][k][:], src, ACT.Identity, scale=cols[:, bass.ds(cw + 4, 1)],
                                         bias=cols[:, bass.ds(cw + 9, 1)]).then_inc(x_free, 1)
                for s in range(2):
                    act.wait_ge(tap_done, before(16 * s + 15, i, 32))
                    nc.scalar.activation(acc[s][0][:], acc[s][0][:], ACT.Silu).then_inc(silu_done, 1)
                for s in range(2):
                    act.wait_ge(hid_f, before(s + 1, i, 2))
                    nc.scalar.activation(hid_hi[:, bass.ds(i * 2 + s, 1), :].rearrange("p o n -> p (o n)"),
                                         acc[s][1][:].rearrange("p r c -> p (r c)"), ACT.Copy).then_inc(hid_h, 1)
            for n in range(HT):
                split_hi(act, Block(B_DOWN + n))
                if n < 16:
                    ada_load(act, 32 + n)
            norm_act(act, nf1, res, L, bn, own(y_free, JY["down"]), None, None)
            act.wait_ge(block_done, B_RET)
            act.dma_start(ctx2_tok[:], ctx2_in).then_inc(ctx2_landed, 16)
            act.dma_start(rope[:], rope_in).then_inc(rope_landed, 16)
            for j in range(KT):
                act.wait_ge(turned2, j + 1)
                nc.scalar.activation(ctx2_t[:, j, :], by[j % 2][:, :LC], ACT.Copy).then_inc(y_free, 1)
            norm_act(act, nmx, res, L, bn, own(norm_lo, nf1.tiles), lambda j: ada[:, 32 + j:33 + j], hx_hi)
            norm_act(act, nmc, ctx2_t, LC, bank[4], own(y_free, JY["turn2"]), lambda j: ada_c[:, j:j + 1], hc_hi)
            act.wait_ge(norm_lo, nmc.tiles + KT)
            with act.Fori(0, HEADS) as i:
                jx, jy = JX["ret"], JY["ret"]
                act.wait_ge(y_free, before(jy - 8, i, 16))
                act.dma_start(dec[:], dec_in[bass.ds(i, 1)].rearrange("o p n -> (o p) n")).then_inc(dec_landed, 16)
                for n in range(4):
                    b = Block(B_RET + n, i, 16)
                    split_hi(act, b)
                    ada_load(act, 48 + n, i, 8)
                    if n >= 2:
                        act.wait_ge(block_done, b.count(1))
                        act.wait_ge(dec_landed, before(16, i, 16))
                        for d in range(2):
                            for t in range(LCT):
                                w = DEC_W + 2 * L + LCT * d + t
                                ins = nc.scalar.activation(rkc[:, d, t, (n - 2) * P:(n - 1) * P],
                                                           bx[n % 2][:, t * P:(t + 1) * P], ACT.Copy,
                                                           scale=dec[:, w:w + 1])
                        ins.then_inc(x_free, 1)
                for n in range(4):
                    split_hi(act, Block(B_RET + 4 + n, i, 16))
                    ada_load(act, 52 + n, i, 8)
                act.wait_ge(block_done, Block(B_RET + 7, i, 16).count(1))
                for t in range(LT + LCT):
                    dst = rv[:, t, :] if t < LT else rvc[:, t - LT, :]
                    nc.scalar.activation(dst, six[t][:], ACT.Copy).then_inc(rv_done, 1)
                for n in range(4):
                    b = Block(B_RET + 8 + n, i, 16)
                    split_hi(act, b)
                    act.wait_ge(block_done, b.count(1))
                    nc.scalar.activation(rg[:, n, :], bx[n % 2][:], ACT.Silu).then_inc(x_free, 1)
                for n in range(4):
                    act.wait_ge(st_mm, before(n + 1, i, 4))
                    nc.scalar.activation(rst[:, n // 2, n % 2, :], bw[n % 2][:], ACT.Copy).then_inc(st_done, 1)
                for e in range(HEADS):
                    act.wait_ge(ro_mm, before(e + 1, i, HEADS))
                    nc.scalar.activation(ro[:, e, :], bx[e % 2][:], ACT.Copy).then_inc(ro_done, 1)
                    if e >= 2:
                        act.wait_ge(rsum_mm, before(e - 1, i, HEADS))
                    nc.scalar.activation(rsq[e % 2][:], bx[e % 2][:], ACT.Square).then_inc(x_free, 1)
                act.wait_ge(rsum_mm, before(HEADS, i, HEADS))
                nc.scalar.activation(std[:], bn[:], ACT.Sqrt, scale=1.0 / L, bias=eps_col[:]).then_inc(rstd_s, 1)
                for e in range(HEADS):
                    act.wait_ge(ry_f, before(e + 1, i, HEADS))
                    nc.scalar.activation(ry_hi[:, e, :], rt[e % 2][:], ACT.Copy).then_inc(ry_h, 1)
                for n in range(4):
                    split_hi(act, Block(B_RET + 12 + n, i, 16))
            norm_act(act, nffn0, res, L, bn, own(y_free, JY["sw0"] - 8), lambda j: ada[:, 56 + 0 + j:57 + j], hx_hi)
            act.wait_ge(norm_lo, nffn0.tiles + KT)
            swiglu_act(act, 0, B_SW0, JX["sw0"], JY["sw0"], 80)
            for n in range(HT):
                split_hi(act, Block(B_SD0 + n))
                if n < 4:
                    ada_load(act, 124 + n)
            norm_act(act, nmix1, res, L, bn, own(y_free, JY["sd0"]), lambda j: ada[:, 80 + j:81 + j], hx_hi)
            act.wait_ge(block_done, B_CIN)
            with act.Fori(0, 2) as i:
                for u in range(4):
                    for kind in range(2):
                        b = Block(B_CIN + 3 * u + kind, i, 12)
                        split_hi(act, b)
                        act.wait_ge(block_done, b.count(1))
                        nc.scalar.activation((cb if kind == 0 else cc)[u % 2][:], bx[kind][:], ACT.Copy)\
                            .then_inc(x_free, 1)
                    b = Block(B_CIN + 3 * u + 2, i, 12)
                    split_hi(act, b)
                    act.wait_ge(cy_f, before(u + 1, i, 4))
                    nc.scalar.activation(cy_hi[:, bass.ds(i * 4 + u, 1), :].rearrange("p o n -> p (o n)"), cacc[u % 2][:],
                                         ACT.Copy).then_inc(cy_h, 1)
            for j in range(KT):
                split_hi(act, Block(B_COUT + j))
            norm_act(act, nffn1, res, L, bn, own(y_free, JY["cout"]), lambda j: ada[:, 104 + j:105 + j], hx_hi)
            act.wait_ge(norm_lo, nffn1.tiles + KT)
            act.wait_ge(block_done, B_SW1)
            swiglu_act(act, 1, B_SW1, JX["sw1"], JY["sw1"], None)
            for n in range(HT):
                split_hi(act, Block(B_SD1 + n))
            norm_act(act, nf2, res, L, bn, own(y_free, JY["sd1"]), None, None)
            for n in range(2 * LT):
                act.wait_ge(turned_out, n + 1)
                nc.scalar.activation(out_tok[:, n // 2, (n % 2) * L:(n % 2 + 1) * L], bw[n % 2][:], ACT.Copy)\
                    .then_inc(out_copied, 1)

        def swiglu_dve(dve, w, first_block, jy, ada_at):
            with dve.Fori(0, HT // 2) as i:
                for u in range(2):
                    b = Block(first_block + 2 * u, i, 4)
                    split_lo(dve, b)
                    if ada_at is not None:
                        ada_reduce(dve, ada_at + 2 * u, 1, i, 4)
                    split_lo(dve, b.plus(1))
                    if ada_at is not None:
                        ada_reduce(dve, ada_at + 2 * u + 1, 1, i, 4)
                    dve.wait_ge(block_done, b.count(2))
                    dve.wait_ge(x_free, before((JX["sw0"] if w == 0 else JX["sw1"]) + u + 1, i, 2))
                    nc.vector.tensor_tensor(sw[u][:], sw[u][:], by[(jy + u) % 2][:], ALU.mult).then_inc(y_free, 1)
                    dve.wait_ge(y_free, before(jy + u + 1, i, 2))
                    dve.wait_ge(sw_h[w], before(u + 1, i, 2))
                    hs = bass.ds(i * 2 + u, 1)
                    nc.vector.tensor_tensor(hid_lo[:, hs, :].rearrange("p o n -> p (o n)"), sw[u][:],
                                            hid_hi[:, hs, :].rearrange("p o n -> p (o n)").bitcast(F32),
                                            ALU.subtract).then_inc(sw_l[w], 1)

        def down_dve(dve, first_block, job0, gate, ada_of):
            jobs = list(down_jobs(first_block))
            inside = 0
            for n in range(HT):
                split_lo(dve, Block(first_block + n))
                ada_of(n)
                for ct, tiles in jobs:
                    if tiles[-1][0].at == first_block + n:
                        if tiles[-1][1] == KT - 1:
                            dve.wait_ge(block_done, first_block + n + 1)
                        else:
                            inside += 1
                            dve.wait_ge(down_done[first_block], inside)
                        nc.vector.scalar_tensor_tensor(out=res[:, ct, :], in0=by[(job0 + ct) % 2][:], scalar=gate(ct),
                                                       in1=res[:, ct, :], op0=ALU.mult, op1=ALU.add)\
                            .then_inc(y_free, 1)

        def square_dve(dve, first_block, job0, gate, ada_of=none):
            for j in range(KT):
                split_lo(dve, Block(first_block + j))
                ada_of(j)
                dve.wait_ge(block_done, first_block + j + 1)
                nc.vector.scalar_tensor_tensor(out=res[:, j, :], in0=by[(job0 + j) % 2][:], scalar=gate(j),
                                               in1=res[:, j, :], op0=ALU.mult, op1=ALU.add).then_inc(y_free, 1)

        def ybrest(dve, c):
            dve.wait_ge(yb_f, c + 1)
            dve.wait_ge(yb_h, c + 1)
            nc.vector.tensor_tensor(yb_lo[:, :, c * P:(c + 1) * P], yt[c % 2][:].rearrange("p (h n) -> p h n", h=HEADS),
                                    yb_hi[:, :, c * P:(c + 1) * P].bitcast(F32), ALU.subtract).then_inc(yb_l, 1)

        def ryrest(dve, e, i):
            dve.wait_ge(ry_f, before(e + 1, i, HEADS))
            dve.wait_ge(ry_h, before(e + 1, i, HEADS))
            nc.vector.tensor_tensor(ry_lo[:, e, :], rt[e % 2][:], ry_hi[:, e, :].bitcast(F32), ALU.subtract)\
                .then_inc(ry_l, 1)

        @block.vector
        def _(dve):
            nc.vector.memset(ones[:], 1.0).then_inc(consts, 1)
            nc.vector.memset(eps_col[:], EPS).then_inc(consts, 1)
            dve.wait_ge(cols_landed, 16)
            nc.vector.tensor_tensor(oml[:], col("lb0", 0, 4), col("lb1", 0, 4), ALU.subtract).then_inc(lb_ready, 1)
            for b in range(RAW):
                split_lo(dve, Block(b - AHEAD))
            dve.wait_ge(lb_ready, 2)
            nc.vector.tensor_scalar(oml[:], lb[:], -1.0, 1.0, ALU.mult, ALU.add).then_inc(lb_ready, 1)
            dve.wait_ge(ada0_mm, 1)
            nc.vector.tensor_tensor(ada0[:], bw[0][:, :32].rearrange("p (a v) -> p a v", v=2),
                                    col("ada_b", 0, 16).rearrange("p (a o) -> p a o", o=1).to_broadcast([P, 16, 2]),
                                    ALU.add).then_inc(ada0_ready, 1)
            dve.wait_ge(ada0_ready, 1)
            for v in range(2):
                nc.vector.scalar_tensor_tensor(out=mod_a[:, v, :], in0=ada0[:, 8:16, v], scalar=1.0,
                                               in1=col("norm1", 0, 8), op0=ALU.add, op1=ALU.mult).then_inc(mod_ready, 1)
            dve.wait_ge(mod_ready, 2)
            norm_dve(dve, n1x, res, L, lambda j: mod_a[:, 0, j:j + 1], lambda j: ada0[:, j, 0:1], hx_hi, hx_lo)
            norm_dve(dve, n1c, ctx_t, LC, lambda j: mod_a[:, 1, j:j + 1], lambda j: ada0[:, j, 1:2], hc_hi, hc_lo)
            for b in range(RAW, AHEAD):
                split_lo(dve, Block(b - AHEAD))
            for n in range(8):
                d, h = n // HEADS, n % HEADS
                split_lo(dve, Block(B_GATES + n))
                dve.wait_ge(f_ready, 2 * n + 2)
                nc.vector.tensor_scalar(hk[:, :, d, h, :], hf[:, :, 1 - d, h, :], -1.0, 1.0, ALU.mult, ALU.add)\
                    .then_inc(k_ready, 1)
                nc.vector.tensor_scalar(kc[:, d, h, :], fc[:, 1 - d, h, :], -1.0, 1.0, ALU.mult, ALU.add)\
                    .then_inc(k_ready, 1)
            for n in range(4):
                split_lo(dve, Block(B_VAL + n))
            dve.wait_ge(k_ready, 16)
            for l in range(LEVELS + 1):
                if l >= 1:
                    dve.wait_ge(kc_level, l)
                t_in = fc[:].rearrange("p d h n -> p (d h n)") if l == 0 else tc[(l - 1) % 2][:, :2 * HEADS * LC >> l]
                t_out = tc[l % 2][:, :2 * HEADS * LC >> (l + 1)] if l < LEVELS else None
                decay_keys(kc, t_in, l, t_out).then_inc(kc_level, 1)
            for n in range(12):
                split_lo(dve, Block(B_Q + n))
                if n < 8:
                    if n == 0:
                        dve.wait_ge(crow_silu, 1)
                    ada_reduce(dve, n, 0)
            dve.wait_ge(x_free, JX["q"] + 4)
            dve.wait_ge(masks_landed, 16)
            dve.wait_ge(kd_ready, 4)
            dve.wait_ge(s0_mm, 2)
            at = 0
            for c0 in (0, 2):
                for c in (c0, c0 + 1):
                    nc.vector.tensor_tensor(ksum[c % 2][:], hk[:, c, 0, :, :], hk[:, c, 1, :, :], ALU.add)\
                        .then_inc(level_ready, 1)
                for r in range(LEVELS + 1):
                    for c in (c0, c0 + 1):
                        at += 1
                        dve.wait_ge(level_mm, at)
                        src = bw[c % 2][:].rearrange("p (h n) -> p h n", h=HEADS)
                        if r == 0:
                            nc.vector.tensor_tensor(att[c][:], src,
                                                    ident[:].rearrange("p (o n) -> p o n", o=1).to_broadcast([P, HEADS, P]),
                                                    ALU.mult)
                            nc.vector.tensor_tensor(hq[:, c], hq[:, c], hf[:, c], ALU.mult).then_inc(level_ready, 1)
                            continue
                        l = r - 1
                        dve.wait_ge(level_ready, level_step(c0, r, c) + 1)
                        nc.vector.copy_predicated(att[c][:], masks[:, l:l + 1, :].to_broadcast([P, HEADS, P]), src)
                        t_in = (hf[:, c].rearrange("p d h n -> p (d h n)") if l == 0
                                else tx[c % 2][(l - 1) % 2][:, :2 * HEADS * P >> l])
                        t_out = tx[c % 2][l % 2][:, :2 * HEADS * P >> (l + 1)] if l < LEVELS - 1 else ttot[:, c, :]
                        decay_queries(c, t_in, l)
                        ins = decay_keys(hk[:, c], t_in, l, t_out)
                        ins.then_inc(chunk_ready if l == LEVELS - 1 else level_ready, 1)
            dve.wait_ge(s_ready, 2)
            dve.wait_ge(chunk_ready, LT)
            for n, (c, d) in enumerate(UPDATES):
                dve.wait_ge(upd_mm, n + 1)
                if n >= 2:
                    dve.wait_ge(upd_done, n - 1)
                old = (S_ENTER_F if d == 0 else S_ENTER_B)[c]
                new = S_ENTER_F[c + 1] if d == 0 else S_ENTER_B[c - 1]
                for h in range(HEADS):
                    ins = nc.vector.scalar_tensor_tensor(out=new[:, h, :], in0=old[:, h, :],
                                                         scalar=ttot[:, c, HEADS * (1 - d) + h:HEADS * (1 - d) + h + 1],
                                                         in1=by[n % 2][:, h * P:(h + 1) * P], op0=ALU.mult, op1=ALU.add)
                ins.then_inc(upd_done, 1)
            dve.wait_ge(o_mm, LT)
            for c in range(LT):
                dve.wait_ge(ostd, c + 1)
                nc.vector.reciprocal(rstd[:], std[:]).then_inc(orstd, 1)
                dve.wait_ge(orstd, c + 1)
                dve.wait_ge(gs_ready, HEADS)
                if c >= 2:
                    dve.wait_ge(yb_l, c - 1)
                y3 = yt[c % 2][:].rearrange("p (h n) -> p h n", h=HEADS)
                nc.vector.tensor_tensor(y3, ho[:, c, 0, :, :], rstd[:].rearrange("p (h n) -> p h n", h=HEADS),
                                        ALU.mult).then_inc(on_ready, 1)
                dve.wait_ge(on_ready, c + 1)
                nc.vector.tensor_tensor(y3, y3, gs[:, :, c * P:(c + 1) * P], ALU.mult).then_inc(yb_f, 1)
                if c >= 1:
                    ybrest(dve, c - 1)
            ybrest(dve, LT - 1)
            for g in range(HEADS):
                dve.wait_ge(ya_h, g + 1)
                nc.vector.tensor_tensor(ya_lo[:, g, :], bw[g % 2][:], ya_hi[:, g, :].bitcast(F32), ALU.subtract)\
                    .then_inc(ya_l, 1)
            with dve.Fori(0, 2) as i:
                for u in range(4):
                    for kind in range(3):
                        split_lo(dve, Block(B_MERGE + 3 * u + kind, i, 12))
                        ada_reduce(dve, 8 + 3 * u + kind, 0, i, 12)
                    dve.wait_ge(block_done, Block(B_MERGE + 3 * u + 2, i, 12).count(1))
                    dve.wait_ge(x_free, before(JX["merge"] + 2 * u + 2, i, 8))
                    nc.vector.tensor_tensor(gate_a[u % 2][:], gate_a[u % 2][:], by[0][:], ALU.mult).then_inc(y_free, 1)
                    nc.vector.tensor_tensor(gate_b[u % 2][:], gate_b[u % 2][:], by[1][:], ALU.mult).then_inc(y_free, 1)
                    dve.wait_ge(y_free, before(JY["merge"] + 2 * u + 2, i, 8))
                    nc.vector.tensor_tensor(mt[u % 2][:], gate_a[u % 2][:], gate_b[u % 2][:], ALU.add).then_inc(m_f, 1)
                    dve.wait_ge(m_f, before(u + 1, i, 4))
                    dve.wait_ge(m_h, before(u + 1, i, 4))
                    ms = bass.ds(i * 4 + u, 1)
                    nc.vector.tensor_tensor(m_lo[:, ms, :].rearrange("p o n -> p (o n)"), mt[u % 2][:],
                                            m_hi[:, ms, :].rearrange("p o n -> p (o n)").bitcast(F32),
                                            ALU.subtract).then_inc(m_l, 1)
            dve.wait_ge(ada_cols, 32)
            square_dve(dve, B_OUT, JY["out"], lambda j: ada[:, j:j + 1])

            def modulation(at, gain_at, count, v=0, src=None):
                s = ada if src is None else src
                nc.vector.scalar_tensor_tensor(out=mod_a[:, v, :], in0=s[:, at:at + 8], scalar=1.0,
                                               in1=cols[:, gain_at:gain_at + 8], op0=ALU.add,
                                               op1=ALU.mult).then_inc(mod_ready, 1)
                dve.wait_ge(mod_ready, count)

            modulation(16, COLS["norm2"], 3)
            dve.wait_ge(y_free, JY["out"] + 8)
            norm_dve(dve, n2, res, L, lambda j: mod_a[:, 0, j:j + 1], lambda j: ada[:, 8 + j:9 + j], hx_hi, hx_lo)
            dve.wait_ge(norm_lo, n2.tiles + KT)
            for s in range(2):
                for k in range(2):
                    nc.vector.memset(zpad[s][k][:], 0.0).then_inc(z_zero, 1)
            dve.wait_ge(z_zero, 4)
            taps = [t for t in range(9) if t != 4]
            with dve.Fori(0, HT // 2) as i:
                for s in range(2):
                    for k in range(2):
                        split_lo(dve, Block(B_UP + 2 * s + k, i, 4))
                    dve.wait_ge(x_free, before(JX["up"] + 2 * s + 2, i, 4))
                    for n, t in enumerate(taps):
                        for k in range(2):
                            if n >= 1:
                                dve.wait_ge(tap_done, before(16 * s + 2 * n + k - 1, i, 32))
                            cw = i * 40 + (COLS["conv"] + 20 * s + 10 * k + t)
                            nc.vector.scalar_tensor_tensor(
                                out=acc[s][k][:], in0=zpad[s][k][:, t // 3:t // 3 + ROWS, t % 3:t % 3 + GRID],
                                scalar=cols[:, bass.ds(cw, 1)], in1=acc[s][k][:], op0=ALU.mult,
                                op1=ALU.add).then_inc(tap_done, 1)
                for s in range(2):
                    dve.wait_ge(tap_done, before(16 * s + 16, i, 32))
                    dve.wait_ge(silu_done, before(s + 1, i, 2))
                    nc.vector.tensor_tensor(acc[s][1][:], acc[s][0][:], acc[s][1][:], ALU.mult).then_inc(hid_f, 1)
                for s in range(2):
                    dve.wait_ge(hid_f, before(s + 1, i, 2))
                    dve.wait_ge(hid_h, before(s + 1, i, 2))
                    hs = bass.ds(i * 2 + s, 1)
                    nc.vector.tensor_tensor(hid_lo[:, hs, :].rearrange("p o n -> p (o n)"),
                                            acc[s][1][:].rearrange("p r c -> p (r c)"),
                                            hid_hi[:, hs, :].rearrange("p o n -> p (o n)").bitcast(F32),
                                            ALU.subtract).then_inc(hid_l, 1)
            down_dve(dve, B_DOWN, JY["down"], lambda j: ada[:, 24 + j:25 + j],
                     lambda n: ada_reduce(dve, 32 + n, 1, row_c=2) if n < 16 else None)
            dve.wait_ge(y_free, JY["down"] + 8)
            rms_dve(dve, nf1, lambda j: col("final1", j))
            dve.wait_ge(norm_lo, nf1.tiles + KT)
            dve.wait_ge(ada_cols, 48)
            modulation(40, COLS["mix"], 4)
            modulation(8, COLS["mix"], 5, 1, ada_c)
            norm_dve(dve, nmx, res, L, lambda j: mod_a[:, 0, j:j + 1], lambda j: ada[:, 32 + j:33 + j], hx_hi, hx_lo)
            norm_dve(dve, nmc, ctx2_t, LC, lambda j: mod_a[:, 1, j:j + 1], lambda j: ada_c[:, j:j + 1], hc_hi, hc_lo)
            dve.wait_ge(rope_landed, 16)
            dve.wait_ge(norm_lo, nmc.tiles + KT)
            with dve.Fori(0, HEADS) as i:
                jx, jy = JX["ret"], JY["ret"]
                for n in range(4):
                    b = Block(B_RET + n, i, 16)
                    split_lo(dve, b)
                    ada_reduce(dve, 48 + n, 1, i, 8)
                    dve.wait_ge(block_done, b.count(1))
                    src, ht = by[n % 2], n % 2
                    dst = (rq if n < 2 else rk)[:, ht, :]
                    nc.vector.tensor_tensor(rt[0][:], src[:], rope[:, 2 * ht, :], ALU.mult)
                    for lo_, hi_ in ((0, 64), (64, 128)):
                        o_lo = 64 - lo_
                        ins = nc.vector.tensor_tensor(rt[1][o_lo:o_lo + 64, :], src[lo_:hi_, :],
                                                      rope[lo_:hi_, 2 * ht + 1, :], ALU.mult)
                    ins.then_inc(y_free, 1)
                    dve.wait_ge(y_free, before(jy + n + 1, i, 16))
                    nc.vector.tensor_tensor(dst, rt[0][:], rt[1][:], ALU.add).then_inc(rot_done, 1)
                    dve.wait_ge(rot_done, before(n + 1, i, 4))
                for n in range(4):
                    split_lo(dve, Block(B_RET + 4 + n, i, 16))
                    ada_reduce(dve, 52 + n, 1, i, 8)
                dve.wait_ge(dec_landed, before(16, i, 16))
                for d in range(2):
                    for dt in range(2):
                        w = DEC_W + L * d
                        nc.vector.tensor_tensor(rqd[:, d, dt, :], rq[:, dt, :], dec[:, w:w + L], ALU.mult)\
                            .then_inc(qd_done, 1)
                for n in range(4):
                    split_lo(dve, Block(B_RET + 8 + n, i, 16))
                dve.wait_ge(st_done, before(4, i, 4))
                for s in range(LT):
                    dve.wait_ge(sc_mm, before(s + 1, i, LT))
                    w = (LT - 1 - s) * P
                    nc.vector.tensor_tensor(rsc[:, s, :], by[s % 2][:], dec[:, w:w + L], ALU.mult).then_inc(y_free, 1)
                dve.wait_ge(rstd_s, before(1, i, 1))
                nc.vector.reciprocal(rstd[:], std[:]).then_inc(rstd_r, 1)
                dve.wait_ge(rstd_r, before(1, i, 1))
                dve.wait_ge(ro_done, before(HEADS, i, HEADS))
                dve.wait_ge(x_free, before(jx + 6, i, 10))
                for e in range(HEADS):
                    if e >= 2:
                        dve.wait_ge(ry_l, before(e - 1, i, HEADS))
                    nc.vector.tensor_tensor(rt[e % 2][:], ro[:, e, :], rstd[:], ALU.mult).then_inc(ry_t, 1)
                    dve.wait_ge(ry_t, before(e + 1, i, HEADS))
                    nc.vector.tensor_tensor(rt[e % 2][:], rt[e % 2][:], rg[:, e, :], ALU.mult).then_inc(ry_f, 1)
                    if e >= 1:
                        ryrest(dve, e - 1, i)
                ryrest(dve, HEADS - 1, i)
                dve.wait_ge(ada_cols, before(56, i, 8))
                for n in range(4):
                    b = Block(B_RET + 12 + n, i, 16)
                    split_lo(dve, b)
                    dve.wait_ge(block_done, b.count(1))
                    for u in range(2):
                        j = 2 * n + u
                        nc.vector.scalar_tensor_tensor(out=res[:, j, :], in0=by[u][:], scalar=ada[:, 48 + j:49 + j],
                                                       in1=res[:, j, :], op0=ALU.mult, op1=ALU.add)\
                            .then_inc(y_free, 1)
                dve.wait_ge(y_free, before(jy + 16, i, 16))
            modulation(64, COLS["ffn"], 6)
            norm_dve(dve, nffn0, res, L, lambda j: mod_a[:, 0, j:j + 1], lambda j: ada[:, 56 + j:57 + j], hx_hi, hx_lo)
            dve.wait_ge(norm_lo, nffn0.tiles + KT)
            swiglu_dve(dve, 0, B_SW0, JY["sw0"], 80)
            down_dve(dve, B_SD0, JY["sd0"], lambda j: ada[:, 72 + j:73 + j],
                     lambda n: ada_reduce(dve, 124 + n, 1) if n < 4 else None)
            dve.wait_ge(ada_cols, 128)
            modulation(88, COLS["mix"] + 8, 7)
            dve.wait_ge(y_free, JY["sd0"] + 8)
            norm_dve(dve, nmix1, res, L, lambda j: mod_a[:, 0, j:j + 1], lambda j: ada[:, 80 + j:81 + j], hx_hi, hx_lo)
            dve.wait_ge(block_done, B_CIN)
            for s in range(2):
                nc.vector.memset(cpad[s][:], 0.0).then_inc(cpad_zero, 1)
            dve.wait_ge(cpad_zero, 2)
            with dve.Fori(0, 2) as i:
                for u in range(4):
                    for kind in range(3):
                        split_lo(dve, Block(B_CIN + 3 * u + kind, i, 12))
                    s = u % 2
                    dve.wait_ge(block_done, Block(B_CIN + 3 * u + 2, i, 12).count(1))
                    dve.wait_ge(x_free, before(JX["cin"] + 2 * u + 2, i, 8))
                    nc.vector.tensor_tensor(cpad[s][:, 1:L + 1], cc[s][:], by[u % 2][:], ALU.mult).then_inc(y_free, 1)
                    dve.wait_ge(y_free, before(JY["cin"] + u + 1, i, 4))
                    for t in range(3):
                        wcol = cols[:, bass.ds(i * 12 + (COLS["sconv"] + 3 * u + t), 1)]
                        if t == 0:
                            nc.vector.tensor_scalar(cacc[s][:], cpad[s][:, 0:L], wcol, None, ALU.mult)\
                                .then_inc(cacc_step, 1)
                        else:
                            dve.wait_ge(cacc_step, before(3 * u + t, i, 12))
                            nc.vector.scalar_tensor_tensor(out=cacc[s][:], in0=cpad[s][:, t:t + L], scalar=wcol,
                                                           in1=cacc[s][:], op0=ALU.mult, op1=ALU.add)\
                                .then_inc(cacc_step, 1)
                    dve.wait_ge(cacc_step, before(3 * u + 3, i, 12))
                    nc.vector.tensor_tensor(cacc[s][:], cacc[s][:], cb[s][:], ALU.mult).then_inc(cy_f, 1)
                    dve.wait_ge(cy_f, before(u + 1, i, 4))
                    dve.wait_ge(cy_h, before(u + 1, i, 4))
                    ms = bass.ds(i * 4 + u, 1)
                    nc.vector.tensor_tensor(cy_lo[:, ms, :].rearrange("p o n -> p (o n)"), cacc[s][:],
                                            cy_hi[:, ms, :].rearrange("p o n -> p (o n)").bitcast(F32),
                                            ALU.subtract).then_inc(cy_l, 1)
            square_dve(dve, B_COUT, JY["cout"], lambda j: ada[:, 96 + j:97 + j])
            modulation(112, COLS["ffn"] + 8, 8)
            dve.wait_ge(y_free, JY["cout"] + 8)
            norm_dve(dve, nffn1, res, L, lambda j: mod_a[:, 0, j:j + 1], lambda j: ada[:, 104 + j:105 + j], hx_hi, hx_lo)
            dve.wait_ge(norm_lo, nffn1.tiles + KT)
            swiglu_dve(dve, 1, B_SW1, JY["sw1"], None)
            down_dve(dve, B_SD1, JY["sd1"], lambda j: ada[:, 120 + j:121 + j], none)
            dve.wait_ge(y_free, JY["sd1"] + 8)
            rms_dve(dve, nf2, lambda j: col("final2", j))


def stream_blocks(inputs):
    def tiles(w, cols=P):
        r, n = w.shape
        return w.reshape(r // P, P, n // cols, cols).transpose(2, 1, 0, 3)

    def tall(w):
        r, n = w.shape
        t = w.reshape(r // P, P, n // P, P).transpose(2, 0, 1, 3).reshape(-1, KT, P, P)
        return t.transpose(0, 2, 1, 3)

    def rows(w):
        return w.reshape(4, 2, P, L).transpose(0, 2, 1, 3)

    def pairs(a, b):
        return np.stack([a, b], 1).reshape((-1,) + a.shape[1:])

    w_in = inputs["w_in"][0]
    fnet, q, f_f, f_b, val, g = (w_in[:, n * L:(n + 1) * L] for n in range(6))
    gate_a, gate_b = w_in[:, 6 * L:6 * L + D], w_in[:, 6 * L + D:]
    wab = np.concatenate([tiles(inputs["w_a"][0]), tiles(inputs["w_b"][0])], 2)
    merge = np.stack([tiles(gate_a), tiles(gate_b), wab], 1).reshape(-1, P, KT, P)
    up = inputs["ffn_up"][0]
    parts = [tiles(f_f), tiles(f_b), rows(val), tiles(q), tiles(fnet), tiles(g), merge, tiles(inputs["w_out"][0]),
             pairs(tiles(up[:, :FF]), tiles(up[:, FF:])), tall(inputs["ffn_down"][0])]
    ret, w_o = inputs["ret_w_qkvg_2"][0], inputs["ret_w_o_2"][0]
    for h in range(HEADS):
        o = tiles(w_o[h * L:(h + 1) * L]).reshape(4, 2, P, HEADS, P).transpose(0, 2, 1, 3, 4)
        parts += [tiles(ret[:, h * 256:(h + 1) * 256]), tiles(ret[:, D + h * 256:D + (h + 1) * 256]),
                  rows(ret[:, 2 * D + h * L:2 * D + (h + 1) * L]),
                  tiles(ret[:, 4 * D + h * L:4 * D + (h + 1) * L]), o]
    c_in = inputs["conv_w_in_2"][0]
    cin = np.stack([tiles(c_in[:, n * D:(n + 1) * D]) for n in range(3)], 1).reshape(-1, P, KT, P)
    for layer in range(2):
        parts += [pairs(tiles(inputs["ffn_w1_2"][layer]), tiles(inputs["ffn_w3_2"][layer])),
                  tall(inputs["ffn_w2_2"][layer])]
        if layer == 0:
            parts += [cin, tiles(inputs["conv_w_out_2"][0])]
    return np.concatenate([p.reshape(-1, P, BLK) for p in parts])


def small_columns(inputs):
    def col(v):
        return v.reshape(-1, P).T

    conv = inputs["ffn_conv_w"][0].reshape(9, 2, HT, P)
    conv = np.concatenate([conv, inputs["ffn_conv_b"][0].reshape(1, 2, HT, P)])
    conv = conv.transpose(3, 2, 1, 0).reshape(P, HT * 20)
    sconv = inputs["conv_w_2"][0].reshape(3, KT, P).transpose(2, 1, 0).reshape(P, 24)
    parts = [col(inputs["c"][0]), col(inputs["c_ctx"]), col(inputs["norm1_g"][0]), col(inputs["norm2_g"][0]),
             col(inputs["final_g"]), col(inputs["hg_lb"][0]), col(inputs["hg_lb"][1]), col(inputs["hg_onorm_g"][0]),
             conv, col(inputs["ada_b"][0]), col(inputs["ada_b_2"][0]), col(inputs["ada_b_2"][1]),
             col(inputs["norm_mix_2"].reshape(-1)), col(inputs["norm_ffn_2"].reshape(-1)),
             col(inputs["final_norm_2"]), sconv]
    return np.concatenate(parts, 1)


def constants():
    f64 = np.float64
    n = np.arange(P)
    top = n[:, None] ^ n[None, :]
    masks = np.stack([(top >> l) == 1 for l in range(LEVELS)], 1).astype(np.int32)
    a1 = 2 * np.pi * ((n[:, None] * n[None, :]) % P) / P
    dft1 = np.concatenate([np.cos(a1), np.sin(a1)], 1) / np.sqrt(f64(P * L))
    t = np.arange(L)
    a2 = 2 * np.pi * ((t[:, None] * t[None, :]) % L) / L
    dft2 = np.stack([np.cos(a2), -np.sin(a2)]).reshape(2, LT, P, L).transpose(2, 0, 1, 3)
    half = 64
    freqs = (np.float32(10000.0) ** (-np.arange(half, dtype=np.float32) / np.float32(half))).astype(np.float32)
    rope = []
    for pos in (t // GRID, t % GRID):
        ang = (freqs[:, None] * pos[None, :].astype(np.float32)).astype(f64)
        rope += [np.concatenate([np.cos(ang)] * 2), np.concatenate([np.sin(ang), -np.sin(ang)])]
    rope = np.stack(rope, 1)
    dec = np.zeros((HEADS, P, DEC_N))
    scale = 256.0 ** -0.5
    for h in range(HEADS):
        gf, gb = 1 - 2.0 ** (-5.0 - h), 1 - 2.0 ** (-5.5 - h)
        d = np.arange(DEC_W)[None, :] - (LT - 1) * P - n[:, None]
        dec[h, :, :DEC_W] = scale * (np.where(d >= 0, gf ** np.maximum(d, 0), 0) + np.where(d <= 0, gb ** np.maximum(-d, 0), 0))
        dec[h, :, DEC_W:DEC_W + L] = gf ** (t + 1.0)
        dec[h, :, DEC_W + L:DEC_W + 2 * L] = gb ** (f64(L) - t)
        for ct in range(LCT):
            j = ct * P + n
            dec[h, :, DEC_W + 2 * L + ct] = scale * gf ** (LC - 1.0 - j)
            dec[h, :, DEC_W + 2 * L + LCT + ct] = scale * gb ** j.astype(f64)
    f32 = lambda a: np.ascontiguousarray(a, dtype=np.float32)
    return {"ident": f32(np.eye(P)), "masks": masks, "dft1": f32(dft1), "dft2": f32(dft2), "rope": f32(rope), "dec": f32(dec)}


def kernel(**inputs):
    import concourse.bacc as bacc
    from concourse.bass_utils import run_bass_kernel_spmd

    inputs = {k: np.asarray(v) for k, v in inputs.items()}
    ada_w = [inputs["ada_w"][0], inputs["ada_w_2"][0], inputs["ada_w_2"][1]]
    arrays = {
        "wstream": stream_blocks(inputs),
        "ada_kn": ada_w[0][:, :2 * D].reshape(KT, P, 16, P).transpose(2, 1, 0, 3).reshape(16, P, D),
        "ada_nk": np.concatenate([ada_w[0].T[2 * D:], ada_w[1].T, ada_w[2].T]).reshape(128, P, D),
        "x": inputs["x"][0].reshape(LT, P, D).transpose(1, 0, 2),
        "ctx1": inputs["ctx"][0].reshape(LCT, P, D).transpose(1, 0, 2),
        "ctx2": inputs["ctx_2"][0].reshape(LCT, P, D).transpose(1, 0, 2),
        "cols": small_columns(inputs),
        "crow": np.stack([inputs["c"][0], inputs["c_2"][0], inputs["c_ctx_2"]]),
        **constants(),
    }
    arrays = {k: np.ascontiguousarray(v) for k, v in arrays.items()}
    nc = bacc.Bacc("TRN2", target_bir_lowering=False, num_devices=1, dynamic_dma_scratch_size=1024)
    aps = {k: nc.dram_tensor("in_" + k, v.shape, mybir.dt.from_np(v.dtype), kind="ExternalInput").ap()
           for k, v in arrays.items()}
    out = nc.dram_tensor("out_x", (L, D), F32, kind="ExternalOutput").ap()
    program(nc, aps["wstream"], aps["ada_kn"], aps["ada_nk"], aps["x"], aps["ctx1"], aps["ctx2"], aps["cols"],
            aps["crow"], aps["ident"], aps["masks"], aps["dft1"], aps["dft2"], aps["rope"], aps["dec"], out)
    r = run_bass_kernel_spmd(nc, [{"in_" + k: v for k, v in arrays.items()}], core_ids=[0])
    return r.results[0]["out_x"].reshape(1, L, D)
```

```python
from contextlib import ExitStack

import numpy as np
import concourse.bass as bass
from concourse import mybir

F32 = mybir.dt.float32
F32R = mybir.dt.float32r
I32 = mybir.dt.int32
ALU = mybir.AluOpType
ACT = mybir.ActivationFunctionType

P = 128
D = 1024
KT = D // P
L, LC = 512, 256
LT, LCT = L // P, LC // P
GRID = 64
ROWS = L // GRID
FF = 2816
HT = FF // P
HEADS = 4
LEVELS = 7
STEPS = LT * (LEVELS + 1) // 8
EPS = 1e-6
BLK = KT * P

RING = 4
RAW = 2
AHEAD = RING - 1

B_GATES = 0
B_VAL = B_GATES + 8
B_Q = B_VAL + 4
B_FNET = B_Q + 4
B_G = B_FNET + 4
B_MERGE = B_G + 4
B_OUT = B_MERGE + 24
B_UP = B_OUT + 8
B_DOWN = B_UP + 2 * HT
B_RET = B_DOWN + HT
B_SW0 = B_RET + 16 * HEADS
B_SD0 = B_SW0 + 2 * HT
B_CIN = B_SD0 + HT
B_COUT = B_CIN + 24
B_SW1 = B_COUT + 8
B_SD1 = B_SW1 + 2 * HT
N_BLOCKS = B_SD1 + HT

COLS = {}
_at = 0
for _name, _n in [("c", 8), ("c_ctx", 8), ("norm1", 8), ("norm2", 8), ("final1", 8), ("lb0", 4),
                  ("lb1", 4), ("onorm", 4), ("conv", HT * 20), ("ada_b", 144), ("mix", 16),
                  ("ffn", 16), ("final2", 8), ("sconv", 24)]:
    COLS[_name] = _at
    _at += _n
N_COLS = _at

KEYS = LT + LCT
DEC_W = L + (LT - 1) * P
DEC_N = DEC_W + LCT * L
ROW_C2, ROW_C, ROW_CTX2 = range(3)


TAPS = [(k, t) for t in range(9) if t != 4 for k in range(2)]


class Block:

    def __init__(self, at, i=None, per=0):
        self.at, self.i, self.per = at, i, per

    def plus(self, n):
        return Block(self.at + n, self.i, self.per)

    def count(self, n=0):
        return self.at + n if self.i is None else self.i * self.per + (self.at + n)

    def loads(self):
        first = 16 * (self.at // RAW + 1)
        return first if self.i is None else self.i * (16 * self.per // RAW) + first


def program(nc, wstream, ada_kn, ada_nk, x_in, ctx1_in, ctx2_in, cols_in, crow_in, ident_in, masks_in,
            dft1_in, dft2_in, rope_in, dec_in, out):
    with ExitStack() as ctx:
        def sem(name):
            return ctx.enter_context(nc.semaphore(name))

        base = (nc.sbuf_base + 63) // 64 * 64
        cursor = [base]

        def region(nbytes):
            at = cursor[0]
            cursor[0] += (nbytes + 31) // 32 * 32
            assert cursor[0] <= nc.sbuf_usable_end, cursor[0] - nc.sbuf_usable_end
            return at

        def sb(name, shape, dt=F32, at=None):
            nbytes = 4 * int(np.prod(shape[1:]))
            return nc.alloc_sbuf_tensor_at(name, shape, dt, offset=region(nbytes) if at is None else at)

        w_raw = [sb(f"w_raw{s}", [P, BLK]) for s in range(RAW)]
        w_hi = [sb(f"w_hi{s}", [P, BLK], F32R) for s in range(RING)]
        w_lo = [sb(f"w_lo{s}", [P, BLK], F32R) for s in range(RING)]
        res = sb("res", [P, KT, L])
        KB = 1024
        r_hx = region(32 * KB)
        hx_hi = sb("hx_hi", [P, KT, L], F32R, r_hx)
        hx_lo = sb("hx_lo", [P, KT, L], F32R, r_hx + 16 * KB)
        x_tok = sb("x_tok", [P, LT, D], F32, r_hx)
        ctx_tok = sb("ctx_tok", [P, LCT, D], F32, r_hx + 16 * KB)
        ada_raw = [sb(f"ada_raw{s}", [P, D]) for s in range(2)]
        r_crow = region(12 * KB)
        crow = sb("crow", [P, 3, D], F32, r_crow)
        dec = sb("dec", [P, DEC_N], F32, r_crow + 4 * KB)
        cols = sb("cols", [P, N_COLS])
        ident = sb("ident", [P, P])
        ones = sb("ones", [P, P])
        eps_col = sb("eps_col", [P, 1])
        eps2_col = sb("eps2_col", [P, 1])
        fcol = sb("fcol", [P, KT])
        table_col = sb("table_col", [P, 1])
        scol = sb("scol", [P, 2, KT])
        ada_sum = sb("ada_sum", [P, 8])
        ada0 = sb("ada0", [P, 16, 2])
        ada = sb("ada", [P, 128])
        ada_c = sb("ada_c", [P, 16])
        mod_a = sb("mod_a", [P, 2, KT])
        lb = sb("lb", [P, HEADS])
        oml = sb("oml", [P, HEADS])
        dft1 = sb("dft1", [P, 2 * P])
        rope = sb("rope", [P, 2 * (ROWS + GRID)])
        r_scr = region(12 * KB)
        r_hc = region(16 * KB)
        r_arena = region(80 * KB)
        hc_hi = sb("hc_hi", [P, KT, LC], F32R, r_hc)
        hc_lo = sb("hc_lo", [P, KT, LC], F32R, r_hc + 8 * KB)
        sq = [sb(f"sq{s}", [P, L], F32, r_scr + 2 * KB * s) for s in range(2)]
        std = sb("std", [P, L], F32, r_scr + 4 * KB)
        rstd = sb("rstd", [P, L], F32, r_scr + 6 * KB)
        tnorm = [sb(f"tnorm{s}", [P, L], F32, r_scr + (8 + 2 * s) * KB) for s in range(2)]
        c_sq, c_std, c_rstd = [], [], []
        for n, at in ((1, r_arena + 72 * KB), (2, r_hx + 16 * KB)):
            c_sq.append([sb(f"c{n}_sq{s}", [P, LC], F32, at + KB * s) for s in range(2)])
            c_std.append(sb(f"c{n}_std", [P, LC], F32, at + 2 * KB))
            c_rstd.append(sb(f"c{n}_rstd", [P, LC], F32, at + 3 * KB if n == 1 else r_crow + 4 * KB))
        f_sq = [sb(f"f_sq{s}", [P, L], F32, r_hx + (20 + 2 * s) * KB) for s in range(2)]
        f_std = sb("f_std", [P, L], F32, r_hx + 24 * KB)
        f_root = sb("f_root", [P, L], F32, r_arena + 76 * KB)
        f_rstd = sb("f_rstd", [P, L], F32, r_arena + 78 * KB)
        ada_w0 = sb("ada_w0", [P, KT, 2 * D], F32, r_arena)
        ada_rows = sb("ada_rows", [2, 2 * D], F32, r_hc)
        ctx_t = sb("ctx_t", [P, KT, LC], F32, r_arena + 64 * KB)
        r_q, r_k, r_f, r_x, r_v = (r_arena + 16 * KB * n for n in range(5))
        hq = sb("hq", [P, LT, 2, HEADS, P], F32, r_q)
        hk = sb("hk", [P, LT, 2, HEADS, P], F32, r_k)
        hf = sb("hf", [P, LT, 2, HEADS, P], F32, r_f)
        kc = sb("kc", [P, 2, HEADS, LC], F32, r_x)
        fc = sb("fc", [P, 2, HEADS, LC], F32, r_x + 8 * KB)
        v_x = sb("v_x", [P, LT, L], F32, r_v)
        v_c = sb("v_c", [P, LCT, L], F32, r_v + 8 * KB)
        masks = sb("masks", [P, LEVELS, P], I32, r_v + 12 * KB)
        sig = [sb(f"sig{s}", [P, L + LC], F32, r_scr + 3 * KB * s) for s in range(2)]
        tc = [sb("tc0", [P, 2 * HEADS * LC // 2], F32, r_scr + 6 * KB),
              sb("tc1", [P, 2 * HEADS * LC // 4], F32, r_scr + 10 * KB)]
        kd_c = sb("kd_c", [P, 2, HEADS, LCT, P], F32, r_scr)
        s_init = sb("s_init", [P, 2, HEADS, P], F32, r_scr + 8 * KB)
        ksum = [sb(f"ksum{s}", [P, HEADS, P], F32, r_scr + 2 * KB * s) for s in range(2)]
        kd_x = [sb(f"kd_x{s}", [P, HEADS, P], F32, r_scr + (4 + 2 * s) * KB) for s in range(2)]
        level_k = [sb(f"level_k{s}", [P, HEADS * P], F32, r_scr + (4 + 2 * s) * KB) for s in range(2)]
        tx = [[sb(f"tx{s}_0", [P, 512], F32, r_x + 3 * KB * s),
               sb(f"tx{s}_1", [P, 256], F32, r_x + 3 * KB * s + 2 * KB)] for s in range(2)]
        att = [sb(f"att{c}", [P, HEADS, P], F32, r_x + (6 + 2 * c) * KB) for c in range(LT)]
        ttot = sb("ttot", [P, LT, 2 * HEADS])
        ho = sb("ho", [P, LT, 2, HEADS, P], F32, r_f)
        yb_hi = sb("yb_hi", [P, HEADS, L], F32R, r_q)
        yb_lo = sb("yb_lo", [P, HEADS, L], F32R, r_q + 8 * KB)
        ut = sb("ut", [P, HEADS, L], F32, r_hc)
        gs = sb("gs", [P, HEADS, L], F32, r_hc + 8 * KB)
        pq = sb("pq", [P, LT, HEADS, 2 * P], F32, r_k)
        dft2 = sb("dft2", [P, 2, LT, L], F32, r_v)
        ya_hi = sb("ya_hi", [P, HEADS, L], F32R, r_x)
        ya_lo = sb("ya_lo", [P, HEADS, L], F32R, r_x + 8 * KB)
        yt = [sb(f"yt{s}", [P, L], F32, r_scr + (8 + 2 * s) * KB) for s in range(2)]
        gate_a = [sb(f"gate_a{s}", [P, L], F32, r_scr + 2 * KB * s) for s in range(2)]
        gate_b = [sb(f"gate_b{s}", [P, L], F32, r_scr + (4 + 2 * s) * KB) for s in range(2)]
        mt = [sb(f"mt{s}", [P, L], F32, r_scr + (8 + 2 * s) * KB) for s in range(2)]
        m_hi = sb("m_hi", [P, KT, L], F32R, r_k)
        m_lo = sb("m_lo", [P, KT, L], F32R, r_f)
        hid_hi = sb("hid_hi", [P, HT, L], F32R, r_hc)
        hid_lo = sb("hid_lo", [P, HT, L], F32R, r_hc + 44 * KB)
        sgate = [sb(f"sgate{s}", [P, L], F32, r_hc + (88 + 2 * s) * KB) for s in range(2)]
        hidden = [sb(f"hidden{s}", [P, L], F32, r_hc + (92 + 2 * s) * KB) for s in range(2)]
        zpad = [[sb(f"zpad{s}{k}", [P, ROWS + 2, GRID + 2], F32, r_scr + 2656 * (2 * s + k)) for k in range(2)]
                for s in range(2)]
        sw = [sb(f"sw{s}", [P, L], F32, r_scr + 2 * KB * s) for s in range(2)]
        r_a = r_arena
        rq_hi = sb("rq_hi", [P, 2, L], F32R, r_a)
        rq_lo = sb("rq_lo", [P, 2, L], F32R, r_a + 4 * KB)
        ro = sb("ro", [P, HEADS, L], F32, r_a)
        rk_hi = sb("rk_hi", [P, 2, L + LC], F32R, r_a + 8 * KB)
        rk_lo = sb("rk_lo", [P, 2, L + LC], F32R, r_a + 14 * KB)
        rv_hi = sb("rv_hi", [P, KEYS, L], F32R, r_a + 20 * KB)
        rv_lo = sb("rv_lo", [P, KEYS, L], F32R, r_a + 32 * KB)
        rsc_hi = sb("rsc_hi", [P, KEYS, L], F32R, r_a + 44 * KB)
        rsc_lo = sb("rsc_lo", [P, KEYS, L], F32R, r_a + 56 * KB)
        ry_hi = sb("ry_hi", [P, HEADS, L], F32R, r_a + 44 * KB)
        ry_lo = sb("ry_lo", [P, HEADS, L], F32R, r_a + 52 * KB)
        rg = sb("rg", [P, HEADS, L], F32, r_a + 68 * KB)
        rt = [sb(f"rt{s}", [P, L], F32, r_scr + (8 + 2 * s) * KB) for s in range(2)]
        rsq = [sb(f"rsq{s}", [P, L], F32, r_scr + 2 * KB * s) for s in range(2)]
        rot = rsq
        ctx2_tok = sb("ctx2_tok", [P, LCT, D], F32, r_hx)
        ctx2_t = sb("ctx2_t", [P, KT, LC], F32, r_arena + 72 * KB)
        cy_hi = sb("cy_hi", [P, KT, L], F32R, r_a)
        cy_lo = sb("cy_lo", [P, KT, L], F32R, r_a + 16 * KB)
        cb = [sb(f"cb{s}", [P, L], F32, r_a + (32 + 2 * s) * KB) for s in range(2)]
        cc = [sb(f"cc{s}", [P, L], F32, r_a + (36 + 2 * s) * KB) for s in range(2)]
        cacc = [sb(f"cacc{s}", [P, L], F32, r_a + (40 + 2 * s) * KB) for s in range(2)]
        cpad = [sb(f"cpad{s}", [P, L + 2], F32, r_a + 44 * KB + 2112 * s) for s in range(2)]
        out_tok = sb("out_tok", [P, LT, D], F32, r_a)

        bank = [ctx.enter_context(nc.psum_tensor(f"bank{n}", [P, L], F32)) for n in range(8)]
        bx, by = bank[0:2], bank[2:4]
        bn = bank[5]
        bw = bank[6:8]
        rbanks = [by[0], by[1], bx[0], bx[1], bw[0], bw[1]]
        acc = [[bw[0], bank[4]], [bw[1], bn]]

        raw_ready = [sem(f"raw_ready{s}") for s in range(RAW)]
        hi_ready, lo_ready, block_done = sem("hi_ready"), sem("lo_ready"), sem("block_done")
        x_free, y_free = sem("x_free"), sem("y_free")
        ada_in = [sem(f"ada_in{s}") for s in range(2)]
        ada_done = sem("ada_done")
        ada_cols = sem("ada_cols")
        x_landed, ctx_landed = sem("x_landed"), sem("ctx_landed")
        cols_landed, crow_landed, ident_landed = sem("cols_landed"), sem("crow_landed"), sem("ident_landed")
        dft1_landed, dft2_landed, masks_landed = sem("dft1_landed"), sem("dft2_landed"), sem("masks_landed")
        ada0_in = [sem(f"ada0_in{k}") for k in range(KT)]
        fcol_ready = sem("fcol_ready")
        consts, crow_silu, scol_ready = sem("consts"), sem("crow_silu"), sem("scol_ready")
        turned, ada0_mm, ada0_rows, ada0_turned, ada0_ready = (
            sem("turned"), sem("ada0_mm"), sem("ada0_rows"), sem("ada0_turned"), sem("ada0_ready"))
        mod_ready = sem("mod_ready")
        lb_ready = sem("lb_ready")
        f_ready, k_ready, v_ready = sem("f_ready"), sem("k_ready"), sem("v_ready")
        kc_level, kc_turned, kd_ready, s0_mm, s_ready = (
            sem("kc_level"), sem("kc_turned"), sem("kd_ready"), sem("s0_mm"), sem("s_ready"))
        gs_ready = sem("gs_ready")
        level_ready, level_mm, chunk_ready = sem("level_ready"), sem("level_mm"), sem("chunk_ready")
        k_gathered = sem("k_gathered")
        k_turned, kd_copied, upd_mm, upd_done = sem("k_turned"), sem("kd_copied"), sem("upd_mm"), sem("upd_done")
        o_mm, o_ready, osq_ready, osum_mm, ostd, orstd, on_ready, yb_f, yb_h, yb_l = (
            sem("o_mm"), sem("o_ready"), sem("osq_ready"), sem("osum_mm"), sem("ostd"), sem("orstd"),
            sem("on_ready"), sem("yb_f"), sem("yb_h"), sem("yb_l"))
        pq_mm, pq_ready, ya_mm, ya_f, ya_h, ya_l = (
            sem("pq_mm"), sem("pq_ready"), sem("ya_mm"), sem("ya_f"), sem("ya_h"), sem("ya_l"))
        m_f, m_h, m_l = sem("m_f"), sem("m_h"), sem("m_l")
        tap_done, silu_done, hid_f, hid_h = sem("tap_done"), sem("silu_done"), sem("hid_f"), sem("hid_h")
        hid_l = sem("hid_l")
        ctx2_landed, turned2, rope_landed, dec_landed = (
            sem("ctx2_landed"), sem("turned2"), sem("rope_landed"), sem("dec_landed"))
        rot_p, ro_sum = sem("rot_p"), sem("ro_sum")
        rot_f, rot_h, rot_l, kc_h = sem("rot_f"), sem("rot_h"), sem("rot_l"), sem("kc_h")
        rv_h, rv_l, sc_mm, sc_h, sc_l = sem("rv_h"), sem("rv_l"), sem("sc_mm"), sem("sc_h"), sem("sc_l")
        wo_half = sem("wo_half")
        ro_mm, ro_done, rsum_mm, rstd_s, rstd_r = (
            sem("ro_mm"), sem("ro_done"), sem("rsum_mm"), sem("rstd_s"), sem("rstd_r"))
        ry_t, ry_f, ry_h, ry_l = sem("ry_t"), sem("ry_f"), sem("ry_h"), sem("ry_l")
        sw_h = [sem("sw_h0"), sem("sw_h1")]
        sw_l = [sem("sw_l0"), sem("sw_l1")]
        cpad_zero, cacc_step, cy_f, cy_h, cy_l = (
            sem("cpad_zero"), sem("cacc_step"), sem("cy_f"), sem("cy_h"), sem("cy_l"))
        turned_out, out_copied, out_stored = sem("turned_out"), sem("out_copied"), sem("out_stored")

        class Norm:

            def __init__(self, sems, scratch, n=0, split=0):
                (self.sq_ready, self.summed, self.mm, self.root, self.rec, self.scaled, self.hi, self.lo) = sems
                self.once, self.tiles, self.split_tiles, self.sums = n, KT * n, KT * split, (KT - 2) * n
                self.sq, self.std, self.rooted, self.rstd = scratch

        def norm_sems(name):
            return [sem(f"{name}_{n}") for n in ("sq", "summed", "mm", "root", "rec", "scaled", "hi", "lo")]

        shared = norm_sems("norm")
        n1x, n2, nmx, nffn0, nmix1, nffn1, nf2 = (Norm(shared, (sq, std, std, rstd), n, n) for n in range(7))
        n1c, nmc = (Norm(norm_sems(f"norm_c{n + 1}"), (c_sq[n], c_std[n], c_std[n], c_rstd[n])) for n in range(2))
        nf1 = Norm(norm_sems("norm_f"), (f_sq, f_std, f_root, f_rstd))

        def split_hi(act, b):
            nb = b.plus(AHEAD)
            if nb.at >= N_BLOCKS:
                return
            act.wait_ge(raw_ready[nb.at % RAW], nb.loads())
            if nb.at >= RING:
                act.wait_ge(block_done, nb.count(1 - RING))
            nc.scalar.activation(w_hi[nb.at % RING][:], w_raw[nb.at % RAW][:], ACT.Copy).then_inc(hi_ready, 1)

        def split_lo(dve, b):
            nb = b.plus(AHEAD)
            if nb.at >= N_BLOCKS:
                return
            dve.wait_ge(hi_ready, nb.count(1))
            nc.vector.tensor_tensor(w_lo[nb.at % RING][:], w_raw[nb.at % RAW][:],
                                    w_hi[nb.at % RING][:].bitcast(F32), ALU.subtract).then_inc(lo_ready, 1)

        def ada_load(act, a, i=None, per=0):
            n = a if i is None else i * per + a
            if a >= 2:
                act.wait_ge(ada_done, n - 1)
            src = ada_nk[a] if i is None else ada_nk[bass.ds(n, 1)].rearrange("o p n -> (o p) n")
            act.dma_start(ada_raw[a % 2][:], src).then_inc(ada_in[a % 2], 16)

        def ada_reduce(dve, a, row, i=None, per=0, row_c=None):
            landed = 16 * (a // 2 + 1)
            dve.wait_ge(ada_in[a % 2], landed if i is None else i * (16 * per // 2) + landed)
            n = a if i is None else i * per + a
            w = ada_raw[a % 2]
            if row_c is not None:
                nc.vector.tensor_tensor_reduce(crow[:, ROW_C, :], w[:], crow[:, row_c, :], 1.0, 0.0, ALU.mult, ALU.add,
                                               ada_sum[:, 4 + a % 4:5 + a % 4])
            nc.vector.tensor_tensor_reduce(w[:], w[:], crow[:, row, :], 1.0, 0.0, ALU.mult, ALU.add,
                                           ada_sum[:, a % 4:a % 4 + 1]).then_inc(ada_done, 1)
            dve.wait_ge(ada_done, n + 1)
            bias = COLS["ada_b"] + 16 + a
            if row_c is not None:
                nc.vector.tensor_tensor(ada_c[:, a - 32:a - 31], ada_sum[:, 4 + a % 4:5 + a % 4],
                                        cols[:, bias:bias + 1], ALU.add)
            if i is None:
                dst, bcol = ada[:, a:a + 1], cols[:, bias:bias + 1]
            else:
                dst, bcol = ada[:, bass.ds(n, 1)], cols[:, bass.ds(n + (COLS["ada_b"] + 16), 1)]
            nc.vector.tensor_tensor(dst, ada_sum[:, a % 4:a % 4 + 1], bcol, ALU.add).then_inc(ada_cols, 1)

        def three(out_ap, terms, first, last):
            n = 3 * len(terms)
            at = 0
            for sh, sl, mh, ml in terms:
                for s, m in ((sh, mh), (sh, ml), (sl, mh)):
                    ins = nc.tensor.matmul(out_ap, s, m, start=first and at == 0, stop=last and at == n - 1)
                    at += 1
            return ins

        def wtile(b, t):
            s = b.at % RING
            return w_hi[s][:, t * P:(t + 1) * P], w_lo[s][:, t * P:(t + 1) * P]

        def wrow(b, r):
            s = b.at % RING
            return w_hi[s][:, r * L:(r + 1) * L], w_lo[s][:, r * L:(r + 1) * L]

        def square(act, nm, j, src, n=L, scale=None):
            if j >= 3:
                act.wait_ge(nm.summed, nm.sums + j - 2)
            nc.scalar.activation((nm.std if j == 0 else nm.sq[j % 2])[:, :n], src[:, j, :], ACT.Square,
                                 scale=1.0 if scale is None else scale[:, j:j + 1]).then_inc(nm.sq_ready, 1)

        def add_square(dve, nm, j, n=L):
            if 1 <= j < KT - 1:
                dve.wait_ge(nm.sq_ready, nm.tiles + j + 1)
                if j >= 2:
                    dve.wait_ge(nm.summed, nm.sums + j - 1)
                nc.vector.tensor_tensor(nm.std[:, :n], nm.std[:, :n], nm.sq[j % 2][:, :n], ALU.add)\
                    .then_inc(nm.summed, 1)

        def norm_pe(pe, nm, n, dst_bank):
            pe.wait_ge(nm.summed, nm.sums + KT - 2)
            nc.tensor.matmul(dst_bank[:, :n], ones[:], nm.std[:, :n], start=True, stop=False)
            pe.wait_ge(nm.sq_ready, nm.tiles + KT)
            nc.tensor.matmul(dst_bank[:, :n], ones[:], nm.sq[(KT - 1) % 2][:, :n], start=False, stop=True)\
                .then_inc(nm.mm, 1)

        def norm_root(act, nm, n, src_bank, eps=eps_col):
            act.wait_ge(nm.mm, nm.once + 1)
            nc.scalar.activation(nm.rooted[:, :n], src_bank[:, :n], ACT.Sqrt, scale=1.0 / D,
                                 bias=eps[:]).then_inc(nm.root, 1)

        def norm_hi(act, nm, n, shift, dst):
            for j in range(KT):
                act.wait_ge(nm.scaled, nm.split_tiles + j + 1)
                nc.scalar.activation(dst[:, j, :], tnorm[j % 2][:, :n], ACT.Identity, bias=shift(j)).then_inc(nm.hi, 1)

        def norm_rec(dve, nm, n=L):
            dve.wait_ge(nm.root, nm.once + 1)
            nc.vector.reciprocal(nm.rstd[:, :n], nm.rooted[:, :n]).then_inc(nm.rec, 1)

        def norm_lo(dve, nm, src, n, gain, shift, dst_hi, dst_lo):
            dve.wait_ge(nm.rec, nm.once + 1)

            def rest(j):
                dve.wait_ge(nm.scaled, nm.split_tiles + j + 1)
                dve.wait_ge(nm.hi, nm.split_tiles + j + 1)
                nc.vector.scalar_tensor_tensor(out=dst_lo[:, j, :], in0=tnorm[j % 2][:, :n], scalar=shift(j),
                                               in1=dst_hi[:, j, :].bitcast(F32), op0=ALU.add,
                                               op1=ALU.subtract).then_inc(nm.lo, 1)

            for j in range(KT):
                if j >= 2:
                    dve.wait_ge(nm.lo, nm.tiles + j - 1)
                nc.vector.scalar_tensor_tensor(out=tnorm[j % 2][:, :n], in0=src[:, j, :], scalar=gain(j),
                                               in1=nm.rstd[:, :n], op0=ALU.mult, op1=ALU.mult).then_inc(nm.scaled, 1)
                if j >= 1:
                    rest(j - 1)
            rest(KT - 1)
            dve.wait_ge(nm.lo, nm.tiles + KT)

        def rms_dve(dve, nm, gain):
            norm_rec(dve, nm)
            dve.wait_ge(nm.rec, nm.once + 1)
            for j in range(KT):
                nc.vector.scalar_tensor_tensor(out=res[:, j, :], in0=res[:, j, :], scalar=gain(j), in1=nm.rstd[:],
                                               op0=ALU.mult, op1=ALU.mult).then_inc(nm.lo, 1)

        def col(name, j, n=1):
            return cols[:, COLS[name] + j:COLS[name] + j + n]

        def level_step(c0, r, c):
            return (c0 // 2) * 2 * (LEVELS + 1) + 2 * r + c - c0

        def pair_halves(tensor_of, c, l, h=None):
            t = tensor_of[:, c, 0, 0 if h is None else h, :]
            n = HEADS * P if h is None else P
            return bass.AP(tensor=t.tensor, offset=t.offset,
                           ap=[list(t.ap[0]), [2 << l, n >> (l + 1)], [HEADS * P + (1 << l), 2], [1, 1 << l]])

        def halves(flat, l, right):
            return flat.rearrange("p (b h i) -> p b h i", h=2, i=1 << l)[:, :, int(right), :]

        def half_decay(t_in, d, l, right):
            t = t_in.rearrange("p (d b h) -> p d b h", d=2, h=2)[:, d, :, int(right):int(right) + 1]
            return t.to_broadcast([P, t.shape[1], 1 << l])

        def decay_keys(k_of, t_in, l, t_out):
            fwd, bwd = (k_of[:, d].rearrange("p h n -> p (h n)") for d in range(2))
            nc.vector.tensor_tensor(halves(fwd, l, False), halves(fwd, l, False), half_decay(t_in, 1, l, True), ALU.mult)
            ins = nc.vector.tensor_tensor(halves(bwd, l, True), halves(bwd, l, True), half_decay(t_in, 0, l, False),
                                          ALU.mult)
            if t_out is not None:
                t = t_in.rearrange("p (b h) -> p b h", h=2)
                ins = nc.vector.tensor_tensor(t_out, t[:, :, 0], t[:, :, 1], ALU.mult)
            return ins

        def decay_queries(c, t_in, l):
            bwd, fwd = (hq[:, c, d].rearrange("p h n -> p (h n)") for d in range(2))
            nc.vector.tensor_tensor(halves(fwd, l, True), halves(fwd, l, True), half_decay(t_in, 1, l, False), ALU.mult)
            nc.vector.tensor_tensor(halves(bwd, l, False), halves(bwd, l, False), half_decay(t_in, 0, l, True), ALU.mult)

        S_ENTER_F = [s_init[:, 0]] + [hk[:, c, 0] for c in range(LT - 1)]
        S_ENTER_B = [hk[:, c + 1, 1] for c in range(LT - 1)] + [s_init[:, 1]]
        UPDATES = [(0, 0), (LT - 1, 1), (1, 0), (LT - 2, 1), (2, 0), (LT - 3, 1)]

        JX = {"turn": 0, "gates": 8, "q": 16, "merge": 28, "up": 44, "turn2": 88, "ret": 96, "sw0": 96 + 10 * HEADS}
        JX["cin"] = JX["sw0"] + HT
        JX["sw1"] = JX["cin"] + 16
        JX["end"] = JX["sw1"] + HT
        JY = {"turn": 0, "gates": 8, "merge": 16, "out": 32, "down": 40, "ret": 48,
              "sw0": 48 + 16 * HEADS}
        JY["sd0"] = JY["sw0"] + HT
        JY["cin"] = JY["sd0"] + 8
        JY["cout"] = JY["cin"] + 8
        JY["sw1"] = JY["cout"] + 8
        JY["sd1"] = JY["sw1"] + HT
        JY["end"] = JY["sd1"] + 8

        def before(base_count, i, per):
            return base_count if i is None else i * per + base_count

        def per_head(i, m, n):
            return n if i is None else i * m + (m + n)

        def head_blocks(i):
            return ((B_RET, JX["ret"], JY["ret"], 0, 0) if i is None else
                    (B_RET + 12, JX["ret"] + 10, JY["ret"] + 8, 4, 8))

        def take_x(pe, job, i=None, per=0):
            if job >= 2:
                pe.wait_ge(x_free, before(job - 1, i, per))
            return bx[job % 2]

        def take_y(pe, job, i=None, per=0):
            if job >= 2:
                pe.wait_ge(y_free, before(job - 1, i, per))
            return by[job % 2]

        def down_jobs(first_block):
            for ct in range(KT):
                yield ct, [(Block(first_block + (ct * HT + k) // KT), (ct * HT + k) % KT, k) for k in range(HT)]

        block = ctx.enter_context(nc.Block())

        @block.sync
        def _(sp):
            sp.dma_start(cols[:], cols_in).then_inc(cols_landed, 16)
            sp.dma_start(x_tok[:], x_in).then_inc(x_landed, 16)
            sp.dma_start(ident[:], ident_in).then_inc(ident_landed, 16)
            sp.dma_start(ctx_tok[:], ctx1_in).then_inc(ctx_landed, 16)
            for k in range(KT):
                sp.dma_start(ada_w0[:, k, :], ada_kn[k]).then_inc(ada0_in[k], 16)
                if k == KT // 2:
                    for s in range(RAW):
                        sp.dma_start(w_raw[s][:], wstream[s]).then_inc(raw_ready[s], 16)
            for n in range(3):
                sp.dma_start(crow[:, n, :], crow_in[n:n + 1, :].to_broadcast([P, D])).then_inc(crow_landed, 16)
            sp.dma_start(dft1[:], dft1_in).then_inc(dft1_landed, 16)
            sp.dma_start(masks[:], masks_in).then_inc(masks_landed, 16)
            with sp.Fori(0, N_BLOCKS // RAW - 1) as i:
                for s in range(RAW):
                    n = i * RAW + (s + RAW)
                    sp.wait_ge(lo_ready, i * RAW + (s + 1))
                    sp.dma_start(w_raw[s][:], wstream[bass.ds(n, 1)].rearrange("o p n -> (o p) n"))\
                        .then_inc(raw_ready[s], 16)
            for t in range(LT):
                sp.wait_ge(out_copied, 2 * t + 2)
                sp.dma_start(out[t * P:(t + 1) * P, :], out_tok[:, t, :]).then_inc(out_stored, 16)
            sp.wait_ge(out_stored, 16 * LT)

        def turn_pe(pe, src_tok, dst_tiles, take, job0, done):
            for j in range(KT):
                b = take(pe, job0 + j)
                for t in range(dst_tiles):
                    ins = nc.tensor.transpose(b[:, t * P:(t + 1) * P], src_tok[:, t, j * P:(j + 1) * P], ident[:])
                ins.then_inc(done, 1)

        def none(j):
            pass

        def hidden_down_pe(pe, first_block, job0, hid_ready, ready0, beside):
            for ct, tiles in down_jobs(first_block):
                dst = take_y(pe, job0 + ct)
                for b, t, k in tiles:
                    if t == 0 or k == 0:
                        pe.wait_ge(lo_ready, b.count(1))
                    if ct == 0:
                        pe.wait_ge(hid_ready, ready0 + k + 1)
                    wh, wl = wtile(b, t)
                    ins = three(dst[:], [(wh, wl, hid_hi[:, k, :], hid_lo[:, k, :])], k == 0, k == HT - 1)
                    if t == KT - 1:
                        ins.then_inc(block_done, 1)
                if tiles[-1][1] != KT - 1:
                    ins.then_inc(down_done[first_block], 1)
                beside(ct)

        down_done = {B_DOWN: sem("down_done0"), B_SD0: sem("down_done1"), B_SD1: sem("down_done2")}

        def pair_pe(pe, nm, pair, ends=True):
            for b, _ in pair:
                pe.wait_ge(lo_ready, b.count(1))
            for k in range(KT):
                pe.wait_ge(nm.lo, nm.tiles + k + 1)
                for b, dst in pair:
                    wh, wl = wtile(b, k)
                    ins = three(dst[:], [(wh, wl, hx_hi[:, k, :], hx_lo[:, k, :])], k == 0, k == KT - 1)
                    if ends and k == KT - 1:
                        ins.then_inc(block_done, 1)

        def block_pe(pe, b, dst):
            pe.wait_ge(lo_ready, b.count(1))
            for k in range(KT):
                wh, wl = wtile(b, k)
                ins = three(dst[:], [(wh, wl, hx_hi[:, k, :], hx_lo[:, k, :])], k == 0, k == KT - 1)
            ins.then_inc(block_done, 1)

        def swiglu_pe(pe, first_block, jx, jy, nm):
            def job(i, u, kind):
                return (Block(first_block + 2 * u + kind, i, 4),
                        (take_x if kind == 0 else take_y)(pe, (jx if kind == 0 else jy) + u, i, 2))

            pair_pe(pe, nm, [job(None, 0, kind) for kind in range(2)])
            for kind in range(2):
                block_pe(pe, *job(None, 1, kind))
            with pe.Fori(0, HT // 2 - 1) as i:
                for u in (2, 3):
                    for kind in range(2):
                        block_pe(pe, *job(i, u, kind))

        def square_pe(pe, first_block, jy, m_hi_, m_lo_, ready):
            for j in range(KT):
                b = Block(first_block + j)
                dst = take_y(pe, jy + j)
                pe.wait_ge(lo_ready, b.count(1))
                for k in range(KT):
                    if j == 0:
                        pe.wait_ge(ready, k + 1)
                    wh, wl = wtile(b, k)
                    ins = three(dst[:], [(wh, wl, m_hi_[:, k, :], m_lo_[:, k, :])], k == 0, k == KT - 1)
                ins.then_inc(block_done, 1)

        def values_pe(pe, b0, dsts, i=None, per=0):
            for n in range(4):
                b = Block(b0 + n, i, per)
                pe.wait_ge(lo_ready, b.count(1))
                for r in range(2):
                    k = 2 * n + r
                    wh, wl = wrow(b, r)
                    for t in range(LT + LCT):
                        if t < LT:
                            sh, sl = (h[:, k, t * P:(t + 1) * P] for h in (hx_hi, hx_lo))
                        else:
                            sh, sl = (h[:, k, (t - LT) * P:(t - LT + 1) * P] for h in (hc_hi, hc_lo))
                        ins = three(dsts[t][:], [(sh, sl, wh, wl)], k == 0, k == KT - 1)
                ins.then_inc(block_done, 1)

        ada_banks = [bw[0], bw[1], by[0], by[1]]
        six = [bx[0], bx[1], by[0], by[1], bw[0], bw[1]]

        @block.tensor
        def _(pe):
            pe.wait_ge(ident_landed, 16)
            pe.wait_ge(x_landed, 16)
            turn_pe(pe, x_tok, LT, take_x, JX["turn"], turned)
            pe.wait_ge(ctx_landed, 16)
            turn_pe(pe, ctx_tok, LCT, take_y, JY["turn"], turned)
            pe.wait_ge(scol_ready, 1)
            pe.wait_ge(y_free, JY["gates"])
            for k in range(KT):
                pe.wait_ge(ada0_in[k], 16)
                for n in range(4):
                    ins = nc.tensor.matmul(ada_banks[n][:2, :], scol[:, :, k], ada_w0[:, k, n * L:(n + 1) * L],
                                           start=(k == 0), stop=(k == KT - 1))
                    if k == KT - 1:
                        ins.then_inc(ada0_mm, 1)
                if k == KT // 2:
                    pe.wait_ge(consts, 2)
                    norm_pe(pe, n1x, L, bn)
                    norm_pe(pe, n1c, LC, bank[4])
            pe.wait_ge(ada0_rows, 4)
            for a in range(16):
                ins = nc.tensor.transpose(bw[0][:, 2 * a:2 * a + 2], ada_rows[:, a * P:(a + 1) * P], ident[:2, :2])
            ins.then_inc(ada0_turned, 1)
            def gate_ctx(n, b):
                dc = take_y(pe, JY["gates"] + n)
                for k in range(KT):
                    if n == 0:
                        pe.wait_ge(n1c.lo, n1c.tiles + k + 1)
                    wh, wl = wtile(b, k)
                    ins = three(dc[:, :LC], [(wh, wl, hc_hi[:, k, :], hc_lo[:, k, :])], k == 0, k == KT - 1)
                ins.then_inc(block_done, 1)

            pair = [(Block(B_GATES + n), take_x(pe, JX["gates"] + n)) for n in range(2)]
            pair_pe(pe, n1x, pair, False)
            for n, (b, _) in enumerate(pair):
                gate_ctx(n, b)
            for n in range(2, 8):
                b = Block(B_GATES + n)
                dx = take_x(pe, JX["gates"] + n)
                pe.wait_ge(lo_ready, b.count(1))
                for k in range(KT):
                    wh, wl = wtile(b, k)
                    three(dx[:], [(wh, wl, hx_hi[:, k, :], hx_lo[:, k, :])], k == 0, k == KT - 1)
                gate_ctx(n, b)
            pe.wait_ge(x_free, JX["q"])
            pe.wait_ge(y_free, JY["merge"])
            pe.wait_ge(ada0_ready, 1)
            values_pe(pe, B_VAL, six)
            for n in range(4):
                if n < 2:
                    pe.wait_ge(v_ready, n + 1)
                block_pe(pe, Block(B_Q + n), take_x(pe, JX["q"] + n))
            pe.wait_ge(v_ready, 6)
            pe.wait_ge(kc_level, LEVELS + 1)
            for g in range(4):
                if g >= 2:
                    pe.wait_ge(kd_ready, g - 1)
                for hh in range(2):
                    h = 2 * (g % 2) + hh
                    for t in range(LCT):
                        ins = nc.tensor.transpose(bw[g % 2][:, (2 * hh + t) * P:(2 * hh + t + 1) * P],
                                                  kc[:, g // 2, h, t * P:(t + 1) * P], ident[:])
                ins.then_inc(kc_turned, 1)
            pe.wait_ge(kd_ready, 4)
            for d in range(2):
                for h in range(HEADS):
                    for t in range(LCT):
                        ins = nc.tensor.matmul(bank[4 + d][:, h * P:(h + 1) * P], kd_c[:, d, h, t, :],
                                               v_c[:, t, h * P:(h + 1) * P], start=(t == 0), stop=(t == LCT - 1))
                ins.then_inc(s0_mm, 1)
            pe.wait_ge(x_free, JX["q"] + 4)
            step = 0
            for c0 in (0, 2):
                for r in range(LEVELS + 1):
                    for c in (c0, c0 + 1):
                        pe.wait_ge(level_ready, level_step(c0, r, c) + 1)
                        if r >= 1:
                            pe.wait_ge(k_gathered, level_step(c0, r, c) - 2 * (c0 // 2) - 1)
                        for h in range(HEADS):
                            dst = bw[c % 2][:, h * P:(h + 1) * P]
                            if r == 0:
                                ins = nc.tensor.matmul(dst, ksum[c % 2][:, h, :], hq[:, c, 0, h, :],
                                                       start=True, stop=True)
                            else:
                                ins = nc.tensor.matmul(dst, level_k[c % 2][:, h * P:(h + 1) * P],
                                                       pair_halves(hq, c, r - 1, h), start=True, stop=True)
                        ins.then_inc(level_mm, 1)
                        b, part = Block(B_FNET + step // STEPS), step % STEPS
                        if part == 0:
                            fg = take_x(pe, JX["q"] + 4 + step // STEPS)
                            pe.wait_ge(lo_ready, b.count(1))
                        for k in range(part * KT // STEPS, (part + 1) * KT // STEPS):
                            wh, wl = wtile(b, k)
                            ins = three(fg[:], [(wh, wl, hx_hi[:, k, :], hx_lo[:, k, :])], k == 0, k == KT - 1)
                        if part == STEPS - 1:
                            ins.then_inc(block_done, 1)
                        step += 1
            pe.wait_ge(x_free, JX["merge"])
            for n, (c, d) in enumerate(UPDATES):
                pe.wait_ge(chunk_ready, c + 1)
                if n >= 2:
                    pe.wait_ge(kd_copied, n - 1)
                for h in range(HEADS):
                    ins = nc.tensor.transpose(bx[n % 2][:, h * P:(h + 1) * P], hk[:, c, d, h, :], ident[:])
                ins.then_inc(k_turned, 1)
                pe.wait_ge(kd_copied, n + 1)
                if n >= 2:
                    pe.wait_ge(upd_done, n - 1)
                for h in range(HEADS):
                    ins = nc.tensor.matmul(by[n % 2][:, h * P:(h + 1) * P], kd_x[n % 2][:, h, :],
                                           v_x[:, c, h * P:(h + 1) * P], start=True, stop=True)
                ins.then_inc(upd_mm, 1)
            pe.wait_ge(upd_done, len(UPDATES))
            def o_pe(c):
                if c >= 2:
                    pe.wait_ge(osq_ready, c - 1)
                for h in range(HEADS):
                    dst = bw[c % 2][:, h * P:(h + 1) * P]
                    nc.tensor.matmul(dst, v_x[:, c, h * P:(h + 1) * P], att[c][:, h, :], start=True, stop=False)
                    nc.tensor.matmul(dst, S_ENTER_F[c][:, h, :], hq[:, c, 1, h, :], start=False, stop=False)
                    ins = nc.tensor.matmul(dst, S_ENTER_B[c][:, h, :], hq[:, c, 0, h, :], start=False, stop=True)
                ins.then_inc(o_mm, 1)

            def osum_pe(c):
                pe.wait_ge(osq_ready, c + 1)
                if c >= 1:
                    pe.wait_ge(ostd, c)
                nc.tensor.matmul(bn[:], ones[:], sq[c % 2][:], start=True, stop=True).then_inc(osum_mm, 1)

            def pq_pe(t):
                for gp in range(2):
                    n = 2 * t + gp
                    if n >= 2:
                        pe.wait_ge(pq_ready, n - 1)
                    for g in (2 * gp, 2 * gp + 1):
                        ins = nc.tensor.matmul(by[gp][:, (g % 2) * 2 * P:(g % 2 + 1) * 2 * P],
                                               ut[:, g, t * P:(t + 1) * P], dft1[:], start=True, stop=True)
                    ins.then_inc(pq_mm, 1)

            pe.wait_ge(dft1_landed, 16)
            for c in range(3):
                o_pe(c)
            osum_pe(0)
            o_pe(3)
            osum_pe(1)
            pq_pe(0)
            osum_pe(2)
            pq_pe(1)
            osum_pe(3)
            pq_pe(2)
            pq_pe(3)
            pe.wait_ge(pq_ready, 2 * LT)
            pe.wait_ge(dft2_landed, 16)
            for g in range(HEADS):
                if g >= 2:
                    pe.wait_ge(ya_l, g - 1)
                for cs in range(2):
                    for t in range(LT):
                        ins = nc.tensor.matmul(bw[g % 2][:], pq[:, t, g, cs * P:(cs + 1) * P], dft2[:, cs, t, :],
                                               start=(cs == 0 and t == 0), stop=(cs == 1 and t == LT - 1))
                ins.then_inc(ya_mm, 1)
            with pe.Fori(0, 2) as i:
                for u in range(4):
                    for kind in range(2):
                        b = Block(B_MERGE + 3 * u + kind, i, 12)
                        dst = take_x(pe, JX["merge"] + 2 * u + kind, i, 8)
                        pe.wait_ge(lo_ready, b.count(1))
                        for k in range(KT):
                            wh, wl = wtile(b, k)
                            ins = three(dst[:], [(wh, wl, hx_hi[:, k, :], hx_lo[:, k, :])], k == 0, k == KT - 1)
                        ins.then_inc(block_done, 1)
                    b = Block(B_MERGE + 3 * u + 2, i, 12)
                    pe.wait_ge(lo_ready, b.count(1))
                    pe.wait_ge(ya_l, HEADS)
                    pe.wait_ge(yb_l, LT)
                    for br, (yh, yl) in enumerate(((ya_hi, ya_lo), (yb_hi, yb_lo))):
                        dst = take_y(pe, JY["merge"] + 2 * u + br, i, 8)
                        for k in range(HEADS):
                            wh, wl = wtile(b, HEADS * br + k)
                            ins = three(dst[:], [(wh, wl, yh[:, k, :], yl[:, k, :])], k == 0, k == HEADS - 1)
                    ins.then_inc(block_done, 1)
            square_pe(pe, B_OUT, JY["out"], m_hi, m_lo, m_l)
            norm_pe(pe, n2, L, bn)
            def up_job(i, u):
                return Block(B_UP + u, i, 4), take_x(pe, JX["up"] + u, i, 4)

            pair_pe(pe, n2, [up_job(None, u) for u in range(2)])
            for u in (2, 3):
                block_pe(pe, *up_job(None, u))
            with pe.Fori(0, HT // 2 - 1) as i:
                for u in range(4, 8):
                    block_pe(pe, *up_job(i, u))

            def context_pe(job):
                if job == 0:
                    pe.wait_ge(ctx2_landed, 16)
                if job < 4:
                    for j in (2 * job, 2 * job + 1):
                        dst = take_x(pe, JX["turn2"] + j)
                        for t in range(LCT):
                            ins = nc.tensor.transpose(dst[:, t * P:(t + 1) * P], ctx2_tok[:, t, j * P:(j + 1) * P], ident[:])
                        ins.then_inc(turned2, 1)
                if job == 5:
                    norm_pe(pe, nmc, LC, bank[4])

            hidden_down_pe(pe, B_DOWN, JY["down"], hid_l, 2, context_pe)
            norm_pe(pe, nmx, L, bn)
            pe.wait_ge(nmc.root, 1)
            norm_pe(pe, nf1, L, bank[4])
            def wo_pe(b0, jy, i, ready):
                for n in range(4):
                    b = Block(b0 + n, i, 16)
                    pe.wait_ge(lo_ready, b.count(1))
                    for u in range(2):
                        dst = take_y(pe, jy + 2 * n + u, i, 16)
                        for k in range(HEADS):
                            if n == 0 and u == 0:
                                pe.wait_ge(ry_l, ready(k + 1))
                            wh, wl = wtile(b, HEADS * u + k)
                            ins = three(dst[:], [(wh, wl, ry_hi[:, k, :], ry_lo[:, k, :])], k == 0, k == HEADS - 1)
                        ins.then_inc(wo_half if u == 0 else block_done, 1)

            def head_pe(i):
                b0, jx, jy, ob, oy = head_blocks(i)
                if i is None:
                    pair_pe(pe, nmx, [(Block(b0 + n), take_y(pe, jy + n)) for n in range(2)])
                for n in range(2 if i is None else 0, 4):
                    b = Block(b0 + n, i, 16)
                    dst = take_y(pe, jy + n, i, 16) if n < 2 else bw[n - 2]
                    pe.wait_ge(lo_ready, b.count(1))
                    for k in range(KT):
                        wh, wl = wtile(b, k)
                        ins = three(dst[:], [(wh, wl, hx_hi[:, k, :], hx_lo[:, k, :])], k == 0, k == KT - 1)
                    if n >= 2:
                        dc = take_x(pe, jx + n - 2, i, 10)
                        if i is None:
                            pe.wait_ge(nmc.lo, nmc.tiles + KT)
                        for k in range(KT):
                            wh, wl = wtile(b, k)
                            ins = three(dc[:, :LC], [(wh, wl, hc_hi[:, k, :], hc_lo[:, k, :])], k == 0, k == KT - 1)
                    ins.then_inc(block_done, 1)
                if i is not None:
                    wo_pe(b0 + 4, jy + 2, i, lambda k: before(k, i, HEADS))
                pe.wait_ge(x_free, before(jx + 2, i, 10))
                pe.wait_ge(y_free, before(jy + oy + 2, i, 16))
                pe.wait_ge(rot_p, per_head(i, 2, 2))
                values_pe(pe, b0 + ob + 4, rbanks, i, 16)
                pe.wait_ge(rot_l, per_head(i, 4, 4))
                pe.wait_ge(x_free, before(jx + 2, i, 10))
                for s in range(KEYS):
                    if s < 2:
                        pe.wait_ge(rv_l, per_head(i, KEYS, s + 1))
                    dst = take_y(pe, jy + oy + 2 + s, i, 16)
                    ins = three(dst[:], [(rk_hi[:, dt, s * P:(s + 1) * P], rk_lo[:, dt, s * P:(s + 1) * P],
                                          rq_hi[:, dt, :], rq_lo[:, dt, :]) for dt in range(2)], True, True)
                    ins.then_inc(sc_mm, 1)
                for n in range(4):
                    b = Block(b0 + ob + 8 + n, i, 16)
                    if n < 2:
                        pe.wait_ge(rv_l, per_head(i, KEYS, n + 3))
                    dst = take_x(pe, jx + 2 + n, i, 10)
                    pe.wait_ge(lo_ready, b.count(1))
                    for k in range(KT):
                        wh, wl = wtile(b, k)
                        ins = three(dst[:], [(wh, wl, hx_hi[:, k, :], hx_lo[:, k, :])], k == 0, k == KT - 1)
                    ins.then_inc(block_done, 1)
                pe.wait_ge(rv_l, per_head(i, KEYS, KEYS))
                for e in range(HEADS):
                    dst = take_x(pe, jx + 6 + e, i, 10)
                    for s in range(KEYS):
                        if e == 0:
                            pe.wait_ge(sc_l, per_head(i, KEYS, s + 1))
                        cut = slice(e * P, (e + 1) * P)
                        ins = three(dst[:], [(rv_hi[:, s, cut], rv_lo[:, s, cut], rsc_hi[:, s, :], rsc_lo[:, s, :])],
                                    s == 0, s == KEYS - 1)
                    ins.then_inc(ro_mm, 1)
                pe.wait_ge(ro_sum, per_head(i, 2, 2))
                nc.tensor.matmul(bn[:], ones[:], std[:], start=True, stop=False)
                pe.wait_ge(x_free, before(jx + 10, i, 10))
                nc.tensor.matmul(bn[:], ones[:], rsq[1][:], start=False, stop=True).then_inc(rsum_mm, 1)

            head_pe(None)
            with pe.Fori(0, HEADS - 1) as i:
                head_pe(i)
            wo_pe(B_SW0 - 4, JY["sw0"] - 8, None, lambda k: HEADS * (HEADS - 1) + k)
            norm_pe(pe, nffn0, L, bn)
            swiglu_pe(pe, B_SW0, JX["sw0"], JY["sw0"], nffn0)
            hidden_down_pe(pe, B_SD0, JY["sd0"], sw_l[0], 0, none)
            norm_pe(pe, nmix1, L, bn)
            def cin_job(u, kind):
                return (Block(B_CIN + 3 * u + kind), take_x(pe, JX["cin"] + 2 * u + kind) if kind < 2 else
                        take_y(pe, JY["cin"] + u))

            pair_pe(pe, nmix1, [cin_job(0, kind) for kind in range(2)])
            for u in range(KT):
                for kind in range(3):
                    if u or kind == 2:
                        block_pe(pe, *cin_job(u, kind))
            square_pe(pe, B_COUT, JY["cout"], cy_hi, cy_lo, cy_l)
            norm_pe(pe, nffn1, L, bn)
            swiglu_pe(pe, B_SW1, JX["sw1"], JY["sw1"], nffn1)
            hidden_down_pe(pe, B_SD1, JY["sd1"], sw_l[1], 0, none)
            norm_pe(pe, nf2, L, bn)
            pe.wait_ge(nf2.lo, nf2.tiles + KT)
            for t in range(LT):
                for half in range(2):
                    n = 2 * t + half
                    if n >= 2:
                        pe.wait_ge(out_copied, n - 1)
                    for j in range(4):
                        ins = nc.tensor.transpose(bw[n % 2][:, j * P:(j + 1) * P],
                                                  res[:, 4 * half + j, t * P:(t + 1) * P], ident[:])
                    ins.then_inc(turned_out, 1)

        def swiglu_act(act, w, first_block, jx, jy, ada0_at):
            with act.Fori(0, HT // 2) as i:
                for u in range(2):
                    b = Block(first_block + 2 * u, i, 4)
                    split_hi(act, b)
                    if ada0_at is not None:
                        ada_load(act, ada0_at + 2 * u + 1, i, 4)
                    act.wait_ge(block_done, b.count(1))
                    act.wait_ge(lo_ready, b.count(AHEAD - 1))
                    nc.scalar.activation(sw[u][:], bx[(jx + u) % 2][:], ACT.Silu).then_inc(x_free, 1)
                    split_hi(act, b.plus(1))
                    if ada0_at is not None:
                        ada_load(act, ada0_at + 2 * u + 2, i, 4)
                    act.wait_ge(y_free, before(jy + u + 1, i, 2))
                    nc.scalar.activation(hid_hi[:, bass.ds(i * 2 + u, 1), :].rearrange("p o n -> p (o n)"), sw[u][:],
                                         ACT.Copy).then_inc(sw_h[w], 1)

        def square_act(act, first_block, job0, nm):
            for j in range(KT + 1):
                if j < KT:
                    split_hi(act, Block(first_block + j))
                if j >= 1:
                    act.wait_ge(y_free, job0 + j)
                    square(act, nm, j - 1, res)

        def down_act(act, first_block, job0, norms, ada_of, beside):
            ends = [tiles[-1][0].at - first_block for _, tiles in down_jobs(first_block)]
            for n in range(HT + 1):
                if n < HT:
                    split_hi(act, Block(first_block + n))
                    ada_of(n)
                for j in range(KT):
                    if ends[j] == n - 1:
                        act.wait_ge(y_free, job0 + j + 1)
                        for nm, scale in norms:
                            square(act, nm, j, res, scale=scale)
                        beside(j)

        def osqrt(act, c):
            act.wait_ge(osum_mm, c + 1)
            if c >= 1:
                act.wait_ge(orstd, c)
            nc.scalar.activation(std[:], bn[:], ACT.Sqrt, scale=1.0 / P, bias=eps_col[:]).then_inc(ostd, 1)

        @block.scalar
        def _(act):
            act.wait_ge(cols_landed, 16)
            nc.scalar.activation(scol[:], cols[:, COLS["c"]:COLS["c"] + 16].rearrange("p (v k) -> p v k", v=2),
                                 ACT.Silu).then_inc(scol_ready, 1)
            act.wait_ge(lb_ready, 1)
            nc.scalar.activation(lb[:], oml[:], ACT.Sigmoid).then_inc(lb_ready, 1)
            for j in range(KT):
                act.wait_ge(turned, j + 1)
                nc.scalar.activation(res[:, j, :], bx[j % 2][:], ACT.Copy).then_inc(x_free, 1)
            for j in range(KT):
                act.wait_ge(x_free, JX["turn"] + j + 1)
                square(act, n1x, j, res)
            for j in range(KT):
                act.wait_ge(y_free, JY["turn"] + j + 1)
                square(act, n1c, j, ctx_t, LC)
            for b in range(RAW):
                split_hi(act, Block(b - AHEAD))
            act.wait_ge(consts, 2)
            nc.scalar.activation(fcol[:], col("final1", 0, KT), ACT.Square).then_inc(fcol_ready, 1)
            norm_root(act, n1x, L, bn)
            norm_root(act, n1c, LC, bank[4])
            act.wait_ge(fcol_ready, 1)
            nc.scalar.activation(fcol[:], fcol[:], ACT.Sqrt, bias=eps_col[:]).then_inc(fcol_ready, 1)
            for n in range(2):
                act.wait_ge(ada0_mm, n + 1)
                nc.scalar.activation(ada_rows[:, n * L:(n + 1) * L], ada_banks[n][:2, :], ACT.Copy).then_inc(ada0_rows, 1)
            norm_hi(act, n1x, L, lambda j: ada0[:, j, 0:1], hx_hi)
            norm_hi(act, n1c, LC, lambda j: ada0[:, j, 1:2], hc_hi)
            for b in range(RAW, AHEAD):
                split_hi(act, Block(b - AHEAD))
            ada_load(act, 0)
            act.wait_ge(crow_landed, 48)
            nc.scalar.activation(crow[:], crow[:], ACT.Silu).then_inc(crow_silu, 1)
            act.wait_ge(n1c.lo, n1c.tiles + KT)
            act.wait_ge(lb_ready, 3)
            for n in range(8):
                b = Block(B_GATES + n)
                d, h = n // HEADS, n % HEADS
                split_hi(act, b)
                ada_load(act, n + 1)
                act.wait_ge(block_done, b.count(1))
                if n >= 2:
                    act.wait_ge(f_ready, 2 * n - 2)
                nc.scalar.activation(sig[n % 2][:, :L], bx[n % 2][:], ACT.Sigmoid).then_inc(x_free, 1)
                nc.scalar.activation(sig[n % 2][:, L:], by[n % 2][:, :LC], ACT.Sigmoid).then_inc(y_free, 1)
                act.wait_ge(x_free, JX["gates"] + n + 1)
                nc.scalar.activation(hf[:, :, 1 - d, h, :], sig[n % 2][:, :L].rearrange("p (c t) -> p c t", c=LT),
                                     ACT.Identity, scale=oml[:, h:h + 1], bias=lb[:, h:h + 1]).then_inc(f_ready, 1)
                act.wait_ge(y_free, JY["gates"] + n + 1)
                nc.scalar.activation(fc[:, 1 - d, h, :], sig[n % 2][:, L:], ACT.Identity, scale=oml[:, h:h + 1],
                                     bias=lb[:, h:h + 1]).then_inc(f_ready, 1)
            for n in range(4):
                split_hi(act, Block(B_VAL + n))
            act.wait_ge(block_done, B_VAL + 4)
            for t in range(LT + LCT):
                dst = v_x[:, t, :] if t < LT else v_c[:, t - LT, :]
                nc.scalar.activation(dst, six[t][:], ACT.Copy).then_inc(v_ready, 1)
            for n in range(4):
                b = Block(B_Q + n)
                split_hi(act, b)
                act.wait_ge(block_done, b.count(1))
                for d in range(2):
                    ins = nc.scalar.activation(hq[:, :, d, n, :], bx[n % 2][:].rearrange("p (c t) -> p c t", c=LT), ACT.Silu)
                ins.then_inc(x_free, 1)
            for g in range(4):
                act.wait_ge(kc_turned, g + 1)
                nc.scalar.activation(kd_c[:, g // 2, 2 * (g % 2):2 * (g % 2) + 2, :, :].rearrange("p h t n -> p (h t n)"),
                                     bw[g % 2][:], ACT.Copy).then_inc(kd_ready, 1)
            for d in range(2):
                act.wait_ge(s0_mm, d + 1)
                nc.scalar.activation(s_init[:, d, :, :].rearrange("p h n -> p (h n)"), bank[4 + d][:], ACT.Copy)\
                    .then_inc(s_ready, 1)
            step = 0
            for c0 in (0, 2):
                for r in range(LEVELS + 1):
                    for c in (c0, c0 + 1):
                        fg, h = step // STEPS, step // STEPS % HEADS
                        if step % STEPS == 0:
                            split_hi(act, Block(B_FNET + fg))
                        if r >= 1:
                            n = level_step(c0, r, c)
                            act.wait_ge(level_ready, n + 1)
                            if r >= 2:
                                act.wait_ge(level_mm, n - 1)
                            nc.scalar.activation(level_k[c % 2][:].rearrange(
                                "p (b h i) -> p b h i", h=2, i=1 << (r - 1)), pair_halves(hk, c, r - 1), ACT.Copy)\
                                .then_inc(k_gathered, 1)
                        if step % STEPS == STEPS - 1:
                            act.wait_ge(block_done, B_FNET + fg + 1)
                            if fg < HEADS:
                                nc.scalar.activation(ut[:, h, :], bx[fg % 2][:], ACT.Copy).then_inc(x_free, 1)
                            else:
                                nc.scalar.activation(gs[:, h, :], bx[fg % 2][:], ACT.Silu).then_inc(x_free, 1)
                        step += 1
            act.wait_ge(x_free, JX["merge"])
            for h in range(HEADS):
                nc.scalar.activation(gs[:, h, :], gs[:, h, :], ACT.Copy, scale=col("onorm", h)).then_inc(gs_ready, 1)
            for n in range(len(UPDATES)):
                act.wait_ge(k_turned, n + 1)
                if n >= 2:
                    act.wait_ge(upd_mm, n - 1)
                nc.scalar.activation(kd_x[n % 2][:].rearrange("p h n -> p (h n)"), bx[n % 2][:], ACT.Copy)\
                    .then_inc(kd_copied, 1)
            for c in range(LT):
                act.wait_ge(o_mm, c + 1)
                nc.scalar.activation(ho[:, c, 0, :, :].rearrange("p h n -> p (h n)"), bw[c % 2][:], ACT.Copy)\
                    .then_inc(o_ready, 1)
                if c >= 2:
                    act.wait_ge(osum_mm, c - 1)
                nc.scalar.activation(sq[c % 2][:], bw[c % 2][:], ACT.Square).then_inc(osq_ready, 1)
                if c >= 1:
                    osqrt(act, c - 1)
            act.dma_start(dft2[:], dft2_in).then_inc(dft2_landed, 16)
            for c in range(LT):
                for n in (2 * c, 2 * c + 1):
                    act.wait_ge(pq_mm, n + 1)
                    nc.scalar.activation(pq[:, n // 2, 2 * (n % 2):2 * (n % 2) + 2, :].rearrange("p g n -> p (g n)"),
                                         by[n % 2][:], ACT.Copy).then_inc(pq_ready, 1)
                if c == 1:
                    osqrt(act, LT - 1)
                act.wait_ge(yb_f, c + 1)
                nc.scalar.activation(yb_hi[:, :, c * P:(c + 1) * P],
                                     yt[c % 2][:].rearrange("p (h n) -> p h n", h=HEADS), ACT.Copy).then_inc(yb_h, 1)
            for g in range(HEADS):
                act.wait_ge(ya_mm, g + 1)
                nc.scalar.activation(ya_hi[:, g, :], bw[g % 2][:], ACT.Copy).then_inc(ya_h, 1)
            act.wait_ge(yb_l, LT)
            act.wait_ge(ya_l, HEADS)
            with act.Fori(0, 2) as i:
                for u in range(4):
                    for kind in range(2):
                        b = Block(B_MERGE + 3 * u + kind, i, 12)
                        split_hi(act, b)
                        ada_load(act, 9 + 3 * u + kind, i, 12)
                        act.wait_ge(block_done, b.count(1))
                        nc.scalar.activation((gate_a if kind == 0 else gate_b)[u % 2][:], bx[kind][:], ACT.Sigmoid)\
                            .then_inc(x_free, 1)
                    b = Block(B_MERGE + 3 * u + 2, i, 12)
                    split_hi(act, b)
                    ada_load(act, 9 + 3 * u + 2, i, 12)
                    act.wait_ge(m_f, before(u + 1, i, 4))
                    nc.scalar.activation(m_hi[:, bass.ds(i * 4 + u, 1), :].rearrange("p o n -> p (o n)"), mt[u % 2][:],
                                         ACT.Copy).then_inc(m_h, 1)
            act.wait_ge(m_l, KT)
            square_act(act, B_OUT, JY["out"], n2)
            norm_root(act, n2, L, bn)
            norm_hi(act, n2, L, lambda j: ada[:, 8 + j:9 + j], hx_hi)
            act.wait_ge(n2.lo, n2.tiles + KT)
            def conv_in(i, s, at):
                for k in range(2):
                    b = Block(B_UP + 2 * (at + s) + k, i, 4)
                    split_hi(act, b)
                    act.wait_ge(block_done, b.count(1))
                    act.wait_ge(hid_l, before(at + s + 1, i, 2))
                    cw = COLS["conv"] + 20 * (at + s) + 10 * k
                    centre, bias = ((cols[:, bass.ds(i * 40 + (cw + t), 1)] if i is not None else
                                     cols[:, cw + t:cw + t + 1]) for t in (4, 9))
                    src = bx[k][:].rearrange("p (r c) -> p r c", r=ROWS)
                    nc.scalar.activation(zpad[s][k][:, 1:ROWS + 1, 1:GRID + 1], src, ACT.Copy)
                    nc.scalar.activation(acc[s][k][:], bx[k][:], ACT.Identity, scale=centre, bias=bias).then_inc(x_free, 1)

            def conv_out(i, s, at):
                act.wait_ge(tap_done, before(16 * (at + s) + 15, i, 32))
                nc.scalar.activation(sgate[s][:], acc[s][0][:], ACT.Silu)
                act.wait_ge(tap_done, before(16 * (at + s) + 16, i, 32))
                nc.scalar.activation(hidden[s][:], acc[s][1][:], ACT.Copy).then_inc(silu_done, 1)
                act.wait_ge(hid_f, before(at + s + 1, i, 2))
                dst = hid_hi[:, at + s, :] if i is None else \
                    hid_hi[:, bass.ds(i * 2 + (at + s), 1), :].rearrange("p o n -> p (o n)")
                nc.scalar.activation(dst, hidden[s][:], ACT.Copy).then_inc(hid_h, 1)

            nc.scalar.activation(table_col[:], eps_col[:], ACT.Silu)
            conv_in(None, 0, 0)
            with act.Fori(0, HT // 2 - 1) as i:
                conv_in(i, 1, 0)
                conv_out(i, 0, 0)
                conv_in(i, 0, 2)
                conv_out(i, 1, 0)
            conv_in(None, 1, HT - 2)
            conv_out(None, 0, HT - 2)
            conv_out(None, 1, HT - 2)
            def context_act(job):
                if job < 4:
                    for j in (2 * job, 2 * job + 1):
                        act.wait_ge(turned2, j + 1)
                        nc.scalar.activation(ctx2_t[:, j, :], bx[j % 2][:, :LC], ACT.Copy).then_inc(x_free, 1)
                if job == 4:
                    for j in range(KT):
                        act.wait_ge(x_free, JX["turn2"] + j + 1)
                        square(act, nmc, j, ctx2_t, LC)
                if job == 6:
                    norm_root(act, nmc, LC, bank[4])

            act.wait_ge(fcol_ready, 2)
            act.wait_ge(block_done, B_DOWN)
            act.dma_start(ctx2_tok[:], ctx2_in).then_inc(ctx2_landed, 16)
            down_act(act, B_DOWN, JY["down"], [(nmx, fcol), (nf1, None)], lambda n: ada_load(act, 33 + n) if n < 16 else None, context_act)
            act.wait_ge(block_done, B_RET)
            act.dma_start(rope[:], rope_in).then_inc(rope_landed, 16)
            norm_root(act, nmx, L, bn, eps2_col)
            norm_hi(act, nmx, L, lambda j: ada[:, 32 + j:33 + j], hx_hi)
            norm_hi(act, nmc, LC, lambda j: ada_c[:, j:j + 1], hc_hi)
            act.wait_ge(nmc.lo, nmc.tiles + KT)
            norm_root(act, nf1, L, bank[4])
            def head_act(i):
                b0, jx, jy, ob, oy = head_blocks(i)
                a0 = 48 if i is None else 56
                if i is None:
                    act.wait_ge(ada_done, 48)
                else:
                    act.wait_ge(y_free, before(jy, i, 16))
                src = dec_in[0] if i is None else dec_in[bass.ds(i + 1, 1)].rearrange("o p n -> (o p) n")
                act.dma_start(dec[:], src).then_inc(dec_landed, 16)

                def rotated_hi(n):
                    act.wait_ge(rot_f, per_head(i, 4, n + 1))
                    nc.scalar.activation((rq_hi if n < 2 else rk_hi)[:, n % 2, :L], rot[n % 2][:], ACT.Copy)\
                        .then_inc(rot_h, 1)

                for n in range(4):
                    b = Block(b0 + n, i, 16)
                    if n >= 1 or i is None:
                        split_hi(act, b)
                    if n >= 2:
                        act.wait_ge(block_done, b.count(1))
                        nc.scalar.activation(rk_hi[:, n - 2, L:], bx[n % 2][:, :LC], ACT.Copy).then_inc(kc_h, 1)
                    if n in (1, 2) or (n == 3 and i is None):
                        rotated_hi(n - 1)
                if i is None:
                    rotated_hi(3)
                else:
                    for n in range(4):
                        split_hi(act, Block(b0 + 4 + n, i, 16))
                        if n % 2:
                            rotated_hi(2 + n // 2)
                for n in range(4):
                    split_hi(act, Block(b0 + ob + 4 + n, i, 16))
                    ada_load(act, a0 + n + 1, i, 8)
                act.wait_ge(block_done, Block(b0 + ob + 7, i, 16).count(1))
                for t in range(KEYS):
                    nc.scalar.activation(rv_hi[:, t, :], rbanks[t][:], ACT.Copy).then_inc(rv_h, 1)
                for n in range(4):
                    b = Block(b0 + ob + 8 + n, i, 16)
                    split_hi(act, b)
                    ada_load(act, a0 + n + 5, i, 8)
                    if n == 0:
                        for s in range(KEYS):
                            act.wait_ge(y_free, before(jy + oy + 3 + s, i, 16))
                            nc.scalar.activation(rsc_hi[:, s, :], rt[s % 2][:], ACT.Copy).then_inc(sc_h, 1)
                    act.wait_ge(block_done, b.count(1))
                    nc.scalar.activation(rg[:, n, :], bx[n % 2][:], ACT.Silu).then_inc(x_free, 1)
                for e in range(HEADS):
                    act.wait_ge(ro_mm, per_head(i, HEADS, e + 1))
                    nc.scalar.activation(ro[:, e, :], bx[e % 2][:], ACT.Copy).then_inc(ro_done, 1)
                    if e == 3:
                        act.wait_ge(ro_sum, per_head(i, 2, 1))
                    nc.scalar.activation((std if e == 0 else rsq[e % 2])[:], bx[e % 2][:], ACT.Square).then_inc(x_free, 1)
                split_hi(act, Block(b0 + ob + 12, i, 16))
                act.wait_ge(rsum_mm, per_head(i, 1, 1))
                nc.scalar.activation(std[:], bn[:], ACT.Sqrt, scale=1.0 / L, bias=eps_col[:]).then_inc(rstd_s, 1)
                for e in range(HEADS):
                    act.wait_ge(ry_f, per_head(i, HEADS, e + 1))
                    nc.scalar.activation(ry_hi[:, e, :], rt[e % 2][:], ACT.Copy).then_inc(ry_h, 1)

            head_act(None)
            with act.Fori(0, HEADS - 1) as i:
                head_act(i)
            for n in range(4):
                if n >= 1:
                    split_hi(act, Block(B_SW0 - 4 + n))
                    for j in (2 * n - 2, 2 * n - 1):
                        act.wait_ge(y_free, JY["sw0"] - 8 + j + 1)
                        square(act, nffn0, j, res)
            for j in (KT - 2, KT - 1):
                act.wait_ge(y_free, JY["sw0"] - 8 + j + 1)
                square(act, nffn0, j, res)
            norm_root(act, nffn0, L, bn)
            norm_hi(act, nffn0, L, lambda j: ada[:, 56 + j:57 + j], hx_hi)
            act.wait_ge(nffn0.lo, nffn0.tiles + KT)
            swiglu_act(act, 0, B_SW0, JX["sw0"], JY["sw0"], 80)
            down_act(act, B_SD0, JY["sd0"], [(nmix1, None)], lambda n: ada_load(act, 125 + n) if n < 3 else None, none)
            norm_root(act, nmix1, L, bn)
            norm_hi(act, nmix1, L, lambda j: ada[:, 80 + j:81 + j], hx_hi)
            act.wait_ge(block_done, B_CIN)
            with act.Fori(0, 2) as i:
                for u in range(4):
                    for kind in range(2):
                        b = Block(B_CIN + 3 * u + kind, i, 12)
                        split_hi(act, b)
                        act.wait_ge(block_done, b.count(1))
                        nc.scalar.activation((cb if kind == 0 else cc)[u % 2][:], bx[kind][:], ACT.Copy)\
                            .then_inc(x_free, 1)
                    b = Block(B_CIN + 3 * u + 2, i, 12)
                    split_hi(act, b)
                    act.wait_ge(cy_f, before(u + 1, i, 4))
                    nc.scalar.activation(cy_hi[:, bass.ds(i * 4 + u, 1), :].rearrange("p o n -> p (o n)"), cacc[u % 2][:],
                                         ACT.Copy).then_inc(cy_h, 1)
            square_act(act, B_COUT, JY["cout"], nffn1)
            norm_root(act, nffn1, L, bn)
            norm_hi(act, nffn1, L, lambda j: ada[:, 104 + j:105 + j], hx_hi)
            act.wait_ge(nffn1.lo, nffn1.tiles + KT)
            act.wait_ge(block_done, B_SW1)
            swiglu_act(act, 1, B_SW1, JX["sw1"], JY["sw1"], None)
            down_act(act, B_SD1, JY["sd1"], [(nf2, None)], none, none)
            norm_root(act, nf2, L, bn)
            for n in range(2 * LT):
                act.wait_ge(turned_out, n + 1)
                nc.scalar.activation(out_tok[:, n // 2, (n % 2) * L:(n % 2 + 1) * L], bw[n % 2][:], ACT.Copy)\
                    .then_inc(out_copied, 1)

        def swiglu_dve(dve, w, first_block, jy, ada_at):
            with dve.Fori(0, HT // 2) as i:
                for u in range(2):
                    b = Block(first_block + 2 * u, i, 4)
                    split_lo(dve, b)
                    if ada_at is not None:
                        ada_reduce(dve, ada_at + 2 * u, ROW_C2, i, 4)
                    split_lo(dve, b.plus(1))
                    if ada_at is not None:
                        ada_reduce(dve, ada_at + 2 * u + 1, ROW_C2, i, 4)
                    dve.wait_ge(block_done, b.count(2))
                    dve.wait_ge(x_free, before((JX["sw0"] if w == 0 else JX["sw1"]) + u + 1, i, 2))
                    nc.vector.tensor_tensor(sw[u][:], sw[u][:], by[(jy + u) % 2][:], ALU.mult).then_inc(y_free, 1)
                    dve.wait_ge(y_free, before(jy + u + 1, i, 2))
                    dve.wait_ge(sw_h[w], before(u + 1, i, 2))
                    hs = bass.ds(i * 2 + u, 1)
                    nc.vector.tensor_tensor(hid_lo[:, hs, :].rearrange("p o n -> p (o n)"), sw[u][:],
                                            hid_hi[:, hs, :].rearrange("p o n -> p (o n)").bitcast(F32),
                                            ALU.subtract).then_inc(sw_l[w], 1)

        def down_dve(dve, first_block, job0, gate, norms, ada_of, beside=none):
            jobs = list(down_jobs(first_block))
            inside = 0
            for n in range(HT):
                split_lo(dve, Block(first_block + n))
                ada_of(n)
                for ct, tiles in jobs:
                    if tiles[-1][0].at == first_block + n:
                        if tiles[-1][1] == KT - 1:
                            dve.wait_ge(block_done, first_block + n + 1)
                        else:
                            inside += 1
                            dve.wait_ge(down_done[first_block], inside)
                        nc.vector.scalar_tensor_tensor(out=res[:, ct, :], in0=by[(job0 + ct) % 2][:], scalar=gate(ct),
                                                       in1=res[:, ct, :], op0=ALU.mult, op1=ALU.add)\
                            .then_inc(y_free, 1)
                        for nm in norms:
                            add_square(dve, nm, ct - 1)
                        beside(ct)

        def square_dve(dve, first_block, job0, gate, nm):
            for j in range(KT):
                split_lo(dve, Block(first_block + j))
                dve.wait_ge(block_done, first_block + j + 1)
                nc.vector.scalar_tensor_tensor(out=res[:, j, :], in0=by[(job0 + j) % 2][:], scalar=gate(j),
                                               in1=res[:, j, :], op0=ALU.mult, op1=ALU.add).then_inc(y_free, 1)
                add_square(dve, nm, j - 1)

        def ybrest(dve, c):
            dve.wait_ge(yb_f, c + 1)
            dve.wait_ge(yb_h, c + 1)
            nc.vector.tensor_tensor(yb_lo[:, :, c * P:(c + 1) * P], yt[c % 2][:].rearrange("p (h n) -> p h n", h=HEADS),
                                    yb_hi[:, :, c * P:(c + 1) * P].bitcast(F32), ALU.subtract).then_inc(yb_l, 1)

        @block.vector
        def _(dve):
            nc.vector.memset(ones[:], 1.0).then_inc(consts, 1)
            nc.vector.memset(eps2_col[:], EPS * EPS)
            nc.vector.memset(eps_col[:], EPS).then_inc(consts, 1)
            dve.wait_ge(cols_landed, 16)
            nc.vector.tensor_tensor(oml[:], col("lb0", 0, 4), col("lb1", 0, 4), ALU.subtract).then_inc(lb_ready, 1)
            for j in range(KT):
                dve.wait_ge(turned, KT + j + 1)
                nc.vector.tensor_copy(ctx_t[:, j, :], by[j % 2][:, :LC]).then_inc(y_free, 1)
            for j in range(KT):
                add_square(dve, n1x, j)
            for j in range(KT):
                add_square(dve, n1c, j, LC)
            for b in range(RAW):
                split_lo(dve, Block(b - AHEAD))
            dve.wait_ge(lb_ready, 2)
            nc.vector.tensor_scalar(oml[:], lb[:], -1.0, 1.0, ALU.mult, ALU.add).then_inc(lb_ready, 1)
            norm_rec(dve, n1x)
            norm_rec(dve, n1c, LC)
            for n in range(2, 4):
                dve.wait_ge(ada0_mm, n + 1)
                nc.vector.tensor_copy(ada_rows[:, n * L:(n + 1) * L], ada_banks[n][:2, :]).then_inc(ada0_rows, 1)
            dve.wait_ge(ada0_turned, 1)
            nc.vector.tensor_tensor(ada0[:], bw[0][:, :32].rearrange("p (a v) -> p a v", v=2),
                                    col("ada_b", 0, 16).rearrange("p (a o) -> p a o", o=1).to_broadcast([P, 16, 2]),
                                    ALU.add).then_inc(ada0_ready, 1)
            dve.wait_ge(ada0_ready, 1)
            for v in range(2):
                nc.vector.scalar_tensor_tensor(out=mod_a[:, v, :], in0=ada0[:, 8:16, v], scalar=1.0,
                                               in1=col("norm1", 0, 8), op0=ALU.add, op1=ALU.mult).then_inc(mod_ready, 1)
            dve.wait_ge(mod_ready, 2)
            norm_lo(dve, n1x, res, L, lambda j: mod_a[:, 0, j:j + 1], lambda j: ada0[:, j, 0:1], hx_hi, hx_lo)
            norm_lo(dve, n1c, ctx_t, LC, lambda j: mod_a[:, 1, j:j + 1], lambda j: ada0[:, j, 1:2], hc_hi, hc_lo)
            for b in range(RAW, AHEAD):
                split_lo(dve, Block(b - AHEAD))
            for n in range(8):
                d, h = n // HEADS, n % HEADS
                split_lo(dve, Block(B_GATES + n))
                if n == 0:
                    dve.wait_ge(crow_silu, 1)
                ada_reduce(dve, n, ROW_C)
                dve.wait_ge(f_ready, 2 * n + 2)
                nc.vector.tensor_scalar(hk[:, :, d, h, :], hf[:, :, 1 - d, h, :], -1.0, 1.0, ALU.mult, ALU.add)\
                    .then_inc(k_ready, 1)
                nc.vector.tensor_scalar(kc[:, d, h, :], fc[:, 1 - d, h, :], -1.0, 1.0, ALU.mult, ALU.add)\
                    .then_inc(k_ready, 1)
            for n in range(4):
                split_lo(dve, Block(B_VAL + n))
            dve.wait_ge(k_ready, 16)
            for l in range(LEVELS + 1):
                if l >= 1:
                    dve.wait_ge(kc_level, l)
                t_in = fc[:].rearrange("p d h n -> p (d h n)") if l == 0 else tc[(l - 1) % 2][:, :2 * HEADS * LC >> l]
                t_out = tc[l % 2][:, :2 * HEADS * LC >> (l + 1)] if l < LEVELS else None
                decay_keys(kc, t_in, l, t_out).then_inc(kc_level, 1)
            for n in range(4):
                split_lo(dve, Block(B_Q + n))
            dve.wait_ge(x_free, JX["q"] + 4)
            dve.wait_ge(masks_landed, 16)
            dve.wait_ge(kd_ready, 4)
            dve.wait_ge(s0_mm, 2)
            at = 0
            for c0 in (0, 2):
                for c in (c0, c0 + 1):
                    nc.vector.tensor_tensor(ksum[c % 2][:], hk[:, c, 0, :, :], hk[:, c, 1, :, :], ALU.add)\
                        .then_inc(level_ready, 1)
                for r in range(LEVELS + 1):
                    for c in (c0, c0 + 1):
                        if at % STEPS == STEPS // 2:
                            split_lo(dve, Block(B_FNET + at // STEPS))
                        at += 1
                        dve.wait_ge(level_mm, at)
                        src = bw[c % 2][:].rearrange("p (h n) -> p h n", h=HEADS)
                        if r == 0:
                            nc.vector.tensor_tensor(att[c][:], src,
                                                    ident[:].rearrange("p (o n) -> p o n", o=1).to_broadcast([P, HEADS, P]),
                                                    ALU.mult)
                            nc.vector.tensor_tensor(hq[:, c], hq[:, c], hf[:, c], ALU.mult).then_inc(level_ready, 1)
                            continue
                        l = r - 1
                        dve.wait_ge(level_ready, level_step(c0, r, c) + 1)
                        nc.vector.copy_predicated(att[c][:], masks[:, l:l + 1, :].to_broadcast([P, HEADS, P]), src)
                        t_in = (hf[:, c].rearrange("p d h n -> p (d h n)") if l == 0
                                else tx[c % 2][(l - 1) % 2][:, :2 * HEADS * P >> l])
                        t_out = tx[c % 2][l % 2][:, :2 * HEADS * P >> (l + 1)] if l < LEVELS - 1 else ttot[:, c, :]
                        decay_queries(c, t_in, l)
                        ins = decay_keys(hk[:, c], t_in, l, t_out)
                        ins.then_inc(chunk_ready if l == LEVELS - 1 else level_ready, 1)
            dve.wait_ge(s_ready, 2)
            dve.wait_ge(chunk_ready, LT)
            for n, (c, d) in enumerate(UPDATES):
                dve.wait_ge(upd_mm, n + 1)
                if n >= 2:
                    dve.wait_ge(upd_done, n - 1)
                old = (S_ENTER_F if d == 0 else S_ENTER_B)[c]
                new = S_ENTER_F[c + 1] if d == 0 else S_ENTER_B[c - 1]
                for h in range(HEADS):
                    ins = nc.vector.scalar_tensor_tensor(out=new[:, h, :], in0=old[:, h, :],
                                                         scalar=ttot[:, c, HEADS * (1 - d) + h:HEADS * (1 - d) + h + 1],
                                                         in1=by[n % 2][:, h * P:(h + 1) * P], op0=ALU.mult, op1=ALU.add)
                ins.then_inc(upd_done, 1)
            dve.wait_ge(o_mm, LT)
            for c in range(LT):
                dve.wait_ge(ostd, c + 1)
                nc.vector.reciprocal(rstd[:], std[:]).then_inc(orstd, 1)
                dve.wait_ge(orstd, c + 1)
                dve.wait_ge(gs_ready, HEADS)
                if c >= 2:
                    dve.wait_ge(yb_l, c - 1)
                y3 = yt[c % 2][:].rearrange("p (h n) -> p h n", h=HEADS)
                nc.vector.tensor_tensor(y3, ho[:, c, 0, :, :], rstd[:].rearrange("p (h n) -> p h n", h=HEADS),
                                        ALU.mult).then_inc(on_ready, 1)
                dve.wait_ge(on_ready, c + 1)
                nc.vector.tensor_tensor(y3, y3, gs[:, :, c * P:(c + 1) * P], ALU.mult).then_inc(yb_f, 1)
                if c >= 1:
                    ybrest(dve, c - 1)
            ybrest(dve, LT - 1)
            for g in range(HEADS):
                dve.wait_ge(ya_h, g + 1)
                nc.vector.tensor_tensor(ya_lo[:, g, :], bw[g % 2][:], ya_hi[:, g, :].bitcast(F32), ALU.subtract)\
                    .then_inc(ya_l, 1)
            with dve.Fori(0, 2) as i:
                for u in range(4):
                    for kind in range(3):
                        split_lo(dve, Block(B_MERGE + 3 * u + kind, i, 12))
                        ada_reduce(dve, 8 + 3 * u + kind, ROW_C, i, 12)
                    dve.wait_ge(block_done, Block(B_MERGE + 3 * u + 2, i, 12).count(1))
                    dve.wait_ge(x_free, before(JX["merge"] + 2 * u + 2, i, 8))
                    nc.vector.tensor_tensor(gate_a[u % 2][:], gate_a[u % 2][:], by[0][:], ALU.mult).then_inc(y_free, 1)
                    nc.vector.tensor_tensor(gate_b[u % 2][:], gate_b[u % 2][:], by[1][:], ALU.mult).then_inc(y_free, 1)
                    dve.wait_ge(y_free, before(JY["merge"] + 2 * u + 2, i, 8))
                    nc.vector.tensor_tensor(mt[u % 2][:], gate_a[u % 2][:], gate_b[u % 2][:], ALU.add).then_inc(m_f, 1)
                    dve.wait_ge(m_f, before(u + 1, i, 4))
                    dve.wait_ge(m_h, before(u + 1, i, 4))
                    ms = bass.ds(i * 4 + u, 1)
                    nc.vector.tensor_tensor(m_lo[:, ms, :].rearrange("p o n -> p (o n)"), mt[u % 2][:],
                                            m_hi[:, ms, :].rearrange("p o n -> p (o n)").bitcast(F32),
                                            ALU.subtract).then_inc(m_l, 1)
            dve.wait_ge(ada_cols, 32)
            def modulation(at, gain_at, count, v=0, src=None):
                s = ada if src is None else src
                nc.vector.scalar_tensor_tensor(out=mod_a[:, v, :], in0=s[:, at:at + 8], scalar=1.0,
                                               in1=cols[:, gain_at:gain_at + 8], op0=ALU.add,
                                               op1=ALU.mult).then_inc(mod_ready, 1)
                dve.wait_ge(mod_ready, count)

            modulation(16, COLS["norm2"], 3)
            square_dve(dve, B_OUT, JY["out"], lambda j: ada[:, j:j + 1], n2)

            dve.wait_ge(y_free, JY["out"] + 8)
            norm_rec(dve, n2)
            norm_lo(dve, n2, res, L, lambda j: mod_a[:, 0, j:j + 1], lambda j: ada[:, 8 + j:9 + j], hx_hi, hx_lo)
            dve.wait_ge(n2.lo, n2.tiles + KT)
            with dve.Fori(0, HT // 2) as i:
                for s in range(2):
                    dve.wait_ge(x_free, before(JX["up"] + 2 * s + 2, i, 4))
                    for n, (k, t) in enumerate(TAPS):
                        if n >= 2:
                            dve.wait_ge(tap_done, before(16 * s + n - 1, i, 32))
                        cw = i * 40 + (COLS["conv"] + 20 * s + 10 * k + t)
                        grid = acc[s][k][:].rearrange("p (r c) -> p r c", r=ROWS)
                        nc.vector.scalar_tensor_tensor(
                            out=grid, in0=zpad[s][k][:, t // 3:t // 3 + ROWS, t % 3:t % 3 + GRID],
                            scalar=cols[:, bass.ds(cw, 1)], in1=grid, op0=ALU.mult, op1=ALU.add).then_inc(tap_done, 1)
            dve.wait_ge(lo_ready, B_DOWN + AHEAD)
            def context_dve(job):
                if job == 4:
                    for j in range(KT):
                        add_square(dve, nmc, j, LC)
                if job == 6:
                    norm_rec(dve, nmc, LC)
                    dve.wait_ge(ada_cols, 48)
                    modulation(40, COLS["mix"], 4)
                    nc.vector.tensor_tensor(mod_a[:, 0, :], mod_a[:, 0, :], col("final1", 0, KT), ALU.mult)\
                        .then_inc(mod_ready, 1)
                    modulation(8, COLS["mix"], 6, 1, ada_c)

            down_dve(dve, B_DOWN, JY["down"], lambda j: ada[:, 24 + j:25 + j], (nmx, nf1),
                     lambda n: ada_reduce(dve, 32 + n, ROW_C2, row_c=ROW_CTX2) if n < 16 else None, context_dve)
            dve.wait_ge(y_free, JY["down"] + 8)
            norm_rec(dve, nmx)
            dve.wait_ge(nf1.mm, 1)
            norm_lo(dve, nmx, res, L, lambda j: mod_a[:, 0, j:j + 1], lambda j: ada[:, 32 + j:33 + j], hx_hi, hx_lo)
            norm_lo(dve, nmc, ctx2_t, LC, lambda j: mod_a[:, 1, j:j + 1], lambda j: ada_c[:, j:j + 1], hc_hi, hc_lo)
            dve.wait_ge(rope_landed, 16)
            dve.wait_ge(nmc.lo, nmc.tiles + KT)
            def wo_dve(b0, jy, i, head0, split_from=0, nm=None, beside=none):
                for n in range(4):
                    b = Block(b0 + n, i, 16)
                    if n >= split_from:
                        split_lo(dve, b)
                    for u in range(2):
                        j = 2 * n + u
                        if u == 0:
                            dve.wait_ge(wo_half, before(4 * head0 + n + 1, i, 4))
                        else:
                            dve.wait_ge(block_done, b.count(1))
                        nc.vector.scalar_tensor_tensor(out=res[:, j, :], in0=by[u][:], scalar=ada[:, 48 + j:49 + j],
                                                       in1=res[:, j, :], op0=ALU.mult, op1=ALU.add)\
                            .then_inc(y_free, 1)
                        if nm is not None and u == 1:
                            add_square(dve, nm, j - 3)
                            add_square(dve, nm, j - 2)
                    beside(n)
                dve.wait_ge(y_free, before(jy + 8, i, 16))
                if nm is not None:
                    add_square(dve, nm, KT - 2)

            def head_dve(i):
                b0, jx, jy, ob, oy = head_blocks(i)
                a0 = 48 if i is None else 56

                def rotated_lo(n):
                    dve.wait_ge(rot_h, per_head(i, 4, n + 1))
                    hi, lo = (t[:, n % 2, :L] for t in ((rq_hi, rq_lo) if n < 2 else (rk_hi, rk_lo)))
                    nc.vector.tensor_tensor(lo, rot[n % 2][:], hi.bitcast(F32), ALU.subtract).then_inc(rot_l, 1)

                def rotate(n):
                    src, ht = (by if n < 2 else bw)[n % 2][:].rearrange("p (r c) -> p r c", r=ROWS), n % 2
                    own, other = (t[:].rearrange("p (r c) -> p r c", r=ROWS) for t in rt)
                    if ht == 0:
                        cos, sin = (rope[:, at:at + ROWS].rearrange("p (r o) -> p r o", o=1).to_broadcast([P, ROWS, GRID])
                                    for at in (0, ROWS))
                    else:
                        cos, sin = (rope[:, at:at + GRID].rearrange("p (o c) -> p o c", o=1).to_broadcast([P, ROWS, GRID])
                                    for at in (2 * ROWS, 2 * ROWS + GRID))
                    nc.vector.tensor_tensor(own, src, cos, ALU.mult)
                    for h0, h1 in ((0, 64), (64, 128)):
                        to = 64 - h0
                        ins = nc.vector.tensor_tensor(other[to:to + 64], src[h0:h1], sin[h0:h1], ALU.mult)
                    ins.then_inc(y_free if n < 2 else rot_p, 1)
                    if n < 2:
                        dve.wait_ge(y_free, before(jy + n + 1, i, 16))
                    else:
                        dve.wait_ge(rot_p, per_head(i, 2, n - 1))
                        dve.wait_ge(rot_l, per_head(i, 4, n - 1))
                    nc.vector.tensor_tensor(rot[n % 2][:], rt[0][:], rt[1][:], ALU.add).then_inc(rot_f, 1)
                    dve.wait_ge(rot_f, per_head(i, 4, n + 1))

                for n in range(4):
                    b = Block(b0 + n, i, 16)
                    if n >= 1 or i is None:
                        split_lo(dve, b)
                    dve.wait_ge(block_done, b.count(1))
                    if n >= 2:
                        dve.wait_ge(kc_h, per_head(i, 2, n - 1))
                        nc.vector.tensor_tensor(rk_lo[:, n - 2, L:], bx[n % 2][:, :LC],
                                                rk_hi[:, n - 2, L:].bitcast(F32), ALU.subtract).then_inc(x_free, 1)
                    if n < 2 or i is None:
                        rotate(n)
                    if n in (1, 2) or (n == 3 and i is None):
                        rotated_lo(n - 1)
                if i is None:
                    rotated_lo(3)
                else:
                    dve.wait_ge(ada_cols, 56)
                    dve.wait_ge(nf1.lo, KT)

                    def keys(n):
                        if n % 2 == 0:
                            rotate(2 + n // 2)
                        else:
                            rotated_lo(2 + n // 2)

                    wo_dve(b0 + 4, jy + 2, i, 0, beside=keys)
                for n in range(4):
                    split_lo(dve, Block(b0 + ob + 4 + n, i, 16))
                    ada_reduce(dve, a0 + n, ROW_C2, i, 8)
                for t in range(KEYS):
                    dve.wait_ge(rv_h, per_head(i, KEYS, t + 1))
                    nc.vector.tensor_tensor(rv_lo[:, t, :], rbanks[t][:], rv_hi[:, t, :].bitcast(F32), ALU.subtract)\
                        .then_inc(rv_l, 1)
                dve.wait_ge(dec_landed, per_head(i, 16, 16))

                def scores_lo(s):
                    dve.wait_ge(sc_h, per_head(i, KEYS, s + 1))
                    nc.vector.tensor_tensor(rsc_lo[:, s, :], rt[s % 2][:], rsc_hi[:, s, :].bitcast(F32), ALU.subtract)\
                        .then_inc(sc_l, 1)

                for s in range(KEYS):
                    dve.wait_ge(sc_mm, per_head(i, KEYS, s + 1))
                    if s == 2:
                        split_lo(dve, Block(b0 + ob + 8, i, 16))
                    if s >= 2:
                        dve.wait_ge(sc_l, per_head(i, KEYS, s - 1))
                    w = (LT - 1 - s) * P if s < LT else DEC_W + (s - LT) * L
                    nc.vector.tensor_tensor(rt[s % 2][:], by[s % 2][:], dec[:, w:w + L], ALU.mult).then_inc(y_free, 1)
                    if s >= 1:
                        dve.wait_ge(y_free, before(jy + oy + 2 + s, i, 16))
                        scores_lo(s - 1)
                dve.wait_ge(y_free, before(jy + oy + 2 + KEYS, i, 16))
                scores_lo(KEYS - 1)
                for n in range(4):
                    if n >= 1:
                        split_lo(dve, Block(b0 + ob + 8 + n, i, 16))
                    ada_reduce(dve, a0 + 4 + n, ROW_C2, i, 8)
                if i is None:
                    rms_dve(dve, nf1, lambda j: col("final1", j))
                for e in (1, 2):
                    dve.wait_ge(x_free, before(jx + 7 + e, i, 10))
                    if e == 2:
                        dve.wait_ge(ro_sum, per_head(i, 2, 1))
                    nc.vector.tensor_tensor(std[:], std[:], rsq[e % 2][:], ALU.add).then_inc(ro_sum, 1)
                split_lo(dve, Block(b0 + ob + 12, i, 16))
                dve.wait_ge(sc_l, per_head(i, KEYS, KEYS))
                dve.wait_ge(rstd_s, per_head(i, 1, 1))
                nc.vector.reciprocal(rstd[:], std[:]).then_inc(rstd_r, 1)
                dve.wait_ge(rstd_r, per_head(i, 1, 1))
                dve.wait_ge(ro_done, per_head(i, HEADS, HEADS))
                dve.wait_ge(x_free, before(jx + 6, i, 10))

                def gated_lo(e):
                    dve.wait_ge(ry_f, per_head(i, HEADS, e + 1))
                    dve.wait_ge(ry_h, per_head(i, HEADS, e + 1))
                    nc.vector.tensor_tensor(ry_lo[:, e, :], rt[e % 2][:], ry_hi[:, e, :].bitcast(F32), ALU.subtract)\
                        .then_inc(ry_l, 1)

                for e in range(HEADS):
                    if e >= 2:
                        dve.wait_ge(ry_l, per_head(i, HEADS, e - 1))
                    nc.vector.tensor_tensor(rt[e % 2][:], ro[:, e, :], rstd[:], ALU.mult).then_inc(ry_t, 1)
                    dve.wait_ge(ry_t, per_head(i, HEADS, e + 1))
                    nc.vector.tensor_tensor(rt[e % 2][:], rt[e % 2][:], rg[:, e, :], ALU.mult).then_inc(ry_f, 1)
                    if e >= 1:
                        gated_lo(e - 1)
                gated_lo(HEADS - 1)
                dve.wait_ge(ry_l, per_head(i, HEADS, HEADS))

            head_dve(None)
            with dve.Fori(0, HEADS - 1) as i:
                head_dve(i)
            modulation(64, COLS["ffn"], 7)
            wo_dve(B_SW0 - 4, JY["sw0"] - 8, None, HEADS - 1, 1, nffn0)
            norm_rec(dve, nffn0)
            norm_lo(dve, nffn0, res, L, lambda j: mod_a[:, 0, j:j + 1], lambda j: ada[:, 56 + j:57 + j], hx_hi, hx_lo)
            dve.wait_ge(nffn0.lo, nffn0.tiles + KT)
            swiglu_dve(dve, 0, B_SW0, JY["sw0"], 80)
            modulation(88, COLS["mix"] + 8, 8)
            down_dve(dve, B_SD0, JY["sd0"], lambda j: ada[:, 72 + j:73 + j], (nmix1,),
                     lambda n: ada_reduce(dve, 124 + n, ROW_C2) if n < 4 else None)
            dve.wait_ge(ada_cols, 128)
            dve.wait_ge(y_free, JY["sd0"] + 8)
            norm_rec(dve, nmix1)
            norm_lo(dve, nmix1, res, L, lambda j: mod_a[:, 0, j:j + 1], lambda j: ada[:, 80 + j:81 + j], hx_hi, hx_lo)
            dve.wait_ge(block_done, B_CIN)
            for s in range(2):
                nc.vector.memset(cpad[s][:], 0.0).then_inc(cpad_zero, 1)
            dve.wait_ge(cpad_zero, 2)
            with dve.Fori(0, 2) as i:
                for u in range(4):
                    for kind in range(3):
                        split_lo(dve, Block(B_CIN + 3 * u + kind, i, 12))
                    s = u % 2
                    dve.wait_ge(block_done, Block(B_CIN + 3 * u + 2, i, 12).count(1))
                    dve.wait_ge(x_free, before(JX["cin"] + 2 * u + 2, i, 8))
                    nc.vector.tensor_tensor(cpad[s][:, 1:L + 1], cc[s][:], by[u % 2][:], ALU.mult).then_inc(y_free, 1)
                    dve.wait_ge(y_free, before(JY["cin"] + u + 1, i, 4))
                    for t in range(3):
                        wcol = cols[:, bass.ds(i * 12 + (COLS["sconv"] + 3 * u + t), 1)]
                        if t == 0:
                            nc.vector.tensor_scalar(cacc[s][:], cpad[s][:, 0:L], wcol, None, ALU.mult)\
                                .then_inc(cacc_step, 1)
                        else:
                            dve.wait_ge(cacc_step, before(3 * u + t, i, 12))
                            nc.vector.scalar_tensor_tensor(out=cacc[s][:], in0=cpad[s][:, t:t + L], scalar=wcol,
                                                           in1=cacc[s][:], op0=ALU.mult, op1=ALU.add)\
                                .then_inc(cacc_step, 1)
                    dve.wait_ge(cacc_step, before(3 * u + 3, i, 12))
                    nc.vector.tensor_tensor(cacc[s][:], cacc[s][:], cb[s][:], ALU.mult).then_inc(cy_f, 1)
                    dve.wait_ge(cy_f, before(u + 1, i, 4))
                    dve.wait_ge(cy_h, before(u + 1, i, 4))
                    ms = bass.ds(i * 4 + u, 1)
                    nc.vector.tensor_tensor(cy_lo[:, ms, :].rearrange("p o n -> p (o n)"), cacc[s][:],
                                            cy_hi[:, ms, :].rearrange("p o n -> p (o n)").bitcast(F32),
                                            ALU.subtract).then_inc(cy_l, 1)
            modulation(112, COLS["ffn"] + 8, 9)
            square_dve(dve, B_COUT, JY["cout"], lambda j: ada[:, 96 + j:97 + j], nffn1)
            dve.wait_ge(y_free, JY["cout"] + 8)
            norm_rec(dve, nffn1)
            norm_lo(dve, nffn1, res, L, lambda j: mod_a[:, 0, j:j + 1], lambda j: ada[:, 104 + j:105 + j], hx_hi, hx_lo)
            dve.wait_ge(nffn1.lo, nffn1.tiles + KT)
            swiglu_dve(dve, 1, B_SW1, JY["sw1"], None)
            down_dve(dve, B_SD1, JY["sd1"], lambda j: ada[:, 120 + j:121 + j], (nf2,), none)
            dve.wait_ge(y_free, JY["sd1"] + 8)
            rms_dve(dve, nf2, lambda j: col("final2", j))

        @block.gpsimd
        def _(pool):
            pool.wait_ge(n2.lo, n2.tiles + KT)
            for s in range(2):
                nc.gpsimd.memset(zpad[s][0][:], 0.0)
                nc.gpsimd.memset(zpad[s][1][:], 0.0).then_inc(hid_l, 1)
            pool.wait_ge(lo_ready, B_UP + AHEAD)
            def split(i, u):
                nb = Block(B_UP + u + AHEAD, i, 4)
                pool.wait_ge(hi_ready, nb.count(1))
                nc.gpsimd.tensor_tensor(w_lo[nb.at % RING][:], w_raw[nb.at % RAW][:],
                                        w_hi[nb.at % RING][:].bitcast(F32), ALU.subtract).then_inc(lo_ready, 1)

            def gated(i, s, at):
                pool.wait_ge(silu_done, before(at + s + 1, i, 2))
                nc.gpsimd.tensor_tensor(hidden[s][:], sgate[s][:], hidden[s][:], ALU.mult).then_inc(hid_f, 1)

            def hidden_lo(i, s, at):
                pool.wait_ge(hid_f, before(at + s + 1, i, 2))
                pool.wait_ge(hid_h, before(at + s + 1, i, 2))
                hi, lo = (h[:, at + s, :] if i is None else
                          h[:, bass.ds(i * 2 + (at + s), 1), :].rearrange("p o n -> p (o n)")
                          for h in (hid_hi, hid_lo))
                nc.gpsimd.tensor_tensor(lo, hidden[s][:], hi.bitcast(F32), ALU.subtract).then_inc(hid_l, 1)

            split(None, 0)
            split(None, 1)
            with pool.Fori(0, HT // 2 - 1) as i:
                for s in range(2):
                    split(i, 2 + 2 * s)
                    gated(i, s, 0)
                    split(i, 3 + 2 * s)
                    hidden_lo(i, s, 0)
            split(None, 2 * HT - 2)
            split(None, 2 * HT - 1)
            for s in range(2):
                gated(None, s, HT - 2)
                hidden_lo(None, s, HT - 2)


def stream_blocks(inputs):
    def tiles(w, cols=P):
        r, n = w.shape
        return w.reshape(r // P, P, n // cols, cols).transpose(2, 1, 0, 3)

    def tall(w):
        r, n = w.shape
        t = w.reshape(r // P, P, n // P, P).transpose(2, 0, 1, 3).reshape(-1, KT, P, P)
        return t.transpose(0, 2, 1, 3)

    def rows(w):
        return w.reshape(4, 2, P, L).transpose(0, 2, 1, 3)

    def pairs(a, b):
        return np.stack([a, b], 1).reshape((-1,) + a.shape[1:])

    w_in = inputs["w_in"][0]
    fnet, q, f_f, f_b, val, g = (w_in[:, n * L:(n + 1) * L] for n in range(6))
    gate_a, gate_b = w_in[:, 6 * L:6 * L + D], w_in[:, 6 * L + D:]
    wab = np.concatenate([tiles(inputs["w_a"][0]), tiles(inputs["w_b"][0])], 2)
    merge = np.stack([tiles(gate_a), tiles(gate_b), wab], 1).reshape(-1, P, KT, P)
    up = inputs["ffn_up"][0]
    parts = [tiles(f_f), tiles(f_b), rows(val), tiles(q), tiles(fnet), tiles(g), merge, tiles(inputs["w_out"][0]),
             pairs(tiles(up[:, :FF]), tiles(up[:, FF:])), tall(inputs["ffn_down"][0])]
    ret, w_o = inputs["ret_w_qkvg_2"][0], inputs["ret_w_o_2"][0]
    outs = [tiles(w_o[h * L:(h + 1) * L]).reshape(4, 2, P, HEADS, P).transpose(0, 2, 1, 3, 4) for h in range(HEADS)]
    for h in range(HEADS):
        parts += [tiles(ret[:, h * 256:(h + 1) * 256]), tiles(ret[:, D + h * 256:D + (h + 1) * 256])]
        parts += outs[h - 1:h]
        parts += [rows(ret[:, 2 * D + h * L:2 * D + (h + 1) * L]), tiles(ret[:, 4 * D + h * L:4 * D + (h + 1) * L])]
    parts += outs[-1:]
    c_in = inputs["conv_w_in_2"][0]
    cin = np.stack([tiles(c_in[:, n * D:(n + 1) * D]) for n in range(3)], 1).reshape(-1, P, KT, P)
    for layer in range(2):
        parts += [pairs(tiles(inputs["ffn_w1_2"][layer]), tiles(inputs["ffn_w3_2"][layer])),
                  tall(inputs["ffn_w2_2"][layer])]
        if layer == 0:
            parts += [cin, tiles(inputs["conv_w_out_2"][0])]
    return np.concatenate([p.reshape(-1, P, BLK) for p in parts])


def small_columns(inputs):
    def col(v):
        return v.reshape(-1, P).T

    conv = inputs["ffn_conv_w"][0].reshape(9, 2, HT, P)
    conv = np.concatenate([conv, inputs["ffn_conv_b"][0].reshape(1, 2, HT, P)])
    conv = conv.transpose(3, 2, 1, 0).reshape(P, HT * 20)
    sconv = inputs["conv_w_2"][0].reshape(3, KT, P).transpose(2, 1, 0).reshape(P, 24)
    parts = [col(inputs["c"][0]), col(inputs["c_ctx"]), col(inputs["norm1_g"][0]), col(inputs["norm2_g"][0]),
             col(inputs["final_g"]), col(inputs["hg_lb"][0]), col(inputs["hg_lb"][1]), col(inputs["hg_onorm_g"][0]),
             conv, col(inputs["ada_b"][0]), col(inputs["ada_b_2"][0]), col(inputs["ada_b_2"][1]),
             col(inputs["norm_mix_2"].reshape(-1)), col(inputs["norm_ffn_2"].reshape(-1)),
             col(inputs["final_norm_2"]), sconv]
    return np.concatenate(parts, 1)


def constants():
    f64 = np.float64
    n = np.arange(P)
    top = n[:, None] ^ n[None, :]
    masks = np.stack([(top >> l) == 1 for l in range(LEVELS)], 1).astype(np.int32)
    a1 = 2 * np.pi * ((n[:, None] * n[None, :]) % P) / P
    dft1 = np.concatenate([np.cos(a1), np.sin(a1)], 1) / np.sqrt(f64(P * L))
    t = np.arange(L)
    a2 = 2 * np.pi * ((t[:, None] * t[None, :]) % L) / L
    dft2 = np.stack([np.cos(a2), -np.sin(a2)]).reshape(2, LT, P, L).transpose(2, 0, 1, 3)
    half = 64
    freqs = (np.float32(10000.0) ** (-np.arange(half, dtype=np.float32) / np.float32(half))).astype(np.float32)
    rope = []
    for pos in (np.arange(ROWS), np.arange(GRID)):
        ang = (freqs[:, None] * pos[None, :].astype(np.float32)).astype(f64)
        rope += [np.concatenate([np.cos(ang)] * 2), np.concatenate([np.sin(ang), -np.sin(ang)])]
    rope = np.concatenate(rope, 1)
    dec = np.zeros((HEADS, P, DEC_N))
    scale = 256.0 ** -0.5
    for h in range(HEADS):
        gf, gb = 1 - 2.0 ** (-5.0 - h), 1 - 2.0 ** (-5.5 - h)
        d = np.arange(DEC_W)[None, :] - (LT - 1) * P - n[:, None]
        dec[h, :, :DEC_W] = scale * (np.where(d >= 0, gf ** np.maximum(d, 0), 0) + np.where(d <= 0, gb ** np.maximum(-d, 0), 0))
        for ct in range(LCT):
            j = ct * P + n[:, None]
            dec[h, :, DEC_W + ct * L:DEC_W + (ct + 1) * L] = scale * (gf ** (t + f64(LC) - j) + gb ** (f64(L) - t + j))
    f32 = lambda a: np.ascontiguousarray(a, dtype=np.float32)
    return {"ident": f32(np.eye(P)), "masks": masks, "dft1": f32(dft1), "dft2": f32(dft2), "rope": f32(rope), "dec": f32(dec)}


def kernel(**inputs):
    import concourse.bacc as bacc
    from concourse.bass_utils import run_bass_kernel_spmd

    inputs = {k: np.asarray(v) for k, v in inputs.items()}
    ada_w = [inputs["ada_w"][0], inputs["ada_w_2"][0], inputs["ada_w_2"][1]]
    arrays = {
        "wstream": stream_blocks(inputs),
        "ada_kn": ada_w[0][:, :2 * D].reshape(KT, P, 2 * D),
        "ada_nk": np.concatenate([ada_w[0].T[2 * D:], ada_w[1].T, ada_w[2].T]).reshape(128, P, D),
        "x": inputs["x"][0].reshape(LT, P, D).transpose(1, 0, 2),
        "ctx1": inputs["ctx"][0].reshape(LCT, P, D).transpose(1, 0, 2),
        "ctx2": inputs["ctx_2"][0].reshape(LCT, P, D).transpose(1, 0, 2),
        "cols": small_columns(inputs),
        "crow": np.stack([inputs["c_2"][0], inputs["c"][0], inputs["c_ctx_2"]]),
        **constants(),
    }
    arrays = {k: np.ascontiguousarray(v) for k, v in arrays.items()}
    nc = bacc.Bacc("TRN2", target_bir_lowering=False, num_devices=1, dynamic_dma_scratch_size=1024)
    aps = {k: nc.dram_tensor("in_" + k, v.shape, mybir.dt.from_np(v.dtype), kind="ExternalInput").ap()
           for k, v in arrays.items()}
    out = nc.dram_tensor("out_x", (L, D), F32, kind="ExternalOutput").ap()
    program(nc, aps["wstream"], aps["ada_kn"], aps["ada_nk"], aps["x"], aps["ctx1"], aps["ctx2"], aps["cols"],
            aps["crow"], aps["ident"], aps["masks"], aps["dft1"], aps["dft2"], aps["rope"], aps["dec"], out)
    r = run_bass_kernel_spmd(nc, [{"in_" + k: v for k, v in arrays.items()}], core_ids=[0])
    return r.results[0]["out_x"].reshape(1, L, D)
```
